# Optimizing a Trainium2 kernel written in Bass

```python
import math
import jax, jax.numpy as jnp
from jax import lax
import numpy as np

D_MODEL = 1024
BATCH = 1
SEQ = 512
DEPTH = 1

D_A = D_MODEL
K_A = 3
D_B = D_MODEL
K_B = 31
N_MEM = 256
N_HEADS = 4
HEAD_DIM = D_MODEL // N_HEADS
D_ATT = N_HEADS * HEAD_DIM
N_BRANCH = 3
D_FF = 2816
K_F = 3
EPS = 1e-6
IN_SPLITS = (3 * D_A, 3 * D_A + 2 * D_B, 3 * D_A + 2 * D_B + D_ATT)
D_IN = 3 * D_A + 2 * D_B + D_ATT + N_BRANCH * D_MODEL


def _rmsnorm(x, g):
    xf = x.astype(jnp.float32)
    r = lax.rsqrt(jnp.mean(xf * xf, axis=-1, keepdims=True) + EPS)
    return (xf * r).astype(x.dtype) * g

def _layernorm(x, g, b):
    xf = x.astype(jnp.float32)
    mu = jnp.mean(xf, axis=-1, keepdims=True)
    var = jnp.mean(jnp.square(xf - mu), axis=-1, keepdims=True)
    return ((xf - mu) * lax.rsqrt(var + EPS)).astype(x.dtype) * g + b

def _causal_dwconv(x, w):
    k, c = w.shape
    return lax.conv_general_dilated(
        x, w[:, None, :].astype(x.dtype), window_strides=(1,), padding=[(k - 1, 0)],
        dimension_numbers=("NWC", "WIO", "NWC"), feature_group_count=c)

def first_inputs(seed: int = 0) -> dict:
    key = jax.random.key(seed)
    ks = jax.random.split(key, 24)
    L, D = DEPTH, D_MODEL

    def nrm(k, shape, fan_in):
        return jax.random.normal(k, shape, jnp.float32) * (fan_in ** -0.5)

    def gain(k, shape):
        return 1.0 + 0.02 * jax.random.normal(k, shape, jnp.float32)

    def small(k, shape):
        return 0.02 * jax.random.normal(k, shape, jnp.float32)

    return {
        "x": jax.random.normal(ks[0], (BATCH, SEQ, D), jnp.float32),
        "mem": jax.random.normal(ks[1], (BATCH, N_MEM, D), jnp.float32),
        "norm_mix_g": gain(ks[2], (L, D)),
        "norm_mem_g": gain(ks[3], (L, D)),
        "w_in": nrm(ks[4], (L, D, D_IN), D),
        "b_gate": small(ks[5], (L, N_BRANCH * D)),
        "conv_a_w": nrm(ks[6], (L, K_A, D_A), K_A),
        "w_a_out": nrm(ks[7], (L, D_A, D), D_A),
        "conv_b_w": nrm(ks[8], (L, K_B, D_B), K_B),
        "conv_b_bias": small(ks[9], (L, D_B)),
        "ln_b_g": gain(ks[10], (L, D_B)),
        "ln_b_b": small(ks[11], (L, D_B)),
        "w_b_out": nrm(ks[12], (L, D_B, D), D_B),
        "w_kv": nrm(ks[13], (L, D, 2 * D_ATT), D),
        "w_att_out": nrm(ks[14], (L, D_ATT, D), D_ATT),
        "w_o": nrm(ks[15], (L, D, D), D),
        "norm_ffn_g": gain(ks[16], (L, D)),
        "w_up": nrm(ks[17], (L, D, 2 * D_FF), D),
        "conv_ffn_w": nrm(ks[18], (L, K_F, 2 * D_FF), K_F),
        "w_down": nrm(ks[19], (L, D_FF, D), D_FF),
        "norm_final_g": gain(ks[20], (D,)),
    }

def _mixer(x, mem, norm_mix_g, norm_mem_g, w_in, b_gate, conv_a_w, w_a_out,
           conv_b_w, conv_b_bias, ln_b_g, ln_b_b, w_b_out, w_kv, w_att_out, w_o):
    bsz, seq, _ = x.shape
    h = _rmsnorm(x, norm_mix_g)
    proj = h @ w_in
    p_a, p_b, q, p_g = jnp.split(proj, IN_SPLITS, axis=-1)

    gb, gc, v = jnp.split(p_a, 3, axis=-1)
    y_a = (gb * _causal_dwconv(gc * v, conv_a_w)) @ w_a_out

    u, ug = jnp.split(p_b, 2, axis=-1)
    u = u * jax.nn.sigmoid(ug)
    u = _causal_dwconv(u, conv_b_w) + conv_b_bias
    u = jax.nn.silu(_layernorm(u, ln_b_g, ln_b_b))
    y_b = u @ w_b_out

    memn = _rmsnorm(mem, norm_mem_g)
    k, vm = jnp.split(memn @ w_kv, 2, axis=-1)
    qh = q.reshape(bsz, seq, N_HEADS, HEAD_DIM)
    kh = k.reshape(bsz, N_MEM, N_HEADS, HEAD_DIM)
    vh = vm.reshape(bsz, N_MEM, N_HEADS, HEAD_DIM)
    s = jnp.einsum("bshd,bmhd->bhsm", qh, kh).astype(jnp.float32) * (1.0 / math.sqrt(HEAD_DIM))
    pr = jax.nn.softmax(s, axis=-1).astype(x.dtype)
    o = jnp.einsum("bhsm,bmhd->bshd", pr, vh).reshape(bsz, seq, D_ATT)
    y_c = o @ w_att_out

    g = jax.nn.sigmoid((p_g + b_gate).reshape(bsz, seq, N_BRANCH, D_MODEL))
    merged = g[:, :, 0] * y_a + g[:, :, 1] * y_b + g[:, :, 2] * y_c
    return merged @ w_o

def _conv_ffn(x, norm_ffn_g, w_up, conv_ffn_w, w_down):
    h = _rmsnorm(x, norm_ffn_g)
    u = _causal_dwconv(h @ w_up, conv_ffn_w)
    gt, up = jnp.split(u, 2, axis=-1)
    return (jax.nn.silu(gt) * up) @ w_down

def first_block(x, mem, norm_mix_g, norm_mem_g, w_in, b_gate, conv_a_w, w_a_out,
              conv_b_w, conv_b_bias, ln_b_g, ln_b_b, w_b_out, w_kv, w_att_out, w_o,
              norm_ffn_g, w_up, conv_ffn_w, w_down, norm_final_g):
    for l in range(DEPTH):
        x = x + _mixer(x, mem, norm_mix_g[l], norm_mem_g[l], w_in[l], b_gate[l],
                       conv_a_w[l], w_a_out[l], conv_b_w[l], conv_b_bias[l],
                       ln_b_g[l], ln_b_b[l], w_b_out[l], w_kv[l], w_att_out[l], w_o[l])
        x = x + _conv_ffn(x, norm_ffn_g[l], w_up[l], conv_ffn_w[l], w_down[l])
    return _rmsnorm(x, norm_final_g)


N_MIXERS = 4
NEG = -1e30
BIG = 1e30
T5_BUCKETS = 32
T5_MAX_DIST = 128
ATTN_HEADS = 16
HEAD_DIM_2 = D_MODEL // ATTN_HEADS
KV_HEADS = 4
GQA = ATTN_HEADS // KV_HEADS
Q_BLOCK = 128
SWA_WINDOW = 128
RWKV_HEAD = 64
RWKV_HEADS = D_MODEL // RWKV_HEAD
RWKV_LORA_W = 64
RWKV_LORA_A = 64
RWKV_GN_EPS = 64e-5
NSA_CMP_LEN = 32
NSA_CMP_STRIDE = 16
NSA_CMP_HIDDEN = 128
NSA_SEL_LEN = 64
NSA_TOPK = 16
NSA_WINDOW = 512
NSA_SEL_QCHUNK = 64
LRU_WIDTH = 1280
LRU_BLOCKS = 16
LRU_BLOCK = LRU_WIDTH // LRU_BLOCKS
LRU_C = 8.0
CONV_WIDTH = 4


def _layers_of(m):
    return len(range(m, DEPTH, N_MIXERS))

def rms_norm(x, g):
    xf = x.astype(jnp.float32)
    y = xf * lax.rsqrt(jnp.mean(xf * xf, axis=-1, keepdims=True) + EPS)
    return (y * g.astype(jnp.float32)).astype(x.dtype)

def t5_bucket(dist):
    max_exact = T5_BUCKETS // 2
    d = jnp.maximum(dist, 0)
    df = jnp.maximum(d, 1).astype(jnp.float32)
    large = max_exact + (jnp.log(df / max_exact) / math.log(T5_MAX_DIST / max_exact)
                         * (T5_BUCKETS - max_exact)).astype(jnp.int32)
    large = jnp.minimum(large, T5_BUCKETS - 1)
    return jnp.where(d < max_exact, d, large)

def q_heads(t, B, T):
    return t.reshape(B, T, KV_HEADS, GQA, HEAD_DIM_2).transpose(0, 2, 3, 1, 4)

def kv_heads(t, B, T):
    return t.reshape(B, T, KV_HEADS, HEAD_DIM_2).transpose(0, 2, 1, 3)

def merge_heads(o, B, T):
    return o.transpose(0, 3, 1, 2, 4).reshape(B, T, ATTN_HEADS * HEAD_DIM_2)

def banded_attention(q, k, v, t5_table, window, sinks=None):
    B, G, R, T, Dh = q.shape
    nb = T // Q_BLOCK
    nprev = -(-window // Q_BLOCK)
    kc = (nprev + 1) * Q_BLOCK
    qb = q.reshape(B, G, R, nb, Q_BLOCK, Dh)
    pad = ((0, 0), (0, 0), (nprev * Q_BLOCK, 0), (0, 0))
    kp = jnp.pad(k, pad).reshape(B, G, nb + nprev, Q_BLOCK, Dh)
    vp = jnp.pad(v, pad).reshape(B, G, nb + nprev, Q_BLOCK, Dh)
    kb = jnp.concatenate([kp[:, :, j:j + nb] for j in range(nprev + 1)], axis=3)
    vb = jnp.concatenate([vp[:, :, j:j + nb] for j in range(nprev + 1)], axis=3)
    s = jnp.einsum('bgrnqd,bgnkd->bgrnqk', qb, kb,
                   preferred_element_type=jnp.float32) * (Dh ** -0.5)
    dist = nprev * Q_BLOCK + jnp.arange(Q_BLOCK)[:, None] - jnp.arange(kc)[None, :]
    kpos = (jnp.arange(nb)[:, None, None] - nprev) * Q_BLOCK + jnp.arange(kc)[None, None, :]
    valid = (dist >= 0) & (dist < window) & (kpos >= 0)
    bias = jnp.take(t5_table, t5_bucket(dist), axis=0)
    bias = jnp.moveaxis(bias, -1, 0).reshape(G, R, Q_BLOCK, kc).astype(jnp.float32)
    s = jnp.where(valid, s + bias[None, :, :, None], NEG)
    if sinks is None:
        p = jax.nn.softmax(s, axis=-1)
    else:
        sk = jnp.broadcast_to(sinks.astype(jnp.float32).reshape(1, G, R, 1, 1, 1), s.shape[:-1] + (1,))
        p = jax.nn.softmax(jnp.concatenate([s, sk], axis=-1), axis=-1)[..., :-1]
    o = jnp.einsum('bgrnqk,bgnkd->bgrnqd', p.astype(v.dtype), vb)
    return o.reshape(B, G, R, T, Dh)

def swa_sink_mixer(xn, w_in, sinks, w_out, t5_table):
    B, T, _ = xn.shape
    nq, nkv = ATTN_HEADS * HEAD_DIM_2, KV_HEADS * HEAD_DIM_2
    q, k, v, z = jnp.split(xn @ w_in, [nq, nq + nkv, nq + 2 * nkv], axis=-1)
    o = banded_attention(q_heads(q, B, T), kv_heads(k, B, T), kv_heads(v, B, T),
                         t5_table, SWA_WINDOW, sinks)
    return (merge_heads(o, B, T) * jax.nn.silu(z)) @ w_out

def rwkv7_mixer(xn, mu, w_in, w0, w1, w2, a0, a1, a2, k_k, k_a, r_k, lnx_w, lnx_b, w_out):
    B, T, D = xn.shape
    H, N = RWKV_HEADS, RWKV_HEAD
    C = H * N
    f32 = jnp.float32
    xx = jnp.pad(xn, ((0, 0), (1, 0), (0, 0)))[:, :-1] - xn
    lerp = xn[None] + xx[None] * mu[:, None, None, :]
    rkvz = jnp.einsum('sbtd,dsc->sbtc', lerp[:4], w_in.reshape(D, 4, C))
    r, k, v, z = rkvz[0], rkvz[1], rkvz[2], rkvz[3]
    w = -jax.nn.softplus(-(w0 + jnp.tanh(lerp[4] @ w1) @ w2)) - 0.5
    a = jax.nn.sigmoid(a0 + (lerp[5] @ a1) @ a2)
    hs = lambda t: t.astype(f32).reshape(B, T, H, N)
    kk = hs(k * k_k)
    kk = kk / jnp.maximum(jnp.sqrt(jnp.sum(kk * kk, axis=-1, keepdims=True)), 1e-12)
    k = hs(k * (1 + (a - 1) * k_a))
    r, v, a = hs(r), hs(v), hs(a)
    decay = jnp.exp(-jnp.exp(hs(w)))
    aa, bb = -kk, kk * a

    def step(S, inp):
        r_t, w_t, k_t, v_t, a_t, b_t = inp
        sa = jnp.einsum('bhij,bhj->bhi', S, a_t)
        S = S * w_t[:, :, None, :] + sa[..., None] * b_t[:, :, None, :] + v_t[..., None] * k_t[:, :, None, :]
        return S, jnp.einsum('bhij,bhj->bhi', S, r_t)

    xs = tuple(jnp.moveaxis(t, 1, 0) for t in (r, decay, k, v, aa, bb))
    _, y = lax.scan(step, jnp.zeros((B, H, N, N), f32), xs)
    y = jnp.moveaxis(y, 0, 1)
    mean = jnp.mean(y, axis=-1, keepdims=True)
    var = jnp.mean(jnp.square(y - mean), axis=-1, keepdims=True)
    y = ((y - mean) * lax.rsqrt(var + RWKV_GN_EPS)).reshape(B, T, C) * lnx_w.astype(f32) + lnx_b.astype(f32)
    bonus = jnp.sum(r * k * r_k.astype(f32), axis=-1, keepdims=True) * v
    y = (y + bonus.reshape(B, T, C)) * jax.nn.silu(z.astype(f32))
    return y.astype(xn.dtype) @ w_out

def nsa_mixer(xn, w_in, cmp_pos_k, cmp_k_w1, cmp_k_w2, cmp_pos_v, cmp_v_w1, cmp_v_w2, w_out, t5_table):
    B, T, _ = xn.shape
    G, R, Dh = KV_HEADS, GQA, HEAD_DIM_2
    f32 = jnp.float32
    nq, nkv = ATTN_HEADS * Dh, G * Dh
    splits = np.cumsum([nq] + [nkv] * 6 + [3 * ATTN_HEADS]).tolist()
    q, kc, vc, ks, vs, kw, vw, gates, z = jnp.split(xn @ w_in, splits, axis=-1)
    q = q_heads(q, B, T)
    kc, vc, ks, vs, kw, vw = (kv_heads(t, B, T) for t in (kc, vc, ks, vs, kw, vw))
    scale = Dh ** -0.5
    tpos = jnp.arange(T)

    n_cmp = (T - NSA_CMP_LEN) // NSA_CMP_STRIDE + 1
    tok_idx = np.arange(n_cmp)[:, None] * NSA_CMP_STRIDE + np.arange(NSA_CMP_LEN)[None, :]

    def compress(t, pos, w1, w2):
        blk = (t[:, :, tok_idx] + pos).reshape(B, G, n_cmp, NSA_CMP_LEN * Dh)
        return jax.nn.silu(blk @ w1) @ w2

    k_cmp = compress(kc, cmp_pos_k, cmp_k_w1, cmp_k_w2)
    v_cmp = compress(vc, cmp_pos_v, cmp_v_w1, cmp_v_w2)
    cmp_start = jnp.arange(n_cmp) * NSA_CMP_STRIDE
    cmp_end = cmp_start + NSA_CMP_LEN - 1
    cmp_ok = cmp_end[None, :] <= tpos[:, None]
    s_c = jnp.einsum('bgrtd,bgnd->bgrtn', q, k_cmp, preferred_element_type=f32) * scale
    p_c = jax.nn.softmax(jnp.where(cmp_ok, s_c, NEG), axis=-1) * cmp_ok
    o_cmp = jnp.einsum('bgrtn,bgnd->bgrtd', p_c.astype(v_cmp.dtype), v_cmp)

    n_sel = T // NSA_SEL_LEN
    k_top = min(NSA_TOPK, n_sel)
    sel_start = jnp.arange(n_sel) * NSA_SEL_LEN
    overlap = ((cmp_start[:, None] < sel_start[None, :] + NSA_SEL_LEN)
               & (cmp_end[:, None] >= sel_start[None, :])).astype(f32)
    imp = jnp.einsum('bgrtn,ns->bgts', p_c, overlap)
    blk = jnp.arange(n_sel)[None, :]
    cur = (tpos // NSA_SEL_LEN)[:, None]
    forced = (blk == 0) | (blk == cur) | (blk == cur - 1)
    future = sel_start[None, :] > tpos[:, None]
    imp = jnp.where(forced, BIG, jnp.where(future, NEG, imp))
    _, sel_idx = lax.top_k(imp, k_top)

    ks_blk = ks.reshape(B, G, n_sel, NSA_SEL_LEN, Dh)
    vs_blk = vs.reshape(B, G, n_sel, NSA_SEL_LEN, Dh)
    QC = NSA_SEL_QCHUNK
    nch = T // QC
    q_ch = jnp.moveaxis(q.reshape(B, G, R, nch, QC, Dh), 3, 0)
    idx_ch = jnp.moveaxis(sel_idx.reshape(B, G, nch, QC, k_top), 2, 0)
    pos_ch = tpos.reshape(nch, QC)
    bi = jnp.arange(B)[:, None, None, None]
    gi = jnp.arange(G)[None, :, None, None]
    gi5 = jnp.arange(G)[None, :, None, None, None]
    table_g = t5_table.reshape(T5_BUCKETS, G, R)

    def sel_chunk(args):
        qc, ic, pc = args
        kg = ks_blk[bi, gi, ic]
        vg = vs_blk[bi, gi, ic]
        kpos = ic[..., None] * NSA_SEL_LEN + jnp.arange(NSA_SEL_LEN)
        dist = pc[None, None, :, None, None] - kpos
        s = jnp.einsum('bgrqd,bgqskd->bgrqsk', qc, kg, preferred_element_type=f32) * scale
        bias = jnp.moveaxis(table_g[t5_bucket(dist), gi5], -1, 2).astype(f32)
        s = jnp.where((dist >= 0)[:, :, None], s + bias, NEG)
        p = jax.nn.softmax(s.reshape(B, G, R, QC, k_top * NSA_SEL_LEN), axis=-1)
        p = p.reshape(B, G, R, QC, k_top, NSA_SEL_LEN)
        return jnp.einsum('bgrqsk,bgqskd->bgrqd', p.astype(vg.dtype), vg)

    o_sel = lax.map(sel_chunk, (q_ch, idx_ch, pos_ch))
    o_sel = jnp.moveaxis(o_sel, 0, 3).reshape(B, G, R, T, Dh)

    o_win = banded_attention(q, kw, vw, t5_table, NSA_WINDOW)

    g = jax.nn.sigmoid(gates).reshape(B, T, 3, G, R).transpose(2, 0, 3, 4, 1)[..., None]
    o = g[0] * o_cmp + g[1] * o_sel + g[2] * o_win
    return (merge_heads(o, B, T) * jax.nn.silu(z)) @ w_out

def rglru_mixer(xn, w_in, conv_w, conv_b, gate_a_w, gate_a_b, gate_x_w, gate_x_b, lam, w_out):
    B, T, _ = xn.shape
    f32 = jnp.float32
    u, z = jnp.split(xn @ w_in, 2, axis=-1)
    u = lax.conv_general_dilated(u, conv_w[:, None, :], window_strides=(1,),
                                 padding=[(CONV_WIDTH - 1, 0)],
                                 dimension_numbers=('NWC', 'WIO', 'NWC'),
                                 feature_group_count=LRU_WIDTH) + conv_b
    ub = u.reshape(B, T, LRU_BLOCKS, LRU_BLOCK)
    r = jax.nn.sigmoid(jnp.einsum('btnc,ncd->btnd', ub, gate_a_w).reshape(B, T, LRU_WIDTH) + gate_a_b)
    i = jax.nn.sigmoid(jnp.einsum('btnc,ncd->btnd', ub, gate_x_w).reshape(B, T, LRU_WIDTH) + gate_x_b)
    log_a = -LRU_C * r.astype(f32) * jax.nn.softplus(-lam.astype(f32))
    a = jnp.exp(log_a)
    b = jnp.sqrt(-jnp.expm1(2.0 * log_a)) * (i * u).astype(f32)

    def combine(left, right):
        a1, b1 = left
        a2, b2 = right
        return a1 * a2, a2 * b1 + b2

    _, h = lax.associative_scan(combine, (a, b), axis=1)
    return (h.astype(xn.dtype) * jax.nn.silu(z)) @ w_out

def second_inputs(seed: int = 0) -> dict:
    key = jax.random.key(seed)
    keys = iter(jax.random.split(key, 64))
    f32 = jnp.float32

    def nrm(shape, scale):
        return jax.random.normal(next(keys), shape, f32) * scale

    def dense(shape):
        return nrm(shape, shape[-2] ** -0.5)

    def unif(shape, lo, hi):
        return jax.random.uniform(next(keys), shape, f32, lo, hi)

    LA, LB, LC, LD = (_layers_of(m) for m in range(N_MIXERS))
    C = RWKV_HEADS * RWKV_HEAD
    nq, nkv = ATTN_HEADS * HEAD_DIM_2, KV_HEADS * HEAD_DIM_2
    a_cols = 2 * nq + 2 * nkv
    c_cols = 2 * nq + 6 * nkv + 3 * ATTN_HEADS
    lam_u = unif((LD, LRU_WIDTH), 0.9, 0.999)
    return {
        "x": nrm((BATCH, SEQ, D_MODEL), 1.0),
        "t5_table": nrm((T5_BUCKETS, ATTN_HEADS), 0.5),
        "norm_g": 1.0 + nrm((DEPTH, D_MODEL), 0.05),
        "final_g": 1.0 + nrm((D_MODEL,), 0.05),
        "a_w_in": dense((LA, D_MODEL, a_cols)),
        "a_sinks": nrm((LA, ATTN_HEADS), 0.5),
        "a_w_out": dense((LA, nq, D_MODEL)),
        "b_mu": unif((LB, 6, D_MODEL), 0.0, 1.0),
        "b_w_in": dense((LB, D_MODEL, 4 * C)),
        "b_w0": unif((LB, C), -6.0, 0.0),
        "b_w1": dense((LB, D_MODEL, RWKV_LORA_W)),
        "b_w2": dense((LB, RWKV_LORA_W, C)),
        "b_a0": nrm((LB, C), 0.5),
        "b_a1": dense((LB, D_MODEL, RWKV_LORA_A)),
        "b_a2": dense((LB, RWKV_LORA_A, C)),
        "b_k_k": 0.85 + nrm((LB, C), 0.1),
        "b_k_a": 1.0 + nrm((LB, C), 0.1),
        "b_r_k": nrm((LB, RWKV_HEADS, RWKV_HEAD), 0.1),
        "b_lnx_w": 1.0 + nrm((LB, C), 0.05),
        "b_lnx_b": nrm((LB, C), 0.01),
        "b_w_out": dense((LB, C, D_MODEL)),
        "c_w_in": dense((LC, D_MODEL, c_cols)),
        "c_cmp_pos_k": nrm((LC, NSA_CMP_LEN, HEAD_DIM_2), 0.1),
        "c_cmp_k_w1": dense((LC, NSA_CMP_LEN * HEAD_DIM_2, NSA_CMP_HIDDEN)),
        "c_cmp_k_w2": dense((LC, NSA_CMP_HIDDEN, HEAD_DIM_2)),
        "c_cmp_pos_v": nrm((LC, NSA_CMP_LEN, HEAD_DIM_2), 0.1),
        "c_cmp_v_w1": dense((LC, NSA_CMP_LEN * HEAD_DIM_2, NSA_CMP_HIDDEN)),
        "c_cmp_v_w2": dense((LC, NSA_CMP_HIDDEN, HEAD_DIM_2)),
        "c_w_out": dense((LC, nq, D_MODEL)),
        "d_w_in": dense((LD, D_MODEL, 2 * LRU_WIDTH)),
        "d_conv_w": nrm((LD, CONV_WIDTH, LRU_WIDTH), CONV_WIDTH ** -0.5),
        "d_conv_b": nrm((LD, LRU_WIDTH), 0.01),
        "d_gate_a_w": dense((LD, LRU_BLOCKS, LRU_BLOCK, LRU_BLOCK)),
        "d_gate_a_b": nrm((LD, LRU_WIDTH), 0.01),
        "d_gate_x_w": dense((LD, LRU_BLOCKS, LRU_BLOCK, LRU_BLOCK)),
        "d_gate_x_b": nrm((LD, LRU_WIDTH), 0.01),
        "d_lambda": jnp.log(lam_u) - jnp.log1p(-lam_u),
        "d_w_out": dense((LD, LRU_WIDTH, D_MODEL)),
    }

def second_block(x, t5_table, norm_g, final_g,
              a_w_in, a_sinks, a_w_out,
              b_mu, b_w_in, b_w0, b_w1, b_w2, b_a0, b_a1, b_a2, b_k_k, b_k_a, b_r_k,
              b_lnx_w, b_lnx_b, b_w_out,
              c_w_in, c_cmp_pos_k, c_cmp_k_w1, c_cmp_k_w2, c_cmp_pos_v, c_cmp_v_w1, c_cmp_v_w2, c_w_out,
              d_w_in, d_conv_w, d_conv_b, d_gate_a_w, d_gate_a_b, d_gate_x_w, d_gate_x_b,
              d_lambda, d_w_out):
    for layer in range(DEPTH):
        m, j = layer % N_MIXERS, layer // N_MIXERS
        xn = rms_norm(x, norm_g[layer])
        if m == 0:
            y = swa_sink_mixer(xn, a_w_in[j], a_sinks[j], a_w_out[j], t5_table)
        elif m == 1:
            y = rwkv7_mixer(xn, b_mu[j], b_w_in[j], b_w0[j], b_w1[j], b_w2[j], b_a0[j], b_a1[j],
                            b_a2[j], b_k_k[j], b_k_a[j], b_r_k[j], b_lnx_w[j], b_lnx_b[j], b_w_out[j])
        elif m == 2:
            y = nsa_mixer(xn, c_w_in[j], c_cmp_pos_k[j], c_cmp_k_w1[j], c_cmp_k_w2[j],
                          c_cmp_pos_v[j], c_cmp_v_w1[j], c_cmp_v_w2[j], c_w_out[j], t5_table)
        else:
            y = rglru_mixer(xn, d_w_in[j], d_conv_w[j], d_conv_b[j], d_gate_a_w[j], d_gate_a_b[j],
                            d_gate_x_w[j], d_gate_x_b[j], d_lambda[j], d_w_out[j])
        x = x + y.astype(x.dtype)
    return rms_norm(x, final_g)


def setup_inputs(seed=0):
    out = dict(first_inputs(seed))
    for name, value in second_inputs(seed + 1).items():
        if name != "x":
            out[name + "_2"] = value
    return out


def reference(
    x, mem, norm_mix_g, norm_mem_g, w_in, b_gate, conv_a_w, w_a_out, conv_b_w, conv_b_bias,
    ln_b_g, ln_b_b, w_b_out, w_kv, w_att_out, w_o, norm_ffn_g, w_up, conv_ffn_w, w_down,
    norm_final_g, t5_table_2, norm_g_2, final_g_2, a_w_in_2, a_sinks_2, a_w_out_2, b_mu_2,
    b_w_in_2, b_w0_2, b_w1_2, b_w2_2, b_a0_2, b_a1_2, b_a2_2, b_k_k_2, b_k_a_2, b_r_k_2,
    b_lnx_w_2, b_lnx_b_2, b_w_out_2, c_w_in_2, c_cmp_pos_k_2, c_cmp_k_w1_2, c_cmp_k_w2_2,
    c_cmp_pos_v_2, c_cmp_v_w1_2, c_cmp_v_w2_2, c_w_out_2, d_w_in_2, d_conv_w_2, d_conv_b_2,
    d_gate_a_w_2, d_gate_a_b_2, d_gate_x_w_2, d_gate_x_b_2, d_lambda_2, d_w_out_2,
):
    x = first_block(
        x, mem, norm_mix_g, norm_mem_g, w_in, b_gate, conv_a_w, w_a_out, conv_b_w, conv_b_bias,
        ln_b_g, ln_b_b, w_b_out, w_kv, w_att_out, w_o, norm_ffn_g, w_up, conv_ffn_w, w_down,
        norm_final_g,
    )
    return second_block(
        x, t5_table_2, norm_g_2, final_g_2, a_w_in_2, a_sinks_2, a_w_out_2, b_mu_2, b_w_in_2,
        b_w0_2, b_w1_2, b_w2_2, b_a0_2, b_a1_2, b_a2_2, b_k_k_2, b_k_a_2, b_r_k_2, b_lnx_w_2,
        b_lnx_b_2, b_w_out_2, c_w_in_2, c_cmp_pos_k_2, c_cmp_k_w1_2, c_cmp_k_w2_2,
        c_cmp_pos_v_2, c_cmp_v_w1_2, c_cmp_v_w2_2, c_w_out_2, d_w_in_2, d_conv_w_2, d_conv_b_2,
        d_gate_a_w_2, d_gate_a_b_2, d_gate_x_w_2, d_gate_x_b_2, d_lambda_2, d_w_out_2,
    )


_drawn_inputs = setup_inputs


def setup_inputs(seed=0):
    import zlib

    import numpy as np

    out = dict(_drawn_inputs(seed))
    spreads = {}
    factors = {'norm_mix_g': 2.859,
     'norm_mem_g': 8.0,
     'b_gate': 8.0,
     'conv_b_bias': 4.177,
     'ln_b_g': 7.733,
     'ln_b_b': 8.0,
     'norm_ffn_g': 4.333,
     'norm_final_g': 2.913,
     'norm_g_2': 5.023,
     'a_sinks_2': 33.825}
    for name, (base, spread) in spreads.items():
        noise = np.random.default_rng([zlib.crc32(name.encode()), seed]).standard_normal(out[name].shape)
        drawn = base * np.exp(spread * noise) if base else spread * noise
        out[name] = __import__('jax').numpy.asarray(drawn.astype(out[name].dtype))
    for name, factor in factors.items():
        out[name] = (out[name] * factor).astype(out[name].dtype)
    return out
```

```python
from contextlib import ExitStack

import concourse.bass as bass
from concourse import mybir

F32 = mybir.dt.float32
F32R = mybir.dt.float32r
ALU = mybir.AluOpType
ACT = mybir.ActivationFunctionType
AX_X = mybir.AxisListType.X

P = 128
SEQ = 512
D = 1024
KT = D // P
MEM = 256
TAPS = 31
F_TILES = 22
HEADS_A, HEADS_B, KV_B = 4, 16, 4
WINDOW = 128
EPS = 1e-6
NEG = -1e30
UNIT = KT * P
SLOTS = 4

R_LONG = 0
R_Q = 4
R_KV = 6
R_SHORT = 10
R_MIX_A = 16
R_MIX_C = 20
R_MIX_B = 24
R_OUT = 28
R_UP = 30
R_DOWN = 41
R_QKV = 47
R_Z = 50
R_LAST = 52
ROUNDS = 54
DOWN_SKIPS = 4

PARAMS = {}
_at = 0
for _name, _n in (("g_mix", KT), ("g_mem", KT), ("long_w", KT * TAPS), ("long_b", KT), ("ln_g", KT), ("ln_b", KT),
                  ("gate_b", 3 * KT), ("short_w", 3 * KT), ("g_ffn", KT), ("ffn_w", 3 * 2 * F_TILES),
                  ("g_final", KT), ("g_second", KT), ("g_last", KT), ("sinks", HEADS_B)):
    PARAMS[_name] = _at
    _at += _n
N_PARAMS = _at

N_X, N_MEM, N_LN, N_FFN, N_FINAL, N_SECOND, N_LAST = range(7)


def build(nc, weights, x, mem, params, consts, table, onehot, out):
    with ExitStack() as ctx:
        base = 16512
        top = [0]

        def sb(name, shape, dt, kb=None):
            n = 4
            for v in shape[1:]:
                n *= v
            if kb is None:
                at = TEMPS + top[0]
                top[0] += (n + 31) // 32 * 32
            else:
                at = int(kb * 1024)
            return nc.alloc_sbuf_tensor_at(name, shape, dt, offset=base + at)

        TEMPS = 185 * 1024

        def sem(name):
            return ctx.enter_context(nc.semaphore(name))

        raw = [sb(f"w_raw{s}", [P, UNIT], F32, 4 * s) for s in range(SLOTS)]
        w_high = [sb(f"w_high{s}", [P, UNIT], F32R, 16 + 4 * s) for s in range(SLOTS)]
        w_low = [sb(f"w_low{s}", [P, UNIT], F32R, 32 + 4 * s) for s in range(SLOTS)]
        h_high = sb("h_high", [P, KT, SEQ], F32R, 48)
        h_low = sb("h_low", [P, KT, SEQ], F32R, 64)
        long_u = sb("long_u", [P, KT, SEQ + 1], F32, 80)
        x_in = sb("x_in", [P, KT, SEQ], F32, 97)
        q = sb("q", [P, KT, SEQ], F32, 97)
        o_high = sb("o_high", [P, KT, SEQ], F32R, 97)
        mem_high = sb("mem_high", [P, KT, MEM], F32R, 113)
        mem_low = sb("mem_low", [P, KT, MEM], F32R, 121)
        o_low = sb("o_low", [P, KT, SEQ], F32R, 113)
        ya_high = sb("ya_high", [P, KT, SEQ], F32R, 129)
        ya_low = sb("ya_low", [P, KT, SEQ], F32R, 145)
        yb_high = sb("yb_high", [P, KT, SEQ], F32R, 129)
        yb_low = sb("yb_low", [P, KT, SEQ], F32R, 145)
        mem_in = sb("mem_in", [P, KT, MEM], F32, 161)
        k_mem = sb("k_mem", [P, KT, MEM], F32, 161)
        v_mem = sb("v_mem", [P, 2, D], F32, 169)
        merged = sb("merged", [P, KT, SEQ], F32, 161)
        m_high = sb("m_high", [P, KT, SEQ], F32R, 97)
        m_low = sb("m_low", [P, KT, SEQ], F32R, 113)
        x1 = sb("x1", [P, KT, SEQ], F32, 80)
        f_high = sb("f_high", [P, F_TILES, SEQ], F32R, 97)
        f_low = sb("f_low", [P, F_TILES, SEQ], F32R, 141)
        x2 = sb("x2", [P, KT, SEQ], F32, 48)
        bias = sb("bias", [P, HEADS_B, 2 * P], F32, 64)
        y_res = sb("y_res", [P, KT, SEQ], F32, 80)
        xn_high = sb("xn_high", [P, KT, SEQ], F32R, 97)
        xn_low = sb("xn_low", [P, KT, SEQ], F32R, 113)
        q2 = sb("q2", [P, KT, SEQ], F32, 129)
        k2 = sb("k2", [P, 2, SEQ], F32, 145)
        v2 = sb("v2", [P, 4, 2 * P], F32, 149)
        z = sb("z", [P, KT, SEQ], F32, 153)
        o2 = sb("o2", [P, KT, SEQ], F32, 48)
        o2_high = sb("o2_high", [P, KT, SEQ], F32R, 97)
        o2_low = sb("o2_low", [P, KT, SEQ], F32R, 113)
        x3 = sb("x3", [P, KT, SEQ], F32, 129)
        result = sb("result", [P, KT, SEQ], F32, 153)
        probs = sb("probs", [P, 4, 2 * P], F32, 177)
        probs_t = sb("probs_t", [P, 2, SEQ], F32, 181)

        par = sb("par", [P, N_PARAMS], F32)
        ones_sb = sb("ones_sb", [P, P], F32)
        ident_sb = sb("ident_sb", [P, P], F32, 96.25)
        gate = sb("gate", [P, 2, SEQ], F32)
        conv_acc = sb("conv_acc", [P, SEQ], F32)
        conv_sum = sb("conv_sum", [P, SEQ], F32)
        part = sb("part", [P, 2, SEQ], F32)
        square = sb("square", [P, 2, SEQ], F32)
        sum_sq = sb("sum_sq", [P, SEQ], F32)
        rstd = sb("rstd", [P, SEQ], F32)
        small = sb("small", [P, 6, 4], F32)
        assert TEMPS + top[0] + base <= 229344, TEMPS + top[0] + base - 229344
        short_c = gate[:, 0, :]
        short_t = gate[:, 1, :]
        short_y = square[:, 0, :]
        mean = conv_sum
        ffn_y = [gate[:, 0, :], gate[:, 1, :], conv_acc[:, :], conv_sum[:, :]]
        strip = sb("strip", [HEADS_B, 3 * P], F32, 64)
        table_sb = sb("table_sb", [32, HEADS_B], F32, 66)
        onehot_sb = sb("onehot_sb", [32, 3 * P], F32, 68)
        neg_sb = sb("neg_sb", [HEADS_B, 3 * P], F32, 70)
        ones, ident = ones_sb[:, :], ident_sb[:, :]

        def col(name, j):
            return par[:, bass.ds(j + PARAMS[name], 1)]

        acc = ctx.enter_context(nc.psum_tensor("acc", [P, SLOTS, SEQ], F32))
        side = ctx.enter_context(nc.psum_tensor("side", [P, 4, SEQ], F32))
        strip_dram = nc.dram_tensor("strip_dram", [HEADS_B, 3 * P], F32, kind="Internal")

        rows_dram = nc.dram_tensor("rows_dram", [P, HEADS_B * 3 * P], F32, kind="Internal")

        landed = [sem(f"weights_landed{s}") for s in range(SLOTS)]
        weight_high = sem("weight_high")
        weight_low = sem("weight_low")
        unit_done = sem("unit_done")
        taken = [sem(f"result_taken{s}") for s in range(SLOTS)]
        x_landed = [sem(f"x_landed{i}") for i in range(4)]
        x_again = sem("x_again")
        mem_landed = sem("mem_landed")
        par_landed = sem("par_landed")
        pads_set = sem("pads_set")
        squared = sem("squared")
        square_added = sem("square_added")
        sum_cleared = sem("sum_cleared")
        stat_done = sem("stat_done")
        stat_read = sem("stat_read")
        recip_done = sem("recip_done")
        rstd_ready = sem("rstd_ready")
        scaled = sem("scaled")
        act_high = sem("act_high")
        act_low = sem("act_low")
        conv_step = sem("conv_step")
        short_step = sem("short_step")
        short_high = sem("short_high")
        short_low = sem("short_low")
        merge_part = sem("merge_part")
        merge_done = sem("merge_done")
        merged_high = sem("merged_high")
        merged_low = sem("merged_low")
        mean_done = sem("mean_done")
        mean_read = sem("mean_read")
        centred = sem("centred")
        ln_scaled = sem("ln_scaled")
        ln_silu = sem("ln_silu")
        ln_high = sem("ln_high")
        ln_low = sem("ln_low")
        scores_done = sem("scores_done")
        row_max = sem("row_max")
        exp_done = sem("exp_done")
        recip_rows = sem("recip_rows")
        probs_ready = sem("probs_ready")
        probs_turned = sem("probs_turned")
        turned_act = sem("turned_act")
        turned_dve = sem("turned_dve")
        pv_done = sem("pv_done")
        o_high_done = sem("o_high_done")
        o_low_done = sem("o_low_done")
        ffn_first = sem("ffn_first")
        ffn_step = sem("ffn_step")
        ffn_silu = sem("ffn_silu")
        ffn_mul = sem("ffn_mul")
        ffn_high = sem("ffn_high")
        ffn_low = sem("ffn_low")
        tables_landed = sem("tables_landed")
        strip_done = sem("strip_done")
        strip_ready = sem("strip_ready")
        strip_stored = sem("strip_stored")
        bias_landed = sem("bias_landed")
        y_ready = sem("y_ready")
        sw_scores = sem("sw_scores")
        sw_step = sem("sw_step")
        sw_exp = sem("sw_exp")
        sw_probs = sem("sw_probs")
        sw_turned = sem("sw_turned")
        sw_turned_act = sem("sw_turned_act")
        sw_turned_dve = sem("sw_turned_dve")
        sw_pv = sem("sw_pv")
        sw_out = sem("sw_out")
        z_silu = sem("z_silu")
        gated = sem("gated")
        gated_high = sem("gated_high")
        gated_low = sem("gated_low")
        result_ready = sem("result_ready")
        stored = sem("stored")

        def uses(m):
            return m - DOWN_SKIPS if isinstance(m, int) and m >= R_QKV else m

        def at_least(eng, s, n):
            if not isinstance(n, int) or n > 0:
                eng.wait_ge(s, n)

        def older(step):
            return sum(1 for t in range(step) if t % 8 >= 2)

        block = ctx.enter_context(nc.Block())

        @block.sync
        def _(sp):
            for i in range(4):
                sp.dma_start(x_in[:, 2 * i:2 * i + 2, :], x[:, 2 * i:2 * i + 2, :]).then_inc(x_landed[i], 16)
            for s in range(SLOTS):
                sp.dma_start(raw[s][:, :], weights[s]).then_inc(landed[s], 16)
            with sp.Fori(1, ROUNDS) as m:
                for s in range(SLOTS):
                    sp.wait_ge(weight_low, 4 * m + (s - 3))
                    sp.dma_start(raw[s][:, :], weights[4 * m + s]).then_inc(landed[s], 16)
            for j in range(KT):
                sp.wait_ge(result_ready, j + 1)
                sp.dma_start(out[:, j, :], result[:, j, :]).then_inc(stored, 16)
            sp.wait_ge(stored, 16 * KT)

        @block.gpsimd
        def _(pool):
            pool.dma_start(par[:, :], params).then_inc(par_landed, 16)
            pool.dma_start(ones, consts[:, 0:P]).then_inc(par_landed, 16)
            pool.dma_start(ident, consts[:, P:2 * P]).then_inc(par_landed, 16)
            pool.dma_start(mem_in[:, :, :], mem).then_inc(mem_landed, 16)
            pool.memset(long_u[:, :, 0:1], 0.0).then_inc(pads_set, 1)
            pool.memset(conv_sum[:, :], 0.0).then_inc(pads_set, 1)
            pool.wait_ge(ln_low, KT)
            pool.dma_start(x1[:, :, :], x).then_inc(x_again, 16)
            pool.wait_ge(unit_done, 4 * R_DOWN)
            pool.dma_start(table_sb[:, :], table).then_inc(tables_landed, 16)
            pool.dma_start(onehot_sb[:, :], onehot[0:32, :]).then_inc(tables_landed, 16)
            pool.dma_start(neg_sb[:, :], onehot[32:48, :]).then_inc(tables_landed, 16)
            pool.wait_ge(strip_ready, 1)
            pool.dma_start(strip_dram[:, :], strip[:, :]).then_inc(strip_stored, 16)
            pool.wait_ge(strip_stored, 16)
            row = HEADS_B * 3 * P
            pool.dma_start(rows_dram[:, :], bass.AP(strip_dram, 0, [[0, P], [1, row]])).then_inc(strip_stored, 16)
            pool.wait_ge(strip_stored, 32)
            toeplitz = bass.AP(rows_dram, P - 1, [[row - 1, P], [3 * P, HEADS_B], [1, 2 * P]])
            pool.dma_start(bias[:, :, :], toeplitz).then_inc(bias_landed, 16)
            pool.wait_ge(bias_landed, 16)

        @block.scalar
        def _(act):
            def round_high(m, s):
                if isinstance(m, int) and m >= ROUNDS:
                    return
                act.wait_ge(landed[s], 16 * m + 16)
                at_least(act, unit_done, 4 * m + (s - 3))
                act.activation(w_high[s][:, :], raw[s][:, :], ACT.Copy).then_inc(weight_high, 1)

            def ahead(m, s):
                round_high(m + (s + 2) // 4, (s + 2) % 4)

            def squares(norm, k, src, width, *waits):
                n = KT * norm + k
                for w in waits:
                    act.wait_ge(*w)
                at_least(act, square_added, n - 1)
                act.activation(square[:, k % 2, 0:width], src, ACT.Square).then_inc(squared, 1)

            def root(norm, width):
                act.wait_ge(recip_done, norm + 1)
                act.activation(rstd[:, 0:width], rstd[:, 0:width], ACT.Sqrt).then_inc(rstd_ready, 1)

            def high_tiles(first, high, width):
                for k in range(KT):
                    act.wait_ge(scaled, first + k + 1)
                    act.activation(high[:, k, :], part[:, k % 2, 0:width], ACT.Copy).then_inc(act_high, 1)

            def gate_of(m, half, bias_col=None):
                act.wait_ge(unit_done, 4 * m + (2 * half + 1))
                at_least(act, taken[2 * half + 1], m)
                act.activation(gate[:, half, :], acc[:, 2 * half, :], ACT.Sigmoid,
                               bias=0.0 if bias_col is None else bias_col).then_inc(taken[2 * half], 1)

            round_high(0, 0)
            act.wait_ge(par_landed, 48)
            for k in range(KT):
                squares(N_X, k, x_in[:, k, :], SEQ, (x_landed[k // 2], 16))
            round_high(0, 1)
            root(N_X, SEQ)
            high_tiles(0, h_high, SEQ)
            for k in range(KT):
                squares(N_MEM, k, mem_in[:, k, :], MEM, (mem_landed, 16))

            def long_round(m):
                for s in range(SLOTS):
                    ahead(m, s)
                    if s % 2 == 1:
                        gate_of(m, s // 2)

            long_round(0)
            root(N_MEM, MEM)
            high_tiles(KT, mem_high, MEM)
            with act.Fori(1, R_Q) as m:
                long_round(m)

            def take_q(m):
                for s in range(SLOTS):
                    ahead(m, s)
                    act.wait_ge(unit_done, 4 * m + (s + 1))
                    act.activation(q[:, 4 * m + (s - 4 * R_Q), :], acc[:, s, :], ACT.Copy,
                                   scale=1.0 / 16).then_inc(taken[s], 1)

            with act.Fori(R_Q, R_KV) as m:
                take_q(m)
            with act.Fori(R_KV, R_KV + 2) as m:
                for s in range(SLOTS):
                    ahead(m, s)
                    act.wait_ge(unit_done, 4 * m + (s + 1))
                    act.activation(k_mem[:, 4 * m + (s - 4 * R_KV), :], acc[:, s, 0:MEM], ACT.Copy)\
                       .then_inc(taken[s], 1)
            for m in range(R_KV + 2, R_SHORT):
                for s in range(SLOTS):
                    ahead(m, s)
                    j = 4 * (m - R_KV - 2) + s
                    act.wait_ge(unit_done, 4 * m + s + 1)
                    act.activation(v_mem[:, :, j * P:(j + 1) * P],
                                   acc[:, s, 0:2 * P].rearrange("p (a c) -> p a c", a=2), ACT.Copy)\
                       .then_inc(taken[s], 1)

            def attend(head, stage):
                if stage == 1:
                    act.wait_ge(scores_done, head + 1)
                    act.wait_ge(row_max, head + 1)
                    for t in range(4):
                        act.activation(probs[:, t, :], side[:, t // 2, MEM * (t % 2):MEM * (t % 2) + MEM], ACT.Exp,
                                       bias=small[:, 0, t:t + 1], accum_out=small[:, 1, t:t + 1])\
                           .then_inc(exp_done, 1)
                if stage == 3:
                    act.wait_ge(probs_turned, head + 1)
                    at_least(act, pv_done, head)
                    act.activation(probs_t[:, 0, :], side[:, 2, :], ACT.Copy).then_inc(turned_act, 1)
                if stage == 5:
                    act.wait_ge(pv_done, head + 1)
                    for d in range(2):
                        act.activation(o_high[:, 2 * head + d, :], side[:, d, :], ACT.Copy)\
                           .then_inc(o_high_done, 1)

            def short_body(i):
                for e in range(12):
                    m, s, tile, what = 3 * i + (R_SHORT + e // 4), e % 4, 4 * i + e // 3, e % 3
                    ahead(m, s)
                    if what == 0:
                        act.wait_ge(unit_done, 4 * m + (s + 1))
                        at_least(act, short_step, 4 * tile - 3)
                        if tile == 0:
                            act.wait_ge(taken[1], R_SHORT)
                        act.activation(short_c, acc[:, s, :], ACT.Copy).then_inc(taken[s], 1)
                    if what == 2:
                        act.wait_ge(short_step, 4 * tile + 4)
                        act.activation(ya_high[:, tile, :], part[:, e // 3 % 2, :], ACT.Copy)\
                           .then_inc(short_high, 1)
                    attend(2 * i + e // 6, e % 6)

            for i in range(2):
                short_body(i)

            def mix_round(m, first, branch, extra=None):
                for s in range(SLOTS):
                    ahead(m, s)
                    if s % 2 == 1:
                        gate_of(m, s // 2, col("gate_b", 2 * m + (s // 2 - 2 * first + KT * branch)))
                    if extra:
                        extra(m, s)

            def merge_high(m, s):
                if s % 2 == 1:
                    j = 2 * m + (s // 2 - 2 * R_MIX_B)
                    act.wait_ge(merge_done, j + (KT + 1))
                    act.activation(m_high[:, j, :], merged[:, j, :], ACT.Copy).then_inc(merged_high, 1)

            with act.Fori(R_MIX_A, R_MIX_C) as m:
                mix_round(m, R_MIX_A, 0)

            def centre_squares(m, s):
                for k in (2 * s, 2 * s + 1):
                    squares(N_LN, k, long_u[:, k, 1:SEQ + 1], SEQ, (centred, k + 1))

            def ln_tile(m, s):
                k = 4 * m + (s - 4 * (R_MIX_C + 2))
                act.wait_ge(ln_scaled, k + 1)
                act.activation(part[:, s % 2, :], part[:, s % 2, :], ACT.Silu, bias=col("ln_b", k),
                               scale=col("ln_g", k)).then_inc(ln_silu, 1)
                act.wait_ge(ln_silu, k + 1)
                act.activation(yb_high[:, k, :], part[:, s % 2, :], ACT.Copy).then_inc(ln_high, 1)

            mix_round(R_MIX_C, R_MIX_C, 2)
            mix_round(R_MIX_C + 1, R_MIX_C, 2, centre_squares)
            root(N_LN, SEQ)
            with act.Fori(R_MIX_C + 2, R_MIX_B) as m:
                mix_round(m, R_MIX_C, 2, ln_tile)
            with act.Fori(R_MIX_B, R_OUT) as m:
                mix_round(m, R_MIX_B, 1, merge_high)

            def residual_round(m, first, norm, src):
                for s in range(SLOTS):
                    ahead(m, s)
                    n = 4 * m + (s - 4 * first)
                    act.wait_ge(taken[s], uses(first) + 1 + (m - first))
                    at_least(act, square_added, n + (KT * norm - 1))
                    act.activation(square[:, s % 2, :], src[:, n, :], ACT.Square).then_inc(squared, 1)

            with act.Fori(R_OUT, R_UP) as m:
                residual_round(m, R_OUT, N_FFN, x1)
            root(N_FFN, SEQ)
            high_tiles(2 * KT, h_high, SEQ)

            def up_round(m):
                for s in range(SLOTS):
                    ahead(m, s)
                    half = s // 2
                    j = 2 * m + (half - 2 * R_UP)
                    w = 3 * j + (3 * F_TILES * (s % 2) + 2)
                    act.wait_ge(unit_done, 4 * m + (s + 1))
                    at_least(act, ffn_mul, 2 * m + (half - 2 * R_UP - 1))
                    act.activation(ffn_y[s], acc[:, s, :], ACT.Copy, scale=col("ffn_w", w)).then_inc(ffn_first, 1)
                    if s % 2 == 1:
                        act.wait_ge(taken[s - 1], m + 1)
                        act.activation(ffn_y[s - 1], ffn_y[s - 1], ACT.Silu).then_inc(ffn_silu, 1)
                        act.wait_ge(ffn_mul, j + 1)
                        act.activation(f_high[:, j, :], part[:, half, :], ACT.Copy).then_inc(ffn_high, 1)

            up_round(R_UP)
            with act.Fori(R_UP + 1, R_DOWN) as m:
                up_round(m)

            def down_body(i):
                for e in range(12):
                    m, s, n = 3 * i + (R_DOWN + e // 4), e % 4, 4 * i + e // 3
                    ahead(m, s)
                    if e % 3 == 2:
                        act.wait_ge(taken[e // 3], i + (R_DOWN + 1))
                        at_least(act, square_added, n + (KT * N_FINAL - 1))
                        act.activation(square[:, e // 3 % 2, :], x2[:, n, :], ACT.Square).then_inc(squared, 1)

            with act.Fori(0, 2) as i:
                down_body(i)
            root(N_FINAL, SEQ)
            for k in range(KT):
                squares(N_SECOND, k, y_res[:, k, :], SEQ, (y_ready, k + 1))
            root(N_SECOND, SEQ)
            high_tiles(3 * KT, xn_high, SEQ)

            for m in range(R_QKV, R_QKV + 2):
                for s in range(SLOTS):
                    ahead(m, s)
                    act.wait_ge(unit_done, 4 * m + s + 1)
                    act.activation(q2[:, 4 * (m - R_QKV) + s, :], acc[:, s, :], ACT.Copy, scale=1.0 / 8)\
                       .then_inc(taken[s], 1)
            m = R_QKV + 2
            for s in range(SLOTS):
                ahead(m, s)
                act.wait_ge(unit_done, 4 * m + s + 1)
                if s < 2:
                    act.activation(k2[:, s, :], acc[:, s, :], ACT.Copy).then_inc(taken[s], 1)
                else:
                    act.activation(v2[:, :, (s - 2) * P:(s - 1) * P],
                                   acc[:, s, :].rearrange("p (a c) -> p a c", a=4), ACT.Copy).then_inc(taken[s], 1)

            def window(step, stage):
                g, n = 2 * (step // 8) + step % 2, step % 8 // 2
                lo = 0 if n else P
                if stage == 0:
                    act.wait_ge(sw_step, 6 * step + 4)
                    for r in range(4):
                        act.activation(probs[:, r, lo:], probs[:, r, lo:], ACT.Exp, bias=small[:, 0, r:r + 1],
                                       accum_out=small[:, 1, r:r + 1]).then_inc(sw_exp, 1)
                    act.activation(small[:, 2, :], small[:, 2, :], ACT.Exp).then_inc(sw_exp, 1)
                if stage == 1:
                    act.wait_ge(sw_turned, step + 1)
                    at_least(act, sw_pv, step)
                    act.activation(probs_t[:, 1, :], side[:, 3, :], ACT.Copy).then_inc(sw_turned_act, 1)
                if stage == 2 and step % 2:
                    it = step // 2
                    p, n = it // 4, it % 4
                    act.wait_ge(sw_pv, step + 1)
                    act.activation(o2[:, 4 * p:4 * p + 4, n * P:(n + 1) * P],
                                   side[:, 2, :].rearrange("p (r c) -> p r c", r=4), ACT.Copy).then_inc(sw_out, 1)

            for it in range(KT):
                m, s = R_Z + it // 4, it % 4
                ahead(m, s)
                window(2 * it, 0)
                window(2 * it, 1)
                act.wait_ge(unit_done, 4 * m + s + 1)
                act.activation(z[:, it, :], acc[:, s, :], ACT.Copy).then_inc(taken[s], 1)
                window(2 * it + 1, 0)
                window(2 * it + 1, 1)
                window(2 * it + 1, 2)
            act.wait_ge(taken[3], uses(R_LAST))
            act.activation(z[:, 0, :], z[:, 0, :], ACT.Silu).then_inc(z_silu, 1)
            for k in range(KT):
                if k + 1 < KT:
                    act.activation(z[:, k + 1, :], z[:, k + 1, :], ACT.Silu).then_inc(z_silu, 1)
                act.wait_ge(gated, k + 1)
                act.activation(o2_high[:, k, :], part[:, k % 2, :], ACT.Copy).then_inc(gated_high, 1)
            for m in range(R_LAST, ROUNDS):
                residual_round(m, R_LAST, N_LAST, x3)
            root(N_LAST, SEQ)

        @block.tensor
        def _(pe):
            def product(m, s, moving, width=SEQ, blocks=range(KT), bank=None, first=True, last=True,
                        used=None, ready=None):
                bank = s if bank is None else bank
                pe.wait_ge(weight_low, 4 * m + (s + 1))
                if first:
                    at_least(pe, taken[bank], uses(m) if used is None else used)
                for b, k in enumerate(blocks):
                    if ready:
                        pe.wait_ge(ready[0], ready[1] + k + 1)
                    for w, v in ((w_high, 0), (w_high, 1), (w_low, 0)):
                        mm = pe.matmul(acc[:, bank, 0:width], w[s][:, b * P:(b + 1) * P], moving[v][:, k, :],
                                       start=first and b == 0 and w is w_high and v == 0,
                                       stop=last and b == len(blocks) - 1 and w is w_low)
                mm.then_inc(unit_done, 1)

            def rows(m, s, still, tiles, used=None):
                pe.wait_ge(weight_low, 4 * m + (s + 1))
                pe.wait_ge(taken[s], uses(m))
                for t in range(tiles):
                    for k in range(KT):
                        for v, w in ((0, w_high), (0, w_low), (1, w_high)):
                            mm = pe.matmul(acc[:, s, t * P:(t + 1) * P], still[v][:, k, t * P:(t + 1) * P],
                                           w[s][:, k * P:(k + 1) * P], start=k == 0 and v == 0 and w is w_high,
                                           stop=k == KT - 1 and v == 1)
                mm.then_inc(unit_done, 1)

            def total(norm, width):
                pe.wait_ge(square_added, KT * (norm + 1))
                pe.matmul(side[:, 3, 0:width], ones, sum_sq[:, 0:width], start=True, stop=True)\
                  .then_inc(stat_done, 1)

            h = (h_high, h_low)
            pe.wait_ge(par_landed, 48)
            total(N_X, SEQ)
            product(0, 0, h, ready=(act_low, 0))
            for s in range(1, SLOTS):
                product(0, s, h)
            total(N_MEM, MEM)
            with pe.Fori(1, R_KV) as m:
                for s in range(SLOTS):
                    product(m, s, h)
            pe.wait_ge(act_low, 2 * KT)
            with pe.Fori(R_KV, R_KV + 2) as m:
                for s in range(SLOTS):
                    product(m, s, (mem_high, mem_low), MEM)
            with pe.Fori(R_KV + 2, R_SHORT) as m:
                for s in range(SLOTS):
                    rows(m, s, (mem_high, mem_low), 2)

            def attend(head, stage):
                if stage == 0:
                    for s in range(SLOTS):
                        pe.wait_ge(taken[s], R_SHORT)
                    at_least(pe, o_low_done, 2 * head)
                    for t in range(4):
                        for d in range(2):
                            mm = pe.matmul(side[:, t // 2, MEM * (t % 2):MEM * (t % 2) + MEM],
                                           q[:, 2 * head + d, t * P:(t + 1) * P], k_mem[:, 2 * head + d, :],
                                           start=d == 0, stop=d == 1)
                    mm.then_inc(scores_done, 1)
                if stage == 2:
                    pe.wait_ge(probs_ready, 4 * head + 4)
                    at_least(pe, turned_act, head)
                    at_least(pe, turned_dve, head)
                    for t in range(4):
                        for b in range(2):
                            mm = pe.transpose(side[:, 2 + b, t * P:(t + 1) * P], probs[:, t, b * P:(b + 1) * P],
                                              ident)
                    mm.then_inc(probs_turned, 1)
                if stage == 4:
                    pe.wait_ge(turned_act, head + 1)
                    pe.wait_ge(turned_dve, head + 1)
                    for d in range(2):
                        for b in range(2):
                            mm = pe.matmul(side[:, d, :], v_mem[:, b, (2 * head + d) * P:(2 * head + d + 1) * P],
                                           probs_t[:, b, :], start=b == 0, stop=b == 1)
                    mm.then_inc(pv_done, 1)

            for i in range(2):
                for e in range(12):
                    m, s = 3 * i + R_SHORT + e // 4, e % 4
                    product(m, s, h)
                    attend(2 * i + e // 6, e % 6)

            pe.wait_ge(short_low, KT)

            def mix_round(m, moving):
                for s in range(SLOTS):
                    product(m, s, h if s % 2 == 0 else moving)

            with pe.Fori(R_MIX_A, R_MIX_C) as m:
                mix_round(m, (ya_high, ya_low))
            pe.wait_ge(o_low_done, KT)
            mix_round(R_MIX_C, (o_high, o_low))
            pe.wait_ge(conv_step, 32 * KT)
            pe.matmul(side[:, 2, :], ones, conv_sum[:, :], start=True, stop=True).then_inc(mean_done, 1)
            mix_round(R_MIX_C + 1, (o_high, o_low))
            total(N_LN, SEQ)
            with pe.Fori(R_MIX_C + 2, R_MIX_B) as m:
                mix_round(m, (o_high, o_low))
            pe.wait_ge(ln_low, KT)
            with pe.Fori(R_MIX_B, R_OUT) as m:
                mix_round(m, (yb_high, yb_low))
            product(R_OUT, 0, (m_high, m_low), ready=(merged_low, 0))
            for s in range(1, SLOTS):
                product(R_OUT, s, (m_high, m_low))
            for s in range(SLOTS):
                product(R_OUT + 1, s, (m_high, m_low))
            total(N_FFN, SEQ)
            product(R_UP, 0, h, ready=(act_low, 2 * KT))
            for s in range(1, SLOTS):
                product(R_UP, s, h)
            with pe.Fori(R_UP + 1, R_DOWN) as m:
                for s in range(SLOTS):
                    product(m, s, h)
            pe.wait_ge(ffn_low, F_TILES)

            def down_body(i):
                for e in range(12):
                    m, s = 3 * i + (R_DOWN + e // 4), e % 4
                    blocks = (range(0, 8), range(8, 15), range(15, 22))[e % 3]
                    product(m, s, (f_high, f_low), blocks=blocks, bank=e // 3, first=e % 3 == 0,
                            last=e % 3 == 2, used=i + R_DOWN)

            down_body(0)
            pe.wait_ge(tables_landed, 48)
            pe.matmul(side[0:HEADS_B, 2, 0:3 * P], table_sb[:, :], onehot_sb[:, :], start=True, stop=True)\
              .then_inc(strip_done, 1)
            down_body(1)
            total(N_FINAL, SEQ)
            total(N_SECOND, SEQ)
            xn = (xn_high, xn_low)
            product(R_QKV, 0, xn, ready=(act_low, 3 * KT))
            for s in range(1, SLOTS):
                product(R_QKV, s, xn)
            for s in range(SLOTS):
                product(R_QKV + 1, s, xn)
            for s in range(2):
                product(R_QKV + 2, s, xn)
            for s in range(2, 4):
                rows(R_QKV + 2, s, xn, 4)

            def window(step, stage):
                g, n = 2 * (step // 8) + step % 2, step % 8 // 2
                p, at = g // 2, 64 * (g % 2)
                blocks = (0, 1) if n else (1,)
                if stage == 0:
                    at_least(pe, sw_step, 6 * step - 5)
                    at_least(pe, sw_turned_dve, older(step))
                    for r in range(4):
                        mm = pe.matmul(side[:, r // 2, MEM * (r % 2) + P * blocks[0]:MEM * (r % 2) + MEM],
                                       q2[at:at + 64, 4 * p + r, n * P:(n + 1) * P],
                                       k2[at:at + 64, p, (n - 1 + blocks[0]) * P:(n + 1) * P], start=True, stop=True)
                    mm.then_inc(sw_scores, 1)
                if stage == 1:
                    pe.wait_ge(sw_step, 6 * step + 6)
                    at_least(pe, sw_turned_act, step)
                    for b in blocks:
                        for r in range(4):
                            mm = pe.transpose(turned(step, b)[:, r * P:(r + 1) * P], probs[:, r, b * P:(b + 1) * P], ident)
                    mm.then_inc(sw_turned, 1)
                if stage == 2:
                    pe.wait_ge(sw_turned_act, step + 1)
                    at_least(pe, sw_turned_dve, older(step + 1))
                    if step % 2 == 0:
                        at_least(pe, sw_out, step // 2)
                    for b in blocks:
                        mm = pe.matmul(side[at:at + 64, 2, :], v2[:, n - 1 + b, g * 64:(g + 1) * 64],
                                       probs_t[:, b, :], start=b == blocks[0], stop=b == 1)
                    mm.then_inc(sw_pv, 1)

            def turned(step, b):
                return side[:, 3, :] if b else side[:, 0, :]

            for s in range(SLOTS):
                pe.wait_ge(taken[s], uses(R_Z))
            for it in range(KT):
                window(2 * it, 0)
                if it:
                    window(2 * it - 1, 2)
                window(2 * it, 1)
                product(R_Z + it // 4, it % 4, xn)
                window(2 * it + 1, 0)
                window(2 * it, 2)
                window(2 * it + 1, 1)
            window(2 * KT - 1, 2)
            product(R_LAST, 0, (o2_high, o2_low), ready=(gated_low, 0))
            for s in range(1, SLOTS):
                product(R_LAST, s, (o2_high, o2_low))
            for s in range(SLOTS):
                product(R_LAST + 1, s, (o2_high, o2_low))
            total(N_LAST, SEQ)

        @block.vector
        def _(dve):
            def take_low(m, s):
                if isinstance(m, int) and m >= ROUNDS:
                    return
                dve.wait_ge(weight_high, 4 * m + (s + 1))
                dve.tensor_tensor(w_low[s][:, :], raw[s][:, :], w_high[s][:, :].bitcast(F32), ALU.subtract)\
                   .then_inc(weight_low, 1)

            def ahead(m, s):
                take_low(m + (s + 2) // 4, (s + 2) % 4)

            def clear_sum(n):
                dve.memset(sum_sq[:, :], 0.0).then_inc(sum_cleared, 1)

            def add_square(norm, k, slot, width=SEQ):
                n = k + KT * norm
                dve.wait_ge(squared, n + 1)
                at_least(dve, square_added, n)
                dve.wait_ge(sum_cleared, norm + 1)
                dve.tensor_tensor(sum_sq[:, 0:width], sum_sq[:, 0:width], square[:, slot, 0:width], ALU.add)\
                   .then_inc(square_added, 1)

            def mean_square(norm, width):
                dve.wait_ge(stat_done, norm + 1)
                dve.tensor_scalar(rstd[:, 0:width], side[:, 3, 0:width], 1.0 / D, EPS, ALU.mult, ALU.add)\
                   .then_inc(stat_read, 1)
                dve.wait_ge(stat_read, norm + 1)
                dve.reciprocal(rstd[:, 0:width], rstd[:, 0:width]).then_inc(recip_done, 1)
                clear_sum(norm + 1)

            def scale_tile(first, k, src, gain, width):
                dve.scalar_tensor_tensor(part[:, k % 2, 0:width], src, col(gain, k), rstd[:, 0:width],
                                         ALU.mult, ALU.mult).then_inc(scaled, 1)

            def low_tile(first, k, high, low, width):
                dve.wait_ge(act_high, first + k + 1)
                dve.tensor_tensor(low[:, k, :], part[:, k % 2, 0:width], high[:, k, :].bitcast(F32), ALU.subtract)\
                   .then_inc(act_low, 1)

            def scale_all(norm, first, src, gain, high, low, width):
                dve.wait_ge(rstd_ready, norm + 1)
                for k in range(KT):
                    at_least(dve, act_low, first + k - 1)
                    scale_tile(first, k, src[:, k, :], gain, width)
                    if k:
                        low_tile(first, k - 1, high, low, width)
                low_tile(first, KT - 1, high, low, width)

            taps = list(range(1, TAPS)) + [0]

            def conv(tile, ops):
                for n in ops:
                    if n == TAPS:
                        dve.wait_ge(conv_step, 32 * tile + n)
                        dve.tensor_tensor(conv_sum[:, :], conv_sum[:, :], long_u[:, tile, 1:SEQ + 1], ALU.add)\
                           .then_inc(conv_step, 1)
                        continue
                    shift = taps[n]
                    w = col("long_w", TAPS * tile + (TAPS - 1 - shift))
                    if n == 0:
                        at_least(dve, conv_step, 32 * tile)
                        dve.tensor_scalar(conv_acc[:, :], long_u[:, tile, 0:SEQ], w, col("long_b", tile),
                                          ALU.mult, ALU.add).then_inc(conv_step, 1)
                    elif shift:
                        dve.wait_ge(conv_step, 32 * tile + n)
                        dve.scalar_tensor_tensor(conv_acc[:, shift:SEQ], long_u[:, tile, 1:SEQ + 1 - shift], w,
                                                 conv_acc[:, shift:SEQ], ALU.mult, ALU.add).then_inc(conv_step, 1)
                    else:
                        dve.wait_ge(conv_step, 32 * tile + n)
                        dve.scalar_tensor_tensor(long_u[:, tile, 1:SEQ + 1], long_u[:, tile, 1:SEQ + 1], w,
                                                 conv_acc[:, :], ALU.mult, ALU.add).then_inc(conv_step, 1)

            dve.memset(sum_sq[:, :], 0.0).then_inc(sum_cleared, 1)
            for k in range(KT):
                add_square(N_X, k, k % 2)
            dve.wait_ge(par_landed, 48)
            mean_square(N_X, SEQ)
            take_low(0, 0)
            take_low(0, 1)
            for i in range(4):
                dve.wait_ge(x_landed[i], 16)
            scale_all(N_X, 0, x_in, "g_mix", h_high, h_low, SEQ)
            for k in range(KT):
                add_square(N_MEM, k, k % 2, MEM)

            def long_round(m):
                for s in range(SLOTS):
                    ahead(m, s)
                    if s % 2 == 1:
                        half = s // 2
                        dve.wait_ge(taken[s - 1], m + 1)
                        dve.wait_ge(unit_done, 4 * m + (s + 1))
                        dve.tensor_tensor(long_u[:, 2 * m + half, 1:SEQ + 1], acc[:, s, :], gate[:, half, :],
                                          ALU.mult).then_inc(taken[s], 1)

            long_round(0)
            mean_square(N_MEM, MEM)
            dve.wait_ge(mem_landed, 16)
            scale_all(N_MEM, KT, mem_in, "g_mem", mem_high, mem_low, MEM)
            with dve.Fori(1, R_Q) as m:
                long_round(m)
            dve.wait_ge(pads_set, 2)
            for s in (1, 3):
                dve.wait_ge(taken[s], R_Q)
            steps = TAPS + 1
            for m in range(R_Q, R_KV):
                for s in range(SLOTS):
                    ahead(m, s)
                    conv(m - R_Q, range(steps * s // 4, steps * (s + 1) // 4))
            with dve.Fori(R_KV, R_SHORT) as m:
                for s in range(SLOTS):
                    ahead(m, s)

            def attend(head, stage):
                if stage == 1:
                    dve.wait_ge(scores_done, head + 1)
                    dve.tensor_reduce(small[:, 0, :], side[:, 0:2, :].rearrange("p a (b c) -> p (a b) c", b=2),
                                      AX_X, ALU.max, negate=True).then_inc(row_max, 1)
                if stage == 2:
                    dve.wait_ge(exp_done, 4 * head + 4)
                    dve.reciprocal(small[:, 2, :], small[:, 1, :]).then_inc(recip_rows, 1)
                    dve.wait_ge(recip_rows, head + 1)
                    for t in range(4):
                        dve.tensor_scalar(probs[:, t, :], probs[:, t, :], small[:, 2, t:t + 1], None, ALU.mult)\
                           .then_inc(probs_ready, 1)
                if stage == 3:
                    dve.wait_ge(probs_turned, head + 1)
                    at_least(dve, pv_done, head)
                    dve.tensor_copy(probs_t[:, 1, :], side[:, 3, :]).then_inc(turned_dve, 1)
                if stage == 5:
                    dve.wait_ge(pv_done, head + 1)
                    for d in range(2):
                        dve.wait_ge(o_high_done, 2 * head + (d + 1))
                        dve.tensor_tensor(o_low[:, 2 * head + d, :], side[:, d, :],
                                          o_high[:, 2 * head + d, :].bitcast(F32), ALU.subtract)\
                           .then_inc(o_low_done, 1)

            def short_body(i):
                for e in range(12):
                    m, s, t, what = 3 * i + (R_SHORT + e // 4), e % 4, e // 3, e % 3
                    tile = 4 * i + t
                    ahead(m, s)
                    n = 4 * tile
                    if what == 1:
                        dve.wait_ge(taken[(s - 1) % 4], m + (1 if s else 0))
                        dve.wait_ge(unit_done, 4 * m + (s + 1))
                        at_least(dve, short_step, n)
                        dve.tensor_tensor(short_t, acc[:, s, :], short_c, ALU.mult).then_inc(short_step, 1)
                        dve.wait_ge(short_step, n + 1)
                        dve.tensor_scalar(short_y, short_t, col("short_w", 3 * tile + 2), None, ALU.mult)\
                           .then_inc(short_step, 1)
                        for shift in (1, 2):
                            dve.wait_ge(short_step, n + 1 + shift)
                            ins = dve.scalar_tensor_tensor(
                                square[:, 0, shift:SEQ], gate[:, 1, 0:SEQ - shift],
                                col("short_w", 3 * tile + (2 - shift)), square[:, 0, shift:SEQ], ALU.mult, ALU.add)
                            ins.then_inc(short_step if shift == 1 else taken[s], 1)
                    if what == 2:
                        dve.wait_ge(unit_done, 4 * m + (s + 1))
                        dve.wait_ge(taken[(s - 1) % 4], m + (1 if s else 0))
                        at_least(dve, short_low, tile - 1)
                        dve.tensor_tensor(part[:, t % 2, :], acc[:, s, :], short_y, ALU.mult).then_inc(short_step, 1)
                        dve.wait_ge(short_step, n + 4)
                        dve.memset(small[:, 5, 0:1], 0.0).then_inc(taken[s], 1)
                        dve.wait_ge(short_high, tile + 1)
                        dve.tensor_tensor(ya_low[:, tile, :], part[:, t % 2, :], ya_high[:, tile, :].bitcast(F32),
                                          ALU.subtract).then_inc(short_low, 1)
                    attend(2 * i + e // 6, e % 6)
                    conv(2 + 2 * i + e // 6, range(steps * (e % 6) // 6, steps * (e % 6 + 1) // 6))

            for i in range(2):
                short_body(i)

            def mix_round(m, first, kind, extra=None):
                for s in range(SLOTS):
                    ahead(m, s)
                    if s % 2 == 1:
                        half = s // 2
                        j = 2 * m + (half - 2 * first)
                        dve.wait_ge(taken[s - 1], m + 1)
                        dve.wait_ge(unit_done, 4 * m + (s + 1))
                        if kind == 0:
                            dve.tensor_tensor(merged[:, j, :], acc[:, s, :], gate[:, half, :], ALU.mult)\
                               .then_inc(taken[s], 1)
                        else:
                            dve.tensor_tensor(gate[:, half, :], acc[:, s, :], gate[:, half, :], ALU.mult)\
                               .then_inc(merge_part, 1)
                            dve.wait_ge(merge_part, j + (KT * (kind - 1) + 1))
                            dve.tensor_tensor(merged[:, j, :], merged[:, j, :], gate[:, half, :], ALU.add)\
                               .then_inc(merge_done, 1)
                            dve.wait_ge(merge_done, j + (KT * (kind - 1) + 1))
                            dve.memset(small[:, 5, 0:1], 0.0).then_inc(taken[s], 1)
                    if extra:
                        extra(m, s)

            for i in range(2):
                for half_round in range(2):
                    m = R_MIX_A + 2 * i + half_round

                    def conv_part(m, s):
                        n = 4 * half_round + s
                        conv(6 + i, range(steps * n // 8, steps * (n + 1) // 8))

                    mix_round(m, R_MIX_A, 0, conv_part)
            mix_round(R_MIX_C, R_MIX_C, 1)
            dve.wait_ge(mean_done, 1)
            dve.tensor_scalar(mean[:, :], side[:, 2, :], 1.0 / D, None, ALU.mult).then_inc(mean_read, 1)
            dve.wait_ge(mean_read, 1)

            def centre(m, s):
                for k in (2 * s, 2 * s + 1):
                    dve.tensor_tensor(long_u[:, k, 1:SEQ + 1], long_u[:, k, 1:SEQ + 1], mean[:, :], ALU.subtract)\
                       .then_inc(centred, 1)
                for k in (2 * s, 2 * s + 1):
                    add_square(N_LN, k, k % 2)

            mix_round(R_MIX_C + 1, R_MIX_C, 1, centre)
            mean_square(N_LN, SEQ)
            dve.wait_ge(rstd_ready, N_LN + 1)

            def ln_tile(m, s):
                k = 4 * m + (s - 4 * (R_MIX_C + 2))
                at_least(dve, ln_low, k - 1)
                dve.tensor_tensor(part[:, s % 2, :], long_u[:, k, 1:SEQ + 1], rstd[:, :], ALU.mult)\
                   .then_inc(ln_scaled, 1)
                dve.wait_ge(ln_high, k + 1)
                dve.tensor_tensor(yb_low[:, k, :], part[:, s % 2, :], yb_high[:, k, :].bitcast(F32), ALU.subtract)\
                   .then_inc(ln_low, 1)

            for m in range(R_MIX_C + 2, R_MIX_B):
                mix_round(m, R_MIX_C, 1, ln_tile)

            def merge_low(m, s):
                if s % 2 == 1:
                    j = 2 * m + (s // 2 - 2 * R_MIX_B)
                    dve.wait_ge(merged_high, j + 1)
                    dve.tensor_tensor(m_low[:, j, :], merged[:, j, :], m_high[:, j, :].bitcast(F32), ALU.subtract)\
                       .then_inc(merged_low, 1)

            with dve.Fori(R_MIX_B, R_OUT) as m:
                mix_round(m, R_MIX_B, 2, merge_low)
            dve.wait_ge(x_again, 16)

            def residual_round(m, first, norm, dst, src):
                for s in range(SLOTS):
                    ahead(m, s)
                    n = 4 * m + (s - 4 * first)
                    dve.wait_ge(unit_done, 4 * m + (s + 1))
                    dve.tensor_tensor(dst[:, n, :], acc[:, s, :], src[:, n, :], ALU.add).then_inc(taken[s], 1)
                    add_square(norm, n, s % 2)

            with dve.Fori(R_OUT, R_UP) as m:
                residual_round(m, R_OUT, N_FFN, x1, x1)
            mean_square(N_FFN, SEQ)
            scale_all(N_FFN, 2 * KT, x1, "g_ffn", h_high, h_low, SEQ)

            def up_round(m):
                for s in range(SLOTS):
                    ahead(m, s)
                    half = s // 2
                    j = 2 * m + (half - 2 * R_UP)
                    w = 3 * j + 3 * F_TILES * (s % 2)
                    dve.wait_ge(ffn_first, 4 * m + (s + 1 - 4 * R_UP))
                    y = ffn_y[s]
                    dve.scalar_tensor_tensor(y[:, 1:SEQ], acc[:, s, 0:SEQ - 1], col("ffn_w", w + 1), y[:, 1:SEQ],
                                             ALU.mult, ALU.add).then_inc(ffn_step, 1)
                    dve.wait_ge(ffn_step, 4 * m + (s + 1 - 4 * R_UP))
                    dve.scalar_tensor_tensor(y[:, 2:SEQ], acc[:, s, 0:SEQ - 2], col("ffn_w", w), y[:, 2:SEQ],
                                             ALU.mult, ALU.add).then_inc(taken[s], 1)
                    if s % 2 == 1:
                        dve.wait_ge(taken[s], m + 1)
                        dve.wait_ge(ffn_silu, j + 1)
                        at_least(dve, ffn_low, j - 1)
                        dve.tensor_tensor(part[:, half, :], ffn_y[s - 1], y, ALU.mult).then_inc(ffn_mul, 1)
                        dve.wait_ge(ffn_high, j + 1)
                        dve.tensor_tensor(f_low[:, j, :], part[:, half, :], f_high[:, j, :].bitcast(F32),
                                          ALU.subtract).then_inc(ffn_low, 1)

            up_round(R_UP)
            with dve.Fori(R_UP + 1, R_DOWN) as m:
                up_round(m)

            def down_body(i):
                for e in range(12):
                    m, s, n = 3 * i + (R_DOWN + e // 4), e % 4, 4 * i + e // 3
                    ahead(m, s)
                    if e % 3 == 2:
                        dve.wait_ge(unit_done, 4 * m + (s + 1))
                        dve.tensor_tensor(x2[:, n, :], acc[:, e // 3, :], x1[:, n, :], ALU.add)\
                           .then_inc(taken[e // 3], 1)
                        add_square(N_FINAL, n, e // 3 % 2)

            down_body(0)
            dve.wait_ge(strip_done, 1)
            dve.tensor_tensor(strip[:, :], side[0:HEADS_B, 2, 0:3 * P], neg_sb[:, :], ALU.add).then_inc(strip_ready, 1)
            down_body(1)
            mean_square(N_FINAL, SEQ)
            dve.wait_ge(rstd_ready, N_FINAL + 1)
            for k in range(KT):
                dve.scalar_tensor_tensor(y_res[:, k, :], x2[:, k, :], col("g_final", k), rstd[:, :],
                                         ALU.mult, ALU.mult).then_inc(y_ready, 1)
                if k:
                    add_square(N_SECOND, k - 1, (k - 1) % 2)
            add_square(N_SECOND, KT - 1, (KT - 1) % 2)
            dve.wait_ge(y_ready, KT)
            mean_square(N_SECOND, SEQ)
            scale_all(N_SECOND, 3 * KT, y_res, "g_second", xn_high, xn_low, SEQ)
            for m in range(R_QKV, R_Z):
                for s in range(SLOTS):
                    ahead(m, s)
            dve.wait_ge(bias_landed, 16)

            def window(step, stage):
                g, n = 2 * (step // 8) + step % 2, step % 8 // 2
                lo = 0 if n else P
                c = 6 * step
                if stage == 0:
                    dve.wait_ge(sw_scores, step + 1)
                    at_least(dve, sw_turned, step)
                    dve.tensor_tensor(probs[:, :, lo:], side[:, 0:2, :].rearrange("p a (b c) -> p (a b) c", b=2)[:, :, lo:],
                                      bias[:, 4 * g:4 * g + 4, lo:], ALU.add).then_inc(sw_step, 1)
                    dve.wait_ge(sw_step, c + 1)
                    dve.tensor_reduce(small[:, 3, :], probs[:, :, lo:], AX_X, ALU.max, negate=True).then_inc(sw_step, 1)
                    dve.wait_ge(sw_step, c + 2)
                    sink = par[:, PARAMS["sinks"] + 4 * g:PARAMS["sinks"] + 4 * g + 4]
                    dve.scalar_tensor_tensor(small[:, 0, :], sink, -1.0, small[:, 3, :], ALU.mult, ALU.min)\
                       .then_inc(sw_step, 1)
                    dve.wait_ge(sw_step, c + 3)
                    dve.tensor_tensor(small[:, 2, :], small[:, 0, :], sink, ALU.add).then_inc(sw_step, 1)
                if stage == 1:
                    dve.wait_ge(sw_exp, 5 * step + 5)
                    dve.tensor_tensor(small[:, 4, :], small[:, 1, :], small[:, 2, :], ALU.add).then_inc(sw_step, 1)
                    dve.wait_ge(sw_step, c + 5)
                    dve.reciprocal(small[:, 4, :], small[:, 4, :]).then_inc(sw_probs, 1)
                    dve.wait_ge(sw_probs, step + 1)
                    width = 2 * P - lo
                    dve.tensor_tensor(probs[:, :, lo:], probs[:, :, lo:],
                                      small[:, 4, :].unsqueeze(2).broadcast_to((P, 4, width)), ALU.mult)\
                       .then_inc(sw_step, 1)
                if stage == 2 and n:
                    dve.wait_ge(sw_turned, step + 1)
                    at_least(dve, sw_pv, step)
                    dve.tensor_copy(probs_t[:, 0, :], side[:, 0, :]).then_inc(sw_turned_dve, 1)

            for it in range(KT):
                m, s = R_Z + it // 4, it % 4
                window(2 * it, 0)
                ahead(m, s)
                window(2 * it, 1)
                window(2 * it, 2)
                window(2 * it + 1, 0)
                window(2 * it + 1, 1)
                window(2 * it + 1, 2)
            dve.wait_ge(sw_out, KT)
            for s in range(SLOTS):
                dve.wait_ge(taken[s], uses(R_LAST))

            def gated_low_of(k):
                dve.wait_ge(gated_high, k + 1)
                dve.tensor_tensor(o2_low[:, k, :], part[:, k % 2, :], o2_high[:, k, :].bitcast(F32), ALU.subtract)\
                   .then_inc(gated_low, 1)

            for k in range(KT):
                at_least(dve, gated_low, k - 1)
                dve.wait_ge(z_silu, k + 1)
                dve.tensor_tensor(part[:, k % 2, :], o2[:, k, :], z[:, k, :], ALU.mult).then_inc(gated, 1)
                if k:
                    gated_low_of(k - 1)
            gated_low_of(KT - 1)
            for m in range(R_LAST, ROUNDS):
                residual_round(m, R_LAST, N_LAST, x3, y_res)
            mean_square(N_LAST, SEQ)
            dve.wait_ge(rstd_ready, N_LAST + 1)
            for k in range(KT):
                dve.scalar_tensor_tensor(result[:, k, :], x3[:, k, :], col("g_last", k), rstd[:, :],
                                         ALU.mult, ALU.mult).then_inc(result_ready, 1)


def distance_columns():
    import numpy as np
    exact, buckets, far = 16, 32, 128
    picks = np.zeros((48, 3 * P), np.float32)
    for i in range(3 * P):
        dist = 2 * P - 1 - i
        if 0 <= dist < WINDOW:
            large = exact + int(np.float32(np.log(max(dist, 1) / exact)) / np.log(far / exact) * (buckets - exact)) \
                if dist >= exact else 0
            picks[dist if dist < exact else min(large, buckets - 1), i] = 1.0
        else:
            picks[32:, i] = NEG
    return picks


def kernel(**inputs):
    import numpy as np
    import concourse.bacc as bacc
    from concourse.bass_utils import run_bass_kernel_spmd as run

    a = {k: np.asarray(v) for k, v in inputs.items()}

    def units(w):
        n = w.shape[1] // P
        return w.reshape(KT, P, n, P).transpose(2, 1, 0, 3).reshape(n, P, UNIT)

    def pairs(u, v):
        return np.stack([u, v], 1).reshape(-1, P, UNIT)

    w_in = units(a["w_in"][0])
    gb, gc, v, u, ug, wq = (w_in[8 * i:8 * i + 8] for i in range(6))
    g0, g1, g2 = (w_in[48 + 8 * i:56 + 8 * i] for i in range(3))
    w_up = units(a["w_up"][0])
    down = a["w_down"][0].reshape(F_TILES, P, KT, P).transpose(2, 1, 0, 3)
    down_units = np.zeros((KT, 3, P, KT, P), np.float32)
    for i, (lo, hi) in enumerate(((0, 8), (8, 15), (15, 22))):
        down_units[:, i, :, :hi - lo, :] = down[:, :, lo:hi, :]

    order = np.array([(4 * (2 * p + e) + r) * 64 + c for p in range(2) for r in range(4) for e in range(2)
                      for c in range(64)])
    w2 = a["a_w_in_2"][0]
    qkv = np.concatenate([w2[:, 0:D][:, order], w2[:, D:D + 512]], 1)
    w_z = w2[:, D + 512:][:, order]
    w_last = a["a_w_out_2"][0][order, :]
    weights = np.concatenate([
        pairs(ug, u), wq, units(a["w_kv"][0]),
        np.stack([gc, v, gb], 1).reshape(-1, P, UNIT),
        pairs(g0, units(a["w_a_out"][0])), pairs(g2, units(a["w_att_out"][0])), pairs(g1, units(a["w_b_out"][0])),
        units(a["w_o"][0]), pairs(w_up[:F_TILES], w_up[F_TILES:]), down_units.reshape(-1, P, UNIT),
        units(qkv), units(w_z), units(w_last),
    ])

    def channels(t):
        return np.ascontiguousarray(t.reshape(-1, KT, P).transpose(2, 1, 0))

    def cols(t):
        t = np.atleast_2d(t)
        return t.reshape(t.shape[0], -1, P).transpose(2, 1, 0).reshape(P, -1)

    params = np.concatenate([
        cols(a["norm_mix_g"][0]), cols(a["norm_mem_g"][0]), cols(a["conv_b_w"][0]), cols(a["conv_b_bias"][0]),
        cols(a["ln_b_g"][0]), cols(a["ln_b_b"][0]), cols(a["b_gate"][0]), cols(a["conv_a_w"][0]),
        cols(a["norm_ffn_g"][0]), cols(a["conv_ffn_w"][0]), cols(a["norm_final_g"]), cols(a["norm_g_2"][0]),
        cols(a["final_g_2"]), np.broadcast_to(a["a_sinks_2"][0], (P, HEADS_B)),
    ], 1)
    arrays = {
        "weights": np.ascontiguousarray(weights),
        "x": channels(a["x"][0]),
        "mem": channels(a["mem"][0]),
        "params": np.ascontiguousarray(params),
        "consts": np.concatenate([np.ones((P, P), np.float32), np.eye(P, dtype=np.float32)], 1),
        "table": np.ascontiguousarray(a["t5_table_2"]),
        "onehot": distance_columns(),
    }
    nc = bacc.Bacc("TRN2", target_bir_lowering=False, num_devices=1)
    args = [nc.dram_tensor(n, v.shape, mybir.dt.from_np(v.dtype), kind="ExternalInput").ap()
            for n, v in arrays.items()]
    out = nc.dram_tensor("out", (P, KT, SEQ), F32, kind="ExternalOutput").ap()
    build(nc, *args, out)
    r = run(nc, [arrays], core_ids=[0])
    got = r.results[0]["out"]
    return np.ascontiguousarray(got.transpose(2, 1, 0)).reshape(1, SEQ, D)
```

```python
from contextlib import ExitStack

import concourse.bass as bass
from concourse import mybir

F32 = mybir.dt.float32
F32R = mybir.dt.float32r
ALU = mybir.AluOpType
ACT = mybir.ActivationFunctionType
AX_X = mybir.AxisListType.X

P = 128
SEQ = 512
D = 1024
KT = D // P
MEM = 256
TAPS = 31
F_TILES = 22
HEADS_A, HEADS_B, KV_B = 4, 16, 4
WINDOW = 128
EPS = 1e-6
NEG = -1e30
UNIT = KT * P
SLOTS = 4

R_KV = 0
R_LONG = 4
R_Q = 8
R_SHORT = 10
R_MIX_A = 16
R_MIX_C = 20
R_MIX_B = 24
R_OUT = 28
R_UP = 30
R_DOWN = 41
R_QKV = 47
R_Z = 50
R_LAST = 52
ROUNDS = 54
DOWN_SKIPS = 4

CONV_Q = 6
CONV_SHORT = 108
CONV_A = 5
CONV_ENDS = 3
LN_MEAN = 4
LN_CENTRE = {5: (0, 1), 6: (2, 3), 7: (4, 5), 8: (6, 7)}
LN_TOTAL = 9
LN_ROOT = 10
LN_TILES = {11: (0, 1), 12: (2, 3), 13: (4, 5), 14: (6, 7)}

PARAMS = {}
_at = 0
for _name, _n in (("g_mix", KT), ("g_mem", KT), ("long_w", KT * TAPS), ("long_b", KT), ("ln_g", KT), ("ln_b", KT),
                  ("gate_b", 3 * KT), ("short_w", 3 * KT), ("g_ffn", KT), ("ffn_w", 3 * 2 * F_TILES),
                  ("g_final", KT), ("g_second", KT), ("g_last", KT), ("sinks", HEADS_B)):
    PARAMS[_name] = _at
    _at += _n
N_PARAMS = _at

N_MEM, N_X, N_LN, N_FFN, N_FINAL, N_LAST = range(6)


def build(nc, weights, x, mem, params, consts, table, onehot, out):
    with ExitStack() as ctx:
        base = 16512
        top = [0]

        def sb(name, shape, dt, kb=None):
            n = 4
            for v in shape[1:]:
                n *= v
            if kb is None:
                at = TEMPS + top[0]
                top[0] += (n + 31) // 32 * 32
            else:
                at = int(kb * 1024)
            return nc.alloc_sbuf_tensor_at(name, shape, dt, offset=base + at)

        TEMPS = 185 * 1024

        def sem(name):
            return ctx.enter_context(nc.semaphore(name))

        raw = [sb(f"w_raw{s}", [P, UNIT], F32, 4 * s) for s in range(SLOTS)]
        w_high = sb("w_high", [P, SLOTS, UNIT], F32R, 16)
        w_low = sb("w_low", [P, SLOTS, UNIT], F32R, 32)
        h_high = sb("h_high", [P, KT, SEQ], F32R, 48)
        h_low = sb("h_low", [P, KT, SEQ], F32R, 64)
        long_u = sb("long_u", [P, KT, SEQ + 1], F32, 80)
        x_in = sb("x_in", [P, KT, SEQ], F32, 97)
        q = sb("q", [P, KT, SEQ], F32, 97)
        o_high = sb("o_high", [P, KT, SEQ], F32R, 97)
        mem_high = sb("mem_high", [P, KT, MEM], F32R, 113)
        mem_low = sb("mem_low", [P, KT, MEM], F32R, 121)
        o_low = sb("o_low", [P, KT, SEQ], F32R, 113)
        ya_high = sb("ya_high", [P, KT, SEQ], F32R, 129)
        ya_low = sb("ya_low", [P, KT, SEQ], F32R, 145)
        yb_high = sb("yb_high", [P, KT, SEQ], F32R, 129)
        yb_low = sb("yb_low", [P, KT, SEQ], F32R, 145)
        mem_in = sb("mem_in", [P, KT, MEM], F32, 161)
        k_mem = sb("k_mem", [P, KT, MEM], F32, 161)
        v_mem = sb("v_mem", [P, 2, D], F32, 169)
        merged = sb("merged", [P, KT, SEQ], F32, 161)
        m_high = sb("m_high", [P, KT, SEQ], F32R, 97)
        m_low = sb("m_low", [P, KT, SEQ], F32R, 113)
        x1 = sb("x1", [P, KT, SEQ], F32, 80)
        f_high = sb("f_high", [P, F_TILES, SEQ], F32R, 97)
        f_low = sb("f_low", [P, F_TILES, SEQ], F32R, 141)
        x2 = sb("x2", [P, KT, SEQ], F32, 48)
        bias = sb("bias", [P, HEADS_B, 2 * P], F32, 64)
        y_res = sb("y_res", [P, KT, SEQ], F32, 80)
        xn_high = sb("xn_high", [P, KT, SEQ], F32R, 97)
        xn_low = sb("xn_low", [P, KT, SEQ], F32R, 113)
        q2 = sb("q2", [P, KT, SEQ], F32, 129)
        k2 = sb("k2", [P, 2, SEQ], F32, 145)
        v2 = sb("v2", [P, 4, 2 * P], F32, 149)
        z = sb("z", [P, KT, SEQ], F32, 153)
        o2 = sb("o2", [P, KT, SEQ], F32, 48)
        o2_high = sb("o2_high", [P, KT, SEQ], F32R, 97)
        o2_low = sb("o2_low", [P, KT, SEQ], F32R, 113)
        x3 = sb("x3", [P, KT, SEQ], F32, 129)
        result = sb("result", [P, KT, SEQ], F32, 153)
        probs = sb("probs", [P, 4, 2 * P], F32, 177)
        probs_t = sb("probs_t", [P, 2, SEQ], F32, 181)
        sw_probs = [probs, sb("sw_probs1", [P, 4, 2 * P], F32, 169)]
        sw_probs_t = [probs_t, sb("sw_probs_t1", [P, 2, SEQ], F32, 173)]

        par = sb("par", [P, N_PARAMS], F32)
        ones_sb = sb("ones_sb", [P, P], F32)
        ident_sb = sb("ident_sb", [P, P], F32, 96.25)
        gate = sb("gate", [P, 2, SEQ], F32)
        conv_acc = sb("conv_acc", [P, SEQ], F32)
        conv_sum = sb("conv_sum", [P, SEQ], F32)
        part = sb("part", [P, 2, SEQ], F32)
        square = sb("square", [P, 2, SEQ], F32)
        sum_sq = sb("sum_sq", [P, SEQ], F32)
        rstd = sb("rstd", [P, SEQ], F32)
        small = sb("small", [P, 6, 4], F32)
        sw_small = [small, sb("sw_small1", [P, 6, 4], F32)]
        gain2 = sb("gain2", [P, KT], F32)
        assert TEMPS + top[0] + base <= 229344, TEMPS + top[0] + base - 229344
        short_c = gate[:, 0, :]
        short_t = gate[:, 1, :]
        short_y = square[:, 0, :]
        mean = conv_sum
        sum_gained = conv_sum
        rstd2 = conv_acc
        ffn_y = [gate[:, 0, :], gate[:, 1, :], conv_acc[:, :], conv_sum[:, :]]
        strip = sb("strip", [HEADS_B, 3 * P], F32, 64)
        table_sb = sb("table_sb", [32, HEADS_B], F32, 66)
        onehot_sb = sb("onehot_sb", [32, 3 * P], F32, 68)
        neg_sb = sb("neg_sb", [HEADS_B, 3 * P], F32, 70)
        ones, ident = ones_sb[:, :], ident_sb[:, :]

        def col(name, j):
            return par[:, bass.ds(j + PARAMS[name], 1)]

        acc = ctx.enter_context(nc.psum_tensor("acc", [P, SLOTS, SEQ], F32))
        side = ctx.enter_context(nc.psum_tensor("side", [P, 4, SEQ], F32))
        strip_dram = nc.dram_tensor("strip_dram", [HEADS_B, 3 * P], F32, kind="Internal")

        rows_dram = nc.dram_tensor("rows_dram", [P, HEADS_B * 3 * P], F32, kind="Internal")

        landed = [sem(f"weights_landed{s}") for s in range(SLOTS)]
        weight_high = sem("weight_high")
        weight_low = sem("weight_low")
        unit_done = sem("unit_done")
        taken = [sem(f"result_taken{s}") for s in range(SLOTS)]
        x_landed = [sem(f"x_landed{i}") for i in range(2)]
        x_again = sem("x_again")
        mem_landed = [sem(f"mem_landed{i}") for i in range(2)]
        par_landed = sem("par_landed")
        pads_set = sem("pads_set")
        squared = sem("squared")
        square_added = sem("square_added")
        sum_cleared = sem("sum_cleared")
        stat_done = sem("stat_done")
        stat_read = sem("stat_read")
        recip_done = sem("recip_done")
        rstd_ready = sem("rstd_ready")
        scaled = sem("scaled")
        act_high = sem("act_high")
        act_low = sem("act_low")
        conv_step = sem("conv_step")
        short_step = sem("short_step")
        short_high = sem("short_high")
        short_low = sem("short_low")
        merge_part = sem("merge_part")
        merge_done = sem("merge_done")
        merged_high = sem("merged_high")
        merged_low = sem("merged_low")
        mean_done = sem("mean_done")
        mean_read = sem("mean_read")
        centred = sem("centred")
        ln_scaled = sem("ln_scaled")
        ln_silu = sem("ln_silu")
        ln_high = sem("ln_high")
        ln_low = sem("ln_low")
        scores_done = sem("scores_done")
        row_max = sem("row_max")
        exp_done = sem("exp_done")
        recip_rows = sem("recip_rows")
        probs_ready = sem("probs_ready")
        probs_turned = sem("probs_turned")
        turned_act = sem("turned_act")
        turned_dve = sem("turned_dve")
        pv_done = sem("pv_done")
        o_high_done = sem("o_high_done")
        o_low_done = sem("o_low_done")
        ffn_first = sem("ffn_first")
        ffn_step = sem("ffn_step")
        ffn_silu = sem("ffn_silu")
        ffn_mul = sem("ffn_mul")
        ffn_high = sem("ffn_high")
        ffn_low = sem("ffn_low")
        tables_landed = sem("tables_landed")
        strip_done = sem("strip_done")
        strip_ready = sem("strip_ready")
        strip_stored = sem("strip_stored")
        bias_landed = sem("bias_landed")
        gain2_done = sem("gain2_done")
        gained_cleared = sem("gained_cleared")
        gained_squared = sem("gained_squared")
        gained_added = sem("gained_added")
        gained_stat = sem("gained_stat")
        second_step = sem("second_step")
        rstd2_ready = sem("rstd2_ready")
        y_ready = sem("y_ready")
        sw_scores = sem("sw_scores")
        sw_step = sem("sw_step")
        sw_minus = sem("sw_minus")
        sw_sum = sem("sw_sum")
        sw_recip = sem("sw_recip")
        sw_exp = sem("sw_exp")
        sw_ready = sem("sw_ready")
        sw_turned = sem("sw_turned")
        sw_turned_act = sem("sw_turned_act")
        sw_turned_dve = sem("sw_turned_dve")
        sw_pv = sem("sw_pv")
        sw_out = sem("sw_out")
        gated = sem("gated")
        gated_high = sem("gated_high")
        gated_low = sem("gated_low")
        result_ready = sem("result_ready")
        stored = sem("stored")

        def uses(m):
            return m - DOWN_SKIPS if isinstance(m, int) and m >= R_QKV else m

        def at_least(eng, s, n):
            if not isinstance(n, int) or n > 0:
                eng.wait_ge(s, n)

        def older(step):
            return sum(1 for t in range(step) if t % 8 >= 2)

        GATE_EARLY = {10: 0, 11: 1, 12: 2, 13: 3}

        def take_window(act, it):
            p, n = it // 4, it % 4
            act.wait_ge(sw_pv, 2 * it + 2)
            act.activation(o2[:, 4 * p:4 * p + 4, n * P:(n + 1) * P],
                           acc[:, 2 + it % 2, :].rearrange("p (r c) -> p r c", r=4), ACT.Copy).then_inc(sw_out, 1)

        block = ctx.enter_context(nc.Block())

        @block.sync
        def _(sp):
            for i in range(2):
                sp.dma_start(mem_in[:, 4 * i:4 * i + 4, :], mem[:, 4 * i:4 * i + 4, :]).then_inc(mem_landed[i], 16)
            for s in range(SLOTS):
                sp.dma_start(raw[s][:, :], weights[s]).then_inc(landed[s], 16)
            for i in range(2):
                sp.dma_start(x_in[:, 4 * i:4 * i + 4, :], x[:, 4 * i:4 * i + 4, :]).then_inc(x_landed[i], 16)
            with sp.Fori(1, ROUNDS) as m:
                for s in range(SLOTS):
                    sp.wait_ge(weight_low, 4 * m + (s - 3))
                    sp.dma_start(raw[s][:, :], weights[4 * m + s]).then_inc(landed[s], 16)
            for j in range(KT):
                sp.wait_ge(result_ready, j + 1)
                sp.dma_start(out[:, j, :], result[:, j, :]).then_inc(stored, 16)
            sp.wait_ge(stored, 16 * KT)

        @block.gpsimd
        def _(pool):
            pool.dma_start(par[:, :], params).then_inc(par_landed, 16)
            pool.dma_start(ones, consts[:, 0:P]).then_inc(par_landed, 16)
            pool.dma_start(ident, consts[:, P:2 * P]).then_inc(par_landed, 16)
            pool.memset(long_u[:, :, 0:1], 0.0).then_inc(pads_set, 1)
            pool.memset(conv_sum[:, :], 0.0).then_inc(pads_set, 1)
            pool.wait_ge(ln_low, KT)
            pool.dma_start(x1[:, :, :], x).then_inc(x_again, 16)
            pool.wait_ge(unit_done, 4 * R_DOWN)
            pool.dma_start(table_sb[:, :], table).then_inc(tables_landed, 16)
            pool.dma_start(onehot_sb[:, :], onehot[0:32, :]).then_inc(tables_landed, 16)
            pool.dma_start(neg_sb[:, :], onehot[32:48, :]).then_inc(tables_landed, 16)
            pool.wait_ge(strip_ready, 1)
            pool.dma_start(strip_dram[:, :], strip[:, :]).then_inc(strip_stored, 16)
            pool.wait_ge(strip_stored, 16)
            row = HEADS_B * 3 * P
            pool.dma_start(rows_dram[:, :], bass.AP(strip_dram, 0, [[0, P], [1, row]])).then_inc(strip_stored, 16)
            pool.wait_ge(strip_stored, 32)
            toeplitz = bass.AP(rows_dram, P - 1, [[row - 1, P], [3 * P, HEADS_B], [1, 2 * P]])
            pool.dma_start(bias[:, :, :], toeplitz).then_inc(bias_landed, 16)
            pool.wait_ge(bias_landed, 16)

        @block.scalar
        def _(act):
            def round_high(m, s):
                if isinstance(m, int) and m >= ROUNDS:
                    return
                act.wait_ge(landed[s], 16 * m + 16)
                at_least(act, unit_done, 4 * m + (s - 3))
                act.activation(w_high[:, s, :], raw[s][:, :], ACT.Copy).then_inc(weight_high, 1)

            def ahead(m, s):
                round_high(m + (s + 2) // 4, (s + 2) % 4)

            def squares(norm, k, src, width, *waits):
                n = KT * norm + k
                for w in waits:
                    act.wait_ge(*w)
                at_least(act, square_added, n - 1)
                act.activation(square[:, k % 2, 0:width], src, ACT.Square).then_inc(squared, 1)

            def root(norm, width):
                act.wait_ge(recip_done, norm + 1)
                act.activation(rstd[:, 0:width], rstd[:, 0:width], ACT.Sqrt).then_inc(rstd_ready, 1)

            def high_tiles(first, high, width):
                for k in range(KT):
                    act.wait_ge(scaled, first + k + 1)
                    act.activation(high[:, k, :], part[:, k % 2, 0:width], ACT.Copy).then_inc(act_high, 1)

            def gate_of(m, half, bias_col=None):
                act.wait_ge(unit_done, 4 * m + (2 * half + 1))
                at_least(act, taken[2 * half + 1], m)
                act.activation(gate[:, half, :], acc[:, 2 * half, :], ACT.Sigmoid,
                               bias=0.0 if bias_col is None else bias_col).then_inc(taken[2 * half], 1)

            def x_high(k):
                act.wait_ge(scaled, KT + k + 1)
                act.activation(h_high[:, k, :], part[:, k % 2, :], ACT.Copy).then_inc(act_high, 1)

            for k in range(KT):
                squares(N_MEM, k, mem_in[:, k, :], MEM, (mem_landed[k // 4], 16))
            round_high(0, 0)
            round_high(0, 1)
            root(N_MEM, MEM)
            high_tiles(0, mem_high, MEM)

            for m in range(R_KV, R_LONG):
                for s in range(SLOTS):
                    ahead(m, s)
                    if m == 0:
                        for k in (2 * s, 2 * s + 1):
                            squares(N_X, k, x_in[:, k, :], SEQ, (x_landed[k // 4], 16))
                    if m < 2:
                        act.wait_ge(unit_done, 4 * m + s + 1)
                        act.activation(k_mem[:, 4 * m + s, :], acc[:, s, 0:MEM], ACT.Copy).then_inc(taken[s], 1)
                    elif s % 2 == 1:
                        act.wait_ge(unit_done, 4 * m + s + 1)
                        at = 4 * P * (m - 2) + 2 * P * (s // 2)
                        for t in range(2):
                            act.activation(v_mem[:, t, at:at + 2 * P], acc[:, s - 1 + t, 0:2 * P], ACT.Copy)\
                               .then_inc(taken[s - 1 + t], 1)
                    if m == 1 and s == 0:
                        root(N_X, SEQ)
                    if m in (1, 2):
                        x_high(4 * (m - 1) + s)

            with act.Fori(R_LONG, R_Q) as m:
                for s in range(SLOTS):
                    ahead(m, s)
                    if s % 2 == 1:
                        gate_of(m, s // 2)
            with act.Fori(R_Q, R_SHORT) as m:
                for s in range(SLOTS):
                    ahead(m, s)
                    act.wait_ge(unit_done, 4 * m + (s + 1))
                    act.activation(q[:, 4 * m + (s - 4 * R_Q), :], acc[:, s, :], ACT.Copy,
                                   scale=1.0 / 16).then_inc(taken[s], 1)

            def attend(head, stage):
                if stage == 1:
                    act.wait_ge(scores_done, head + 1)
                    act.wait_ge(row_max, head + 1)
                    for t in range(4):
                        act.activation(probs[:, t, :], side[:, t // 2, MEM * (t % 2):MEM * (t % 2) + MEM], ACT.Exp,
                                       bias=small[:, 0, t:t + 1], accum_out=small[:, 1, t:t + 1])\
                           .then_inc(exp_done, 1)
                if stage == 3:
                    act.wait_ge(probs_turned, head + 1)
                    at_least(act, pv_done, head)
                    act.activation(probs_t[:, 0, :], side[:, 2, :], ACT.Copy).then_inc(turned_act, 1)
                if stage == 5:
                    act.wait_ge(pv_done, head + 1)
                    for d in range(2):
                        act.activation(o_high[:, 2 * head + d, :], side[:, d, :], ACT.Copy)\
                           .then_inc(o_high_done, 1)

            def short_body(i):
                for e in range(12):
                    m, s, tile, what = 3 * i + (R_SHORT + e // 4), e % 4, 4 * i + e // 3, e % 3
                    ahead(m, s)
                    if what == 0:
                        act.wait_ge(unit_done, 4 * m + (s + 1))
                        at_least(act, short_step, 4 * tile - 3)
                        if tile == 0:
                            act.wait_ge(taken[1], R_SHORT)
                        act.activation(short_c, acc[:, s, :], ACT.Copy).then_inc(taken[s], 1)
                    if what == 2:
                        act.wait_ge(short_step, 4 * tile + 4)
                        act.activation(ya_high[:, tile, :], part[:, e // 3 % 2, :], ACT.Copy)\
                           .then_inc(short_high, 1)
                    attend(2 * i + e // 6, e % 6)

            for i in range(2):
                short_body(i)

            def mix_round(m, first, branch, extra=None):
                for s in range(SLOTS):
                    ahead(m, s)
                    if s % 2 == 1:
                        gate_of(m, s // 2, col("gate_b", 2 * m + (s // 2 - 2 * first + KT * branch)))
                    if extra:
                        extra(m, s)

            def merge_high(m, s):
                if s % 2 == 1:
                    j = 2 * m + (s // 2 - 2 * R_MIX_B)
                    act.wait_ge(merge_done, j + (KT + 1))
                    act.activation(m_high[:, j, :], merged[:, j, :], ACT.Copy).then_inc(merged_high, 1)

            with act.Fori(R_MIX_A, R_MIX_C) as m:
                mix_round(m, R_MIX_A, 0)

            def ln_work(m, s):
                i = 4 * (m - R_MIX_C) + s
                if i in LN_CENTRE:
                    for k in LN_CENTRE[i]:
                        squares(N_LN, k, long_u[:, k, 1:SEQ + 1], SEQ, (centred, k + 1))
                if i == LN_ROOT:
                    root(N_LN, SEQ)
                for k in LN_TILES.get(i, ()):
                    act.wait_ge(ln_scaled, k + 1)
                    act.activation(part[:, k % 2, :], part[:, k % 2, :], ACT.Silu, bias=col("ln_b", k),
                                   scale=col("ln_g", k)).then_inc(ln_silu, 1)
                    act.wait_ge(ln_silu, k + 1)
                    act.activation(yb_high[:, k, :], part[:, k % 2, :], ACT.Copy).then_inc(ln_high, 1)

            for m in range(R_MIX_C, R_MIX_B):
                mix_round(m, R_MIX_C, 2, ln_work)
            with act.Fori(R_MIX_B, R_OUT) as m:
                mix_round(m, R_MIX_B, 1, merge_high)

            def residual_round(m, first, norm, src):
                for s in range(SLOTS):
                    ahead(m, s)
                    n = 4 * m + (s - 4 * first)
                    act.wait_ge(taken[s], uses(first) + 1 + (m - first))
                    at_least(act, square_added, n + (KT * norm - 1))
                    act.activation(square[:, s % 2, :], src[:, n, :], ACT.Square).then_inc(squared, 1)

            with act.Fori(R_OUT, R_UP) as m:
                residual_round(m, R_OUT, N_FFN, x1)
            root(N_FFN, SEQ)
            high_tiles(2 * KT, h_high, SEQ)

            def up_round(m):
                for s in range(SLOTS):
                    ahead(m, s)
                    half = s // 2
                    j = 2 * m + (half - 2 * R_UP)
                    w = 3 * j + (3 * F_TILES * (s % 2) + 2)
                    act.wait_ge(unit_done, 4 * m + (s + 1))
                    at_least(act, ffn_mul, 2 * m + (half - 2 * R_UP - 1))
                    act.activation(ffn_y[s], acc[:, s, :], ACT.Copy, scale=col("ffn_w", w)).then_inc(ffn_first, 1)
                    if s % 2 == 1:
                        act.wait_ge(taken[s - 1], m + 1)
                        act.activation(ffn_y[s - 1], ffn_y[s - 1], ACT.Silu).then_inc(ffn_silu, 1)
                        act.wait_ge(ffn_mul, j + 1)
                        act.activation(f_high[:, j, :], part[:, half, :], ACT.Copy).then_inc(ffn_high, 1)

            up_round(R_UP)
            with act.Fori(R_UP + 1, R_DOWN) as m:
                up_round(m)

            def down_body(i):
                for e in range(12):
                    m, s, n = 3 * i + (R_DOWN + e // 4), e % 4, 4 * i + e // 3
                    ahead(m, s)
                    if e % 3 == 2:
                        act.wait_ge(taken[e // 3], i + (R_DOWN + 1))
                        at_least(act, square_added, n + (KT * N_FINAL - 1))
                        act.activation(square[:, e // 3 % 2, :], x2[:, n, :], ACT.Square).then_inc(squared, 1)
                        at_least(act, gained_added, n - 1)
                        act.activation(gate[:, e // 3 % 2, :], x2[:, n, :], ACT.Square, scale=col("g_final", n))\
                           .then_inc(gained_squared, 1)

            for i in range(2):
                down_body(i)
            act.wait_ge(second_step, 2)
            act.activation(rstd2[:, :], rstd2[:, :], ACT.Sqrt, scale=float(D)).then_inc(rstd2_ready, 1)
            root(N_FINAL, SEQ)
            high_tiles(3 * KT, xn_high, SEQ)

            for m in range(R_QKV, R_QKV + 2):
                for s in range(SLOTS):
                    ahead(m, s)
                    act.wait_ge(unit_done, 4 * m + s + 1)
                    act.activation(q2[:, 4 * (m - R_QKV) + s, :], acc[:, s, :], ACT.Copy, scale=1.0 / 8)\
                       .then_inc(taken[s], 1)
            m = R_QKV + 2
            for s in range(SLOTS):
                ahead(m, s)
                if s == 2:
                    continue
                act.wait_ge(unit_done, 4 * m + s + 1)
                if s < 2:
                    act.activation(k2[:, s, :], acc[:, s, :], ACT.Copy).then_inc(taken[s], 1)
                else:
                    for t in range(2):
                        act.activation(v2[:, 2 * t:2 * t + 2, :],
                                       acc[:, 2 + t, :].rearrange("p (a c) -> p a c", a=2), ACT.Copy)\
                           .then_inc(taken[2 + t], 1)
            for m in range(R_Z, R_LAST):
                for s in range(SLOTS):
                    ahead(m, s)
                    act.wait_ge(unit_done, 4 * m + s + 1)
                    act.activation(z[:, 4 * (m - R_Z) + s, :], acc[:, s, :], ACT.Silu).then_inc(taken[s], 1)

            def exps(step):
                lo = 0 if step % 8 >= 2 else P
                pr, sm = sw_probs[step % 2], sw_small[step % 2]
                act.wait_ge(sw_minus, step + 1)
                act.wait_ge(sw_step, 6 * step + 6)
                for r in range(4):
                    act.activation(pr[:, r, lo:], pr[:, r, lo:], ACT.Exp, bias=sm[:, 0, r:r + 1],
                                   accum_out=sm[:, 1, r:r + 1]).then_inc(sw_exp, 1)
                act.activation(sm[:, 2, :], sm[:, 2, :], ACT.Exp).then_inc(sw_exp, 1)

            exps(0)
            exps(1)
            for step in range(2 * KT):
                act.wait_ge(sw_turned, step + 1)
                at_least(act, sw_pv, step - 1)
                act.activation(sw_probs_t[step % 2][:, 1, :], acc[:, 1, :], ACT.Copy).then_inc(sw_turned_act, 1)
                if step % 2 == 1 and step > 1:
                    take_window(act, step // 2 - 1)
                if step + 2 < 2 * KT:
                    exps(step + 2)
                if step in GATE_EARLY:
                    k = GATE_EARLY[step]
                    act.wait_ge(gated, k + 1)
                    act.activation(o2_high[:, k, :], part[:, k % 2, :], ACT.Copy).then_inc(gated_high, 1)
            take_window(act, KT - 1)
            for k in range(4, KT):
                act.wait_ge(gated, k + 1)
                act.activation(o2_high[:, k, :], part[:, k % 2, :], ACT.Copy).then_inc(gated_high, 1)
            for m in range(R_LAST, ROUNDS):
                residual_round(m, R_LAST, N_LAST, x3)
            root(N_LAST, SEQ)

        @block.tensor
        def _(pe):
            def product(m, s, moving, width=SEQ, blocks=range(KT), bank=None, first=True, last=True,
                        used=None, ready=None):
                bank = s if bank is None else bank
                pe.wait_ge(weight_low, 4 * m + (s + 1))
                if first:
                    at_least(pe, taken[bank], uses(m) if used is None else used)
                for b, k in enumerate(blocks):
                    if ready:
                        pe.wait_ge(ready[0], ready[1] + k + 1)
                    for w, v in ((w_high, 0), (w_high, 1), (w_low, 0)):
                        mm = pe.matmul(acc[:, bank, 0:width], w[:, s, b * P:(b + 1) * P], moving[v][:, k, :],
                                       start=first and b == 0 and w is w_high and v == 0,
                                       stop=last and b == len(blocks) - 1 and w is w_low)
                mm.then_inc(unit_done, 1)

            def two(m, s, moving, ready, width=SEQ):
                for i in range(2):
                    pe.wait_ge(weight_low, 4 * m + (s + i + 1))
                    at_least(pe, taken[s + i], uses(m))
                for k in range(KT):
                    pe.wait_ge(ready[0], ready[1] + k + 1)
                    for i in range(2):
                        for w, v in ((w_high, 0), (w_high, 1), (w_low, 0)):
                            mm = pe.matmul(acc[:, s + i, 0:width], w[:, s + i, k * P:(k + 1) * P],
                                           moving[v][:, k, :], start=k == 0 and w is w_high and v == 0,
                                           stop=k == KT - 1 and w is w_low)
                        if k == KT - 1:
                            mm.then_inc(unit_done, 1)

            def rows(m, s, still, tiles):
                pe.wait_ge(weight_low, 4 * m + (s + 2))
                for i in range(2):
                    at_least(pe, taken[s + i], uses(m))
                half = tiles // 2
                for t in range(tiles):
                    at = 2 * P * (t % half)
                    for k in range(KT):
                        for v, w in ((0, w_high), (0, w_low), (1, w_high)):
                            mm = pe.matmul(acc[:, s + t // half, at:at + 2 * P], still[v][:, k, t * P:(t + 1) * P],
                                           w[:, s:s + 2, k * P:(k + 1) * P], start=k == 0 and v == 0 and w is w_high,
                                           stop=k == KT - 1 and v == 1)
                mm.then_inc(unit_done, 2)

            def total(norm, width):
                pe.wait_ge(square_added, KT * (norm + 1))
                pe.matmul(side[:, 3, 0:width], ones, sum_sq[:, 0:width], start=True, stop=True)\
                  .then_inc(stat_done, 1)

            h = (h_high, h_low)
            memory = (mem_high, mem_low)
            pe.wait_ge(par_landed, 48)
            total(N_MEM, MEM)
            two(0, 0, memory, (act_low, 0), MEM)
            for s in range(2, SLOTS):
                product(0, s, memory, MEM)
            total(N_X, SEQ)
            for s in range(SLOTS):
                product(1, s, memory, MEM)
            for m in range(R_KV + 2, R_LONG):
                for s in (0, 2):
                    rows(m, s, memory, 2)
            pe.wait_ge(act_low, 2 * KT)
            with pe.Fori(R_LONG, R_SHORT) as m:
                for s in range(SLOTS):
                    product(m, s, h)

            def attend(head, stage):
                if stage == 0:
                    for s in range(SLOTS):
                        pe.wait_ge(taken[s], R_SHORT)
                    at_least(pe, o_low_done, 2 * head)
                    for t in range(4):
                        for d in range(2):
                            mm = pe.matmul(side[:, t // 2, MEM * (t % 2):MEM * (t % 2) + MEM],
                                           q[:, 2 * head + d, t * P:(t + 1) * P], k_mem[:, 2 * head + d, :],
                                           start=d == 0, stop=d == 1)
                    mm.then_inc(scores_done, 1)
                if stage == 2:
                    pe.wait_ge(probs_ready, 4 * head + 4)
                    at_least(pe, turned_act, head)
                    at_least(pe, turned_dve, head)
                    for t in range(4):
                        for b in range(2):
                            mm = pe.transpose(side[:, 2 + b, t * P:(t + 1) * P], probs[:, t, b * P:(b + 1) * P],
                                              ident)
                    mm.then_inc(probs_turned, 1)
                if stage == 4:
                    pe.wait_ge(turned_act, head + 1)
                    pe.wait_ge(turned_dve, head + 1)
                    for d in range(2):
                        for b in range(2):
                            mm = pe.matmul(side[:, d, :], v_mem[:, b, (2 * head + d) * P:(2 * head + d + 1) * P],
                                           probs_t[:, b, :], start=b == 0, stop=b == 1)
                    mm.then_inc(pv_done, 1)

            for i in range(2):
                for e in range(12):
                    m, s = 3 * i + R_SHORT + e // 4, e % 4
                    product(m, s, h)
                    attend(2 * i + e // 6, e % 6)

            pe.wait_ge(short_low, KT)

            def mix_round(m, moving):
                for s in range(SLOTS):
                    product(m, s, h if s % 2 == 0 else moving)

            with pe.Fori(R_MIX_A, R_MIX_C) as m:
                mix_round(m, (ya_high, ya_low))
            pe.wait_ge(o_low_done, KT)
            for m in range(R_MIX_C, R_MIX_B):
                for s in range(SLOTS):
                    product(m, s, h if s % 2 == 0 else (o_high, o_low))
                    i = 4 * (m - R_MIX_C) + s
                    if i == LN_MEAN:
                        pe.wait_ge(conv_step, 32 * KT)
                        pe.matmul(side[:, 2, :], ones, conv_sum[:, :], start=True, stop=True).then_inc(mean_done, 1)
                    if i == LN_TOTAL:
                        total(N_LN, SEQ)
            product(R_MIX_B, 0, h)
            product(R_MIX_B, 1, (yb_high, yb_low), ready=(ln_low, 0))
            product(R_MIX_B, 2, h)
            product(R_MIX_B, 3, (yb_high, yb_low))
            with pe.Fori(R_MIX_B + 1, R_OUT) as m:
                mix_round(m, (yb_high, yb_low))
            two(R_OUT, 0, (m_high, m_low), (merged_low, 0))
            for s in range(2, SLOTS):
                product(R_OUT, s, (m_high, m_low))
            for s in range(SLOTS):
                product(R_OUT + 1, s, (m_high, m_low))
            total(N_FFN, SEQ)
            two(R_UP, 0, h, (act_low, 2 * KT))
            for s in range(2, SLOTS):
                product(R_UP, s, h)
            with pe.Fori(R_UP + 1, R_DOWN) as m:
                for s in range(SLOTS):
                    product(m, s, h)

            def down_body(i):
                for e in range(12):
                    m, s = 3 * i + (R_DOWN + e // 4), e % 4
                    blocks = (range(0, 8), range(8, 15), range(15, 22))[e % 3]
                    if e < 3:
                        pe.wait_ge(ffn_low, blocks[-1] + 1)
                    product(m, s, (f_high, f_low), blocks=blocks, bank=e // 3, first=e % 3 == 0,
                            last=e % 3 == 2, used=i + R_DOWN)

            down_body(0)
            pe.wait_ge(tables_landed, 48)
            pe.matmul(side[0:HEADS_B, 2, 0:3 * P], table_sb[:, :], onehot_sb[:, :], start=True, stop=True)\
              .then_inc(strip_done, 1)
            down_body(1)
            total(N_FINAL, SEQ)
            pe.wait_ge(gained_added, KT)
            pe.matmul(side[:, 2, :], ones, sum_gained[:, :], start=True, stop=True).then_inc(gained_stat, 1)
            xn = (xn_high, xn_low)
            two(R_QKV, 0, xn, (act_low, 3 * KT))
            for s in range(2, SLOTS):
                product(R_QKV, s, xn)
            for s in range(SLOTS):
                product(R_QKV + 1, s, xn)
            for s in range(2):
                product(R_QKV + 2, s, xn)
            rows(R_QKV + 2, 2, xn, 4)
            for m in range(R_Z, R_LAST):
                for s in range(SLOTS):
                    product(m, s, xn)

            def window_of(step):
                g, n = 2 * (step // 8) + step % 2, step % 8 // 2
                return g, g // 2, 64 * (g % 2), n, (0, 1) if n else (1,)

            def scores(step):
                g, p, at, n, blocks = window_of(step)
                at_least(pe, sw_step, 6 * (step - 2) + 4)
                for r in range(4):
                    mm = pe.matmul(side[:, 2 * (step % 2) + r // 2, MEM * (r % 2) + P * blocks[0]:MEM * (r % 2) + MEM],
                                   q2[at:at + 64, 4 * p + r, n * P:(n + 1) * P],
                                   k2[at:at + 64, p, (n - 1 + blocks[0]) * P:(n + 1) * P], start=True, stop=True)
                mm.then_inc(sw_scores, 1)

            def turn(step):
                blocks = window_of(step)[4]
                pe.wait_ge(sw_ready, step + 1)
                at_least(pe, sw_turned_act, step)
                at_least(pe, sw_turned_dve, older(step))
                for b in blocks:
                    for r in range(4):
                        mm = pe.transpose(acc[:, b, r * P:(r + 1) * P], sw_probs[step % 2][:, r, b * P:(b + 1) * P],
                                          ident)
                mm.then_inc(sw_turned, 1)

            def outputs(step):
                g, p, at, n, blocks = window_of(step)
                pe.wait_ge(sw_turned_act, step + 1)
                at_least(pe, sw_turned_dve, older(step + 1))
                at_least(pe, sw_out, step // 2 - 1)
                for b in blocks:
                    mm = pe.matmul(acc[at:at + 64, 2 + step // 2 % 2, :], v2[:, n - 1 + b, g * 64:(g + 1) * 64],
                                   sw_probs_t[step % 2][:, b, :], start=b == blocks[0], stop=b == 1)
                mm.then_inc(sw_pv, 1)

            for s in range(SLOTS):
                pe.wait_ge(taken[s], uses(R_Z))
            scores(0)
            scores(1)
            for s in range(SLOTS):
                pe.wait_ge(taken[s], uses(R_LAST))
            for step in range(2 * KT):
                turn(step)
                if step + 2 < 2 * KT:
                    scores(step + 2)
                outputs(step)
            pe.wait_ge(sw_out, KT)
            two(R_LAST, 0, (o2_high, o2_low), (gated_low, 0))
            for s in range(2, SLOTS):
                product(R_LAST, s, (o2_high, o2_low))
            for s in range(SLOTS):
                product(R_LAST + 1, s, (o2_high, o2_low))
            total(N_LAST, SEQ)

        @block.vector
        def _(dve):
            def take_low(m, s):
                if isinstance(m, int) and m >= ROUNDS:
                    return
                dve.wait_ge(weight_high, 4 * m + (s + 1))
                dve.tensor_tensor(w_low[:, s, :], raw[s][:, :], w_high[:, s, :].bitcast(F32), ALU.subtract)\
                   .then_inc(weight_low, 1)

            def ahead(m, s):
                take_low(m + (s + 2) // 4, (s + 2) % 4)

            def clear_sum(n):
                dve.memset(sum_sq[:, :], 0.0).then_inc(sum_cleared, 1)

            def add_square(norm, k, slot, width=SEQ):
                n = k + KT * norm
                dve.wait_ge(squared, n + 1)
                at_least(dve, square_added, n)
                dve.wait_ge(sum_cleared, norm + 1)
                dve.tensor_tensor(sum_sq[:, 0:width], sum_sq[:, 0:width], square[:, slot, 0:width], ALU.add)\
                   .then_inc(square_added, 1)

            def mean_square(norm, width):
                dve.wait_ge(stat_done, norm + 1)
                dve.tensor_scalar(rstd[:, 0:width], side[:, 3, 0:width], 1.0 / D, EPS, ALU.mult, ALU.add)\
                   .then_inc(stat_read, 1)
                dve.wait_ge(stat_read, norm + 1)
                dve.reciprocal(rstd[:, 0:width], rstd[:, 0:width]).then_inc(recip_done, 1)
                clear_sum(norm + 1)

            def scale_tile(first, k, src, gain, width):
                dve.scalar_tensor_tensor(part[:, k % 2, 0:width], src, col(gain, k), rstd[:, 0:width],
                                         ALU.mult, ALU.mult).then_inc(scaled, 1)

            def low_tile(first, k, high, low, width):
                dve.wait_ge(act_high, first + k + 1)
                dve.tensor_tensor(low[:, k, :], part[:, k % 2, 0:width], high[:, k, :].bitcast(F32), ALU.subtract)\
                   .then_inc(act_low, 1)

            def scale_all(norm, first, src, gain, high, low, width):
                dve.wait_ge(rstd_ready, norm + 1)
                for k in range(KT):
                    at_least(dve, act_low, first + k - 1)
                    scale_tile(first, k, src[:, k, :], gain, width)
                    if k:
                        low_tile(first, k - 1, high, low, width)
                low_tile(first, KT - 1, high, low, width)

            taps = list(range(1, TAPS)) + [0]

            def conv(tile, ops):
                for n in ops:
                    if n == TAPS:
                        dve.wait_ge(conv_step, 32 * tile + n)
                        dve.tensor_tensor(conv_sum[:, :], conv_sum[:, :], long_u[:, tile, 1:SEQ + 1], ALU.add)\
                           .then_inc(conv_step, 1)
                        continue
                    shift = taps[n]
                    w = col("long_w", TAPS * tile + (TAPS - 1 - shift))
                    if n == 0:
                        at_least(dve, conv_step, 32 * tile)
                        dve.tensor_scalar(conv_acc[:, :], long_u[:, tile, 0:SEQ], w, col("long_b", tile),
                                          ALU.mult, ALU.add).then_inc(conv_step, 1)
                    elif shift:
                        dve.wait_ge(conv_step, 32 * tile + n)
                        dve.scalar_tensor_tensor(conv_acc[:, shift:SEQ], long_u[:, tile, 1:SEQ + 1 - shift], w,
                                                 conv_acc[:, shift:SEQ], ALU.mult, ALU.add).then_inc(conv_step, 1)
                    else:
                        dve.wait_ge(conv_step, 32 * tile + n)
                        dve.scalar_tensor_tensor(long_u[:, tile, 1:SEQ + 1], long_u[:, tile, 1:SEQ + 1], w,
                                                 conv_acc[:, :], ALU.mult, ALU.add).then_inc(conv_step, 1)

            dve.memset(sum_sq[:, :], 0.0).then_inc(sum_cleared, 1)
            for k in range(KT):
                add_square(N_MEM, k, k % 2, MEM)
            dve.wait_ge(par_landed, 48)
            mean_square(N_MEM, MEM)
            take_low(0, 0)
            take_low(0, 1)
            scale_all(N_MEM, 0, mem_in, "g_mem", mem_high, mem_low, MEM)
            for m in range(R_KV, R_LONG):
                for s in range(SLOTS):
                    ahead(m, s)
                    if m == 0:
                        add_square(N_X, 2 * s, 0)
                        add_square(N_X, 2 * s + 1, 1)
                    if m == 1 and s == 0:
                        mean_square(N_X, SEQ)
                        dve.wait_ge(rstd_ready, N_X + 1)
                    if m in (1, 2):
                        scale_tile(KT, 4 * (m - 1) + s, x_in[:, 4 * (m - 1) + s, :], "g_mix", SEQ)
                        low_tile(KT, 4 * (m - 1) + s, h_high, h_low, SEQ)

            with dve.Fori(R_LONG, R_Q) as m:
                for s in range(SLOTS):
                    ahead(m, s)
                    if s % 2 == 1:
                        half = s // 2
                        dve.wait_ge(taken[s - 1], m + 1)
                        dve.wait_ge(unit_done, 4 * m + (s + 1))
                        dve.tensor_tensor(long_u[:, 2 * m + (half - 2 * R_LONG), 1:SEQ + 1], acc[:, s, :],
                                          gate[:, half, :], ALU.mult).then_inc(taken[s], 1)
            dve.wait_ge(pads_set, 2)
            for s in (1, 3):
                dve.wait_ge(taken[s], R_Q)
            steps = TAPS + 1

            def conv_by(n, at=[0]):
                while at[0] < n:
                    conv(at[0] // steps, [at[0] % steps])
                    at[0] += 1

            for m in range(R_Q, R_SHORT):
                for s in range(SLOTS):
                    ahead(m, s)
                    conv_by(CONV_Q * (4 * (m - R_Q) + s + 1))

            def attend(head, stage):
                if stage == 1:
                    dve.wait_ge(scores_done, head + 1)
                    dve.tensor_reduce(small[:, 0, :], side[:, 0:2, :].rearrange("p a (b c) -> p (a b) c", b=2),
                                      AX_X, ALU.max, negate=True).then_inc(row_max, 1)
                if stage == 2:
                    dve.wait_ge(exp_done, 4 * head + 4)
                    dve.reciprocal(small[:, 2, :], small[:, 1, :]).then_inc(recip_rows, 1)
                    dve.wait_ge(recip_rows, head + 1)
                    for t in range(4):
                        dve.tensor_scalar(probs[:, t, :], probs[:, t, :], small[:, 2, t:t + 1], None, ALU.mult)\
                           .then_inc(probs_ready, 1)
                if stage == 3:
                    dve.wait_ge(probs_turned, head + 1)
                    at_least(dve, pv_done, head)
                    dve.tensor_copy(probs_t[:, 1, :], side[:, 3, :]).then_inc(turned_dve, 1)
                if stage == 5:
                    dve.wait_ge(pv_done, head + 1)
                    for d in range(2):
                        dve.wait_ge(o_high_done, 2 * head + (d + 1))
                        dve.tensor_tensor(o_low[:, 2 * head + d, :], side[:, d, :],
                                          o_high[:, 2 * head + d, :].bitcast(F32), ALU.subtract)\
                           .then_inc(o_low_done, 1)

            def short_body(i):
                for e in range(12):
                    m, s, t, what = 3 * i + (R_SHORT + e // 4), e % 4, e // 3, e % 3
                    tile = 4 * i + t
                    ahead(m, s)
                    n = 4 * tile
                    if what == 1:
                        dve.wait_ge(taken[(s - 1) % 4], m + (1 if s else 0))
                        dve.wait_ge(unit_done, 4 * m + (s + 1))
                        at_least(dve, short_step, n)
                        dve.tensor_tensor(short_t, acc[:, s, :], short_c, ALU.mult).then_inc(short_step, 1)
                        dve.wait_ge(short_step, n + 1)
                        dve.tensor_scalar(short_y, short_t, col("short_w", 3 * tile + 2), None, ALU.mult)\
                           .then_inc(short_step, 1)
                        for shift in (1, 2):
                            dve.wait_ge(short_step, n + 1 + shift)
                            ins = dve.scalar_tensor_tensor(
                                square[:, 0, shift:SEQ], gate[:, 1, 0:SEQ - shift],
                                col("short_w", 3 * tile + (2 - shift)), square[:, 0, shift:SEQ], ALU.mult, ALU.add)
                            ins.then_inc(short_step if shift == 1 else taken[s], 1)
                    if what == 2:
                        dve.wait_ge(unit_done, 4 * m + (s + 1))
                        dve.wait_ge(taken[(s - 1) % 4], m + (1 if s else 0))
                        at_least(dve, short_low, tile - 1)
                        dve.tensor_tensor(part[:, t % 2, :], acc[:, s, :], short_y, ALU.mult).then_inc(short_step, 1)
                        dve.wait_ge(short_step, n + 4)
                        dve.memset(small[:, 5, 0:1], 0.0).then_inc(taken[s], 1)
                        dve.wait_ge(short_high, tile + 1)
                        dve.tensor_tensor(ya_low[:, tile, :], part[:, t % 2, :], ya_high[:, tile, :].bitcast(F32),
                                          ALU.subtract).then_inc(short_low, 1)
                    attend(2 * i + e // 6, e % 6)
                    conv_by(8 * CONV_Q + (12 * i + e + 1) * CONV_SHORT // 24)

            for i in range(2):
                short_body(i)

            def mix_round(m, first, kind, extra=None):
                for s in range(SLOTS):
                    ahead(m, s)
                    if s % 2 == 1:
                        half = s // 2
                        j = 2 * m + (half - 2 * first)
                        dve.wait_ge(taken[s - 1], m + 1)
                        dve.wait_ge(unit_done, 4 * m + (s + 1))
                        if kind == 0:
                            dve.tensor_tensor(merged[:, j, :], acc[:, s, :], gate[:, half, :], ALU.mult)\
                               .then_inc(taken[s], 1)
                        else:
                            dve.tensor_tensor(gate[:, half, :], acc[:, s, :], gate[:, half, :], ALU.mult)\
                               .then_inc(merge_part, 1)
                            dve.wait_ge(merge_part, j + (KT * (kind - 1) + 1))
                            dve.tensor_tensor(merged[:, j, :], merged[:, j, :], gate[:, half, :], ALU.add)\
                               .then_inc(merge_done, 1)
                            dve.wait_ge(merge_done, j + (KT * (kind - 1) + 1))
                            dve.memset(small[:, 5, 0:1], 0.0).then_inc(taken[s], 1)
                    if extra:
                        extra(m, s)

            def conv_part(m, s):
                conv_by(8 * CONV_Q + CONV_SHORT + CONV_A * (4 * (m - R_MIX_A) + s + 1))

            for m in range(R_MIX_A, R_MIX_C):
                mix_round(m, R_MIX_A, 0, conv_part)

            def ln_work(m, s):
                i = 4 * (m - R_MIX_C) + s
                if i <= CONV_ENDS:
                    rest = steps * KT - 8 * CONV_Q - CONV_SHORT - 16 * CONV_A
                    conv_by(steps * KT - rest * (CONV_ENDS - i) // (CONV_ENDS + 1))
                if i == LN_MEAN:
                    dve.wait_ge(mean_done, 1)
                    dve.tensor_scalar(mean[:, :], side[:, 2, :], 1.0 / D, None, ALU.mult).then_inc(mean_read, 1)
                    dve.wait_ge(mean_read, 1)
                if i in LN_CENTRE:
                    for k in LN_CENTRE[i]:
                        dve.tensor_tensor(long_u[:, k, 1:SEQ + 1], long_u[:, k, 1:SEQ + 1], mean[:, :],
                                          ALU.subtract).then_inc(centred, 1)
                    for k in LN_CENTRE[i]:
                        add_square(N_LN, k, k % 2)
                if i == LN_ROOT:
                    mean_square(N_LN, SEQ)
                    dve.wait_ge(rstd_ready, N_LN + 1)
                for k in LN_TILES.get(i, ()):
                    at_least(dve, ln_low, k - 1)
                    dve.tensor_tensor(part[:, k % 2, :], long_u[:, k, 1:SEQ + 1], rstd[:, :], ALU.mult)\
                       .then_inc(ln_scaled, 1)
                for k in LN_TILES.get(i, ()):
                    dve.wait_ge(ln_high, k + 1)
                    dve.tensor_tensor(yb_low[:, k, :], part[:, k % 2, :], yb_high[:, k, :].bitcast(F32),
                                      ALU.subtract).then_inc(ln_low, 1)

            for m in range(R_MIX_C, R_MIX_B):
                mix_round(m, R_MIX_C, 1, ln_work)

            def merge_low(m, s):
                if s % 2 == 1:
                    j = 2 * m + (s // 2 - 2 * R_MIX_B)
                    dve.wait_ge(merged_high, j + 1)
                    dve.tensor_tensor(m_low[:, j, :], merged[:, j, :], m_high[:, j, :].bitcast(F32), ALU.subtract)\
                       .then_inc(merged_low, 1)

            with dve.Fori(R_MIX_B, R_OUT) as m:
                mix_round(m, R_MIX_B, 2, merge_low)
            dve.wait_ge(x_again, 16)

            def residual_round(m, first, norm, dst, src):
                for s in range(SLOTS):
                    ahead(m, s)
                    n = 4 * m + (s - 4 * first)
                    dve.wait_ge(unit_done, 4 * m + (s + 1))
                    dve.tensor_tensor(dst[:, n, :], acc[:, s, :], src[:, n, :], ALU.add).then_inc(taken[s], 1)
                    add_square(norm, n, s % 2)

            with dve.Fori(R_OUT, R_UP) as m:
                residual_round(m, R_OUT, N_FFN, x1, x1)
            mean_square(N_FFN, SEQ)
            scale_all(N_FFN, 2 * KT, x1, "g_ffn", h_high, h_low, SEQ)

            def up_round(m):
                for s in range(SLOTS):
                    ahead(m, s)
                    half = s // 2
                    j = 2 * m + (half - 2 * R_UP)
                    w = 3 * j + 3 * F_TILES * (s % 2)
                    dve.wait_ge(ffn_first, 4 * m + (s + 1 - 4 * R_UP))
                    y = ffn_y[s]
                    dve.scalar_tensor_tensor(y[:, 1:SEQ], acc[:, s, 0:SEQ - 1], col("ffn_w", w + 1), y[:, 1:SEQ],
                                             ALU.mult, ALU.add).then_inc(ffn_step, 1)
                    dve.wait_ge(ffn_step, 4 * m + (s + 1 - 4 * R_UP))
                    dve.scalar_tensor_tensor(y[:, 2:SEQ], acc[:, s, 0:SEQ - 2], col("ffn_w", w), y[:, 2:SEQ],
                                             ALU.mult, ALU.add).then_inc(taken[s], 1)
                    if s % 2 == 1:
                        dve.wait_ge(taken[s], m + 1)
                        dve.wait_ge(ffn_silu, j + 1)
                        at_least(dve, ffn_low, j - 1)
                        dve.tensor_tensor(part[:, half, :], ffn_y[s - 1], y, ALU.mult).then_inc(ffn_mul, 1)
                        dve.wait_ge(ffn_high, j + 1)
                        dve.tensor_tensor(f_low[:, j, :], part[:, half, :], f_high[:, j, :].bitcast(F32),
                                          ALU.subtract).then_inc(ffn_low, 1)

            up_round(R_UP)
            with dve.Fori(R_UP + 1, R_DOWN) as m:
                up_round(m)

            def down_body(i):
                for e in range(12):
                    m, s, n = 3 * i + (R_DOWN + e // 4), e % 4, 4 * i + e // 3
                    ahead(m, s)
                    if e % 3 == 2:
                        dve.wait_ge(unit_done, 4 * m + (s + 1))
                        dve.tensor_tensor(x2[:, n, :], acc[:, e // 3, :], x1[:, n, :], ALU.add)\
                           .then_inc(taken[e // 3], 1)
                        add_square(N_FINAL, n, e // 3 % 2)
                        dve.wait_ge(gained_squared, n + 1)
                        at_least(dve, gained_added, n)
                        dve.tensor_tensor(sum_gained[:, :], sum_gained[:, :], gate[:, e // 3 % 2, :], ALU.add)\
                           .then_inc(gained_added, 1)

            dve.wait_ge(ffn_mul, F_TILES)
            dve.memset(sum_gained[:, :], 0.0).then_inc(gained_cleared, 1)
            dve.wait_ge(gained_cleared, 1)
            g_final = par[:, PARAMS["g_final"]:PARAMS["g_final"] + KT]
            g_second = par[:, PARAMS["g_second"]:PARAMS["g_second"] + KT]
            dve.tensor_tensor(gain2[:, :], g_final, g_second, ALU.mult).then_inc(gain2_done, 1)
            down_body(0)
            dve.wait_ge(strip_done, 1)
            dve.tensor_tensor(strip[:, :], side[0:HEADS_B, 2, 0:3 * P], neg_sb[:, :], ALU.add).then_inc(strip_ready, 1)
            down_body(1)
            dve.wait_ge(stat_done, N_FINAL + 1)
            dve.tensor_scalar(rstd[:, :], side[:, 3, :], 1.0 / D, EPS, ALU.mult, ALU.add).then_inc(stat_read, 1)
            dve.wait_ge(stat_read, N_FINAL + 1)
            dve.wait_ge(gained_stat, 1)
            dve.scalar_tensor_tensor(rstd2[:, :], rstd[:, :], EPS * D, side[:, 2, :], ALU.mult, ALU.add)\
               .then_inc(second_step, 1)
            dve.wait_ge(second_step, 1)
            dve.reciprocal(rstd2[:, :], rstd2[:, :]).then_inc(second_step, 1)
            dve.reciprocal(rstd[:, :], rstd[:, :]).then_inc(recip_done, 1)
            clear_sum(N_FINAL + 1)
            dve.wait_ge(gain2_done, 1)
            dve.wait_ge(rstd2_ready, 1)
            for k in range(KT):
                at_least(dve, act_low, 3 * KT + k - 1)
                dve.scalar_tensor_tensor(part[:, k % 2, :], x2[:, k, :], gain2[:, k:k + 1], rstd2[:, :],
                                         ALU.mult, ALU.mult).then_inc(scaled, 1)
                if k:
                    low_tile(3 * KT, k - 1, xn_high, xn_low, SEQ)
            low_tile(3 * KT, KT - 1, xn_high, xn_low, SEQ)
            dve.wait_ge(rstd_ready, N_FINAL + 1)
            for m in range(R_QKV, R_LAST):
                for s in range(SLOTS):
                    ahead(m, s)
                    k = 4 * (m - R_QKV) + s
                    if k < KT:
                        dve.scalar_tensor_tensor(y_res[:, k, :], x2[:, k, :], col("g_final", k), rstd[:, :],
                                                 ALU.mult, ALU.mult).then_inc(y_ready, 1)
            dve.wait_ge(bias_landed, 16)

            def biased(step):
                g, n = 2 * (step // 8) + step % 2, step % 8 // 2
                lo = 0 if n else P
                pr, sm = sw_probs[step % 2], sw_small[step % 2]
                dve.wait_ge(sw_scores, step + 1)
                at_least(dve, sw_turned, step - 1)
                for r in range(4):
                    at = MEM * (r % 2)
                    dve.tensor_tensor_reduce(pr[:, r, lo:], side[:, 2 * (step % 2) + r // 2, at + lo:at + MEM],
                                             bias[:, 4 * g + r, lo:], 1.0, NEG, ALU.add, ALU.max,
                                             sm[:, 3, r:r + 1]).then_inc(sw_step, 1)
                dve.wait_ge(sw_step, 6 * step + 4)
                sink = par[:, PARAMS["sinks"] + 4 * g:PARAMS["sinks"] + 4 * g + 4]
                dve.tensor_tensor(sm[:, 5, :], sm[:, 3, :], sink, ALU.max).then_inc(sw_step, 1)
                dve.wait_ge(sw_step, 6 * step + 5)
                dve.tensor_scalar(sm[:, 0, :], sm[:, 5, :], -1.0, None, ALU.mult).then_inc(sw_minus, 1)
                dve.tensor_tensor(sm[:, 2, :], sink, sm[:, 5, :], ALU.subtract).then_inc(sw_step, 1)

            def normalised(step):
                lo = 0 if step % 8 >= 2 else P
                pr, sm = sw_probs[step % 2], sw_small[step % 2]
                dve.wait_ge(sw_exp, 5 * step + 5)
                dve.tensor_tensor(sm[:, 4, :], sm[:, 1, :], sm[:, 2, :], ALU.add).then_inc(sw_sum, 1)
                dve.wait_ge(sw_sum, step + 1)
                dve.reciprocal(sm[:, 4, :], sm[:, 4, :]).then_inc(sw_recip, 1)
                dve.wait_ge(sw_recip, step + 1)
                dve.tensor_tensor(pr[:, :, lo:], pr[:, :, lo:],
                                  sm[:, 4, :].unsqueeze(2).broadcast_to((P, 4, 2 * P - lo)), ALU.mult)\
                   .then_inc(sw_ready, 1)

            def gate_tile(k):
                dve.wait_ge(sw_out, 4 * (k // 4) + 4)
                at_least(dve, gated_low, k - 1)
                dve.tensor_tensor(part[:, k % 2, :], o2[:, k, :], z[:, k, :], ALU.mult).then_inc(gated, 1)

            def gated_low_of(k):
                dve.wait_ge(gated_high, k + 1)
                dve.tensor_tensor(o2_low[:, k, :], part[:, k % 2, :], o2_high[:, k, :].bitcast(F32), ALU.subtract)\
                   .then_inc(gated_low, 1)

            biased(0)
            biased(1)
            normalised(0)
            for s in range(SLOTS):
                dve.wait_ge(taken[s], uses(R_LAST))
            for step in range(2 * KT):
                if step % 8 >= 2:
                    dve.wait_ge(sw_turned, step + 1)
                    at_least(dve, sw_pv, step - 1)
                    dve.tensor_copy(sw_probs_t[step % 2][:, 0, :], acc[:, 0, :]).then_inc(sw_turned_dve, 1)
                if step + 1 < 2 * KT:
                    normalised(step + 1)
                if step - 1 in GATE_EARLY:
                    gated_low_of(GATE_EARLY[step - 1])
                if step in GATE_EARLY:
                    gate_tile(GATE_EARLY[step])
                if step + 2 < 2 * KT:
                    biased(step + 2)
            for k in range(4, KT):
                gate_tile(k)
                if k > 4:
                    gated_low_of(k - 1)
            gated_low_of(KT - 1)
            for m in range(R_LAST, ROUNDS):
                residual_round(m, R_LAST, N_LAST, x3, y_res)
            mean_square(N_LAST, SEQ)
            dve.wait_ge(rstd_ready, N_LAST + 1)
            for k in range(KT):
                dve.scalar_tensor_tensor(result[:, k, :], x3[:, k, :], col("g_last", k), rstd[:, :],
                                         ALU.mult, ALU.mult).then_inc(result_ready, 1)


def distance_columns():
    import numpy as np
    exact, buckets, far = 16, 32, 128
    picks = np.zeros((48, 3 * P), np.float32)
    for i in range(3 * P):
        dist = 2 * P - 1 - i
        if 0 <= dist < WINDOW:
            large = exact + int(np.float32(np.log(max(dist, 1) / exact)) / np.log(far / exact) * (buckets - exact)) \
                if dist >= exact else 0
            picks[dist if dist < exact else min(large, buckets - 1), i] = 1.0
        else:
            picks[32:, i] = NEG
    return picks


def kernel(**inputs):
    import numpy as np
    import concourse.bacc as bacc
    from concourse.bass_utils import run_bass_kernel_spmd as run

    a = {k: np.asarray(v) for k, v in inputs.items()}

    def units(w):
        n = w.shape[1] // P
        return w.reshape(KT, P, n, P).transpose(2, 1, 0, 3).reshape(n, P, UNIT)

    def pairs(u, v):
        return np.stack([u, v], 1).reshape(-1, P, UNIT)

    w_in = units(a["w_in"][0])
    gb, gc, v, u, ug, wq = (w_in[8 * i:8 * i + 8] for i in range(6))
    g0, g1, g2 = (w_in[48 + 8 * i:56 + 8 * i] for i in range(3))
    w_up = units(a["w_up"][0])
    down = a["w_down"][0].reshape(F_TILES, P, KT, P).transpose(2, 1, 0, 3)
    down_units = np.zeros((KT, 3, P, KT, P), np.float32)
    for i, (lo, hi) in enumerate(((0, 8), (8, 15), (15, 22))):
        down_units[:, i, :, :hi - lo, :] = down[:, :, lo:hi, :]

    order = np.array([(4 * (2 * p + e) + r) * 64 + c for p in range(2) for r in range(4) for e in range(2)
                      for c in range(64)])
    w2 = a["a_w_in_2"][0]
    qkv = np.concatenate([w2[:, 0:D][:, order], w2[:, D:D + 512]], 1)
    w_z = w2[:, D + 512:][:, order]
    w_last = a["a_w_out_2"][0][order, :]
    weights = np.concatenate([
        units(a["w_kv"][0]), pairs(ug, u), wq,
        np.stack([gc, v, gb], 1).reshape(-1, P, UNIT),
        pairs(g0, units(a["w_a_out"][0])), pairs(g2, units(a["w_att_out"][0])), pairs(g1, units(a["w_b_out"][0])),
        units(a["w_o"][0]), pairs(w_up[:F_TILES], w_up[F_TILES:]), down_units.reshape(-1, P, UNIT),
        units(qkv), units(w_z), units(w_last),
    ])

    def channels(t):
        return np.ascontiguousarray(t.reshape(-1, KT, P).transpose(2, 1, 0))

    def cols(t):
        t = np.atleast_2d(t)
        return t.reshape(t.shape[0], -1, P).transpose(2, 1, 0).reshape(P, -1)

    params = np.concatenate([
        cols(a["norm_mix_g"][0]), cols(a["norm_mem_g"][0]), cols(a["conv_b_w"][0]), cols(a["conv_b_bias"][0]),
        cols(a["ln_b_g"][0]), cols(a["ln_b_b"][0]), cols(a["b_gate"][0]), cols(a["conv_a_w"][0]),
        cols(a["norm_ffn_g"][0]), cols(a["conv_ffn_w"][0]), cols(a["norm_final_g"]), cols(a["norm_g_2"][0]),
        cols(a["final_g_2"]), np.broadcast_to(a["a_sinks_2"][0], (P, HEADS_B)),
    ], 1)
    arrays = {
        "weights": np.ascontiguousarray(weights),
        "x": channels(a["x"][0]),
        "mem": channels(a["mem"][0]),
        "params": np.ascontiguousarray(params),
        "consts": np.concatenate([np.ones((P, P), np.float32), np.eye(P, dtype=np.float32)], 1),
        "table": np.ascontiguousarray(a["t5_table_2"]),
        "onehot": distance_columns(),
    }
    nc = bacc.Bacc("TRN2", target_bir_lowering=False, num_devices=1)
    args = [nc.dram_tensor(n, v.shape, mybir.dt.from_np(v.dtype), kind="ExternalInput").ap()
            for n, v in arrays.items()]
    out = nc.dram_tensor("out", (P, KT, SEQ), F32, kind="ExternalOutput").ap()
    build(nc, *args, out)
    r = run(nc, [arrays], core_ids=[0])
    got = r.results[0]["out"]
    return np.ascontiguousarray(got.transpose(2, 1, 0)).reshape(1, SEQ, D)
```

```python
from contextlib import ExitStack

import concourse.bass as bass
from concourse import mybir

F32 = mybir.dt.float32
F32R = mybir.dt.float32r
ALU = mybir.AluOpType
ACT = mybir.ActivationFunctionType
AX_X = mybir.AxisListType.X

P = 128
SEQ = 512
D = 1024
KT = D // P
MEM = 256
TAPS = 31
F_TILES = 22
HEADS_A, HEADS_B, KV_B = 4, 16, 4
WINDOW = 128
EPS = 1e-6
NEG = -1e30
UNIT = KT * P
SLOTS = 4

R_KV = 0
R_LONG = 4
R_Q = 8
R_SHORT = 10
R_MIX_A = 16
R_MIX_C = 20
R_MIX_B = 24
R_OUT = 28
R_UP = 30
R_DOWN = 41
R_QKV = 47
R_Z = 50
R_LAST = 52
ROUNDS = 54
DOWN_SKIPS = 4

X_TILES = (7, 8, 9, 10, 11, 12, 13, 14)
X_SQUARES = {1: (0, 1), 2: (2, 3), 3: (4, 5), 4: (6, 7)}
X_ROOT = 6
CONV_LONG = (5, 4)
CONV_Q = 4
CONV_SHORT = (6, 0, 2, 6, 0, 3)
CONV_A = (6, 5)
CONV_ENDS = 3
LN_MEAN = 4
LN_CENTRE = {5: (0, 1), 6: (2, 3), 7: (4, 5), 8: (6, 7)}
LN_TOTAL = 9
LN_ROOT = 10
LN_TILES = {11: (0, 1), 12: (2, 3), 13: (4, 5), 14: (6, 7)}

Z_BANK = 3

PARAMS = {}
_at = 0
for _name, _n in (("g_mix", KT), ("g_mem", KT), ("long_w", KT * TAPS), ("long_b", KT), ("ln_g", KT), ("ln_b", KT),
                  ("gate_b", 3 * KT), ("short_w", 3 * KT), ("g_ffn", KT), ("ffn_w", 3 * 2 * F_TILES),
                  ("g_final", KT), ("g_second", KT), ("g_last", KT), ("sinks", HEADS_B)):
    PARAMS[_name] = _at
    _at += _n
N_PARAMS = _at

N_MEM, N_X, N_LN, N_FFN, N_FINAL, N_LAST = range(6)


def build(nc, weights, x, mem, params, consts, table, onehot, out):
    with ExitStack() as ctx:
        base = 16512
        top = [0]

        def sb(name, shape, dt, kb=None):
            n = 4
            for v in shape[1:]:
                n *= v
            if kb is None:
                at = TEMPS + top[0]
                top[0] += (n + 31) // 32 * 32
            else:
                at = int(kb * 1024)
            return nc.alloc_sbuf_tensor_at(name, shape, dt, offset=base + at)

        TEMPS = 185 * 1024

        def sem(name):
            return ctx.enter_context(nc.semaphore(name))

        raw = [sb(f"w_raw{s}", [P, UNIT], F32, 4 * s) for s in range(SLOTS)]
        w_high = sb("w_high", [P, SLOTS, UNIT], F32R, 16)
        w_low = sb("w_low", [P, SLOTS, UNIT], F32R, 32)
        h_high = sb("h_high", [P, KT, SEQ], F32R, 48)
        h_low = sb("h_low", [P, KT, SEQ], F32R, 64)
        long_u = sb("long_u", [P, KT, SEQ + 1], F32, 80)
        x_in = sb("x_in", [P, KT, SEQ], F32, 97)
        q_high = sb("q_high", [P, KT, SEQ], F32R, 97)
        q_low = sb("q_low", [P, KT, SEQ], F32R, 113)
        o_high = sb("o_high", [P, KT, SEQ], F32R, 97)
        mem_high = sb("mem_high", [P, KT, MEM], F32R, 113)
        mem_low = sb("mem_low", [P, KT, MEM], F32R, 121)
        o_low = sb("o_low", [P, KT, SEQ], F32R, 113)
        ya_high = sb("ya_high", [P, KT, SEQ], F32R, 129)
        ya_low = sb("ya_low", [P, KT, SEQ], F32R, 145)
        yb_high = sb("yb_high", [P, KT, SEQ], F32R, 129)
        yb_low = sb("yb_low", [P, KT, SEQ], F32R, 145)
        mem_in = sb("mem_in", [P, KT, MEM], F32, 161)
        k_mem = sb("k_mem", [P, KT, MEM], F32, 161)
        v_mem = sb("v_mem", [P, 2, D], F32, 169)
        v_high = sb("v_high", [P, 2, D], F32R, 161)
        v_low = sb("v_low", [P, 2, D], F32R, 169)
        k_high = ya_low[:, :, 0:MEM]
        k_low = ya_low[:, :, MEM:2 * MEM]
        merged = sb("merged", [P, KT, SEQ], F32, 161)
        m_high = sb("m_high", [P, KT, SEQ], F32R, 97)
        m_low = sb("m_low", [P, KT, SEQ], F32R, 113)
        x1 = sb("x1", [P, KT, SEQ], F32, 80)
        f_high = sb("f_high", [P, F_TILES, SEQ], F32R, 97)
        f_low = sb("f_low", [P, F_TILES, SEQ], F32R, 141)
        xg_high = sb("xg_high", [P, KT, SEQ], F32R, 145)
        xg_low = sb("xg_low", [P, KT, SEQ], F32R, 161)
        rstd_ffn = sb("rstd_ffn", [P, SEQ], F32, 177)
        x2 = sb("x2", [P, KT, SEQ], F32, 48)
        bias = sb("bias", [P, HEADS_B, 2 * P], F32, 113)
        y_res = sb("y_res", [P, KT, SEQ], F32, 97)
        xn_high = sb("xn_high", [P, KT, SEQ], F32R, 80)
        xn_low = sb("xn_low", [P, KT, SEQ], F32R, 64)
        q2 = sb("q2", [P, KT, SEQ], F32, 129)
        k2 = sb("k2", [P, 2, SEQ], F32, 145)
        v2 = sb("v2", [P, 4, 2 * P], F32, 149)
        z = sb("z", [P, KT, SEQ], F32, 153)
        o2 = sb("o2", [P, KT, SEQ], F32, 48)
        o2_high = sb("o2_high", [P, KT, SEQ], F32R, 129)
        o2_low = sb("o2_low", [P, KT, SEQ], F32R, 48)
        x3 = sb("x3", [P, KT, SEQ], F32, 80)
        result = sb("result", [P, KT, SEQ], F32, 153)
        probs = sb("probs", [P, 4, 2 * P], F32, 177)
        probs_t = sb("probs_t", [P, 2, SEQ], F32, 181)
        probs_high = sb("probs_high", [P, 2, SEQ], F32R, 181)
        sw_probs = [probs, sb("sw_probs1", [P, 4, 2 * P], F32, 169)]
        sw_probs_t = [probs_t, sb("sw_probs_t1", [P, 2, SEQ], F32, 173)]

        par = sb("par", [P, N_PARAMS], F32)
        ones_sb = sb("ones_sb", [P, P], F32)
        ident_sb = sb("ident_sb", [P, P], F32, 96.25)
        gate = sb("gate", [P, 2, SEQ], F32)
        convs = sb("convs", [P, 2, SEQ], F32)
        conv_acc, conv_sum = convs[:, 0, :], convs[:, 1, :]
        sw_probs_t.append(convs)
        part = sb("part", [P, 2, SEQ], F32)
        square_at = (TEMPS + top[0]) / 1024
        square = sb("square", [P, 2, SEQ], F32)
        sum_sq = sb("sum_sq", [P, SEQ], F32)
        stat_col = sb("stat_col", [P, 8], F32)
        root_col = sb("root_col", [P, 8], F32)
        small = sb("small", [P, 6, 4], F32)
        sw_small = [small, sb("sw_small1", [P, 6, 4], F32), sb("sw_small2", [P, 6, 4], F32)]
        sw_probs.append(gate.rearrange("p a (b c) -> p (a b) c", b=2))
        gain2 = sb("gain2", [P, KT], F32)
        assert TEMPS + top[0] + base <= 229344, TEMPS + top[0] + base - 229344
        short_c = gate[:, 0, :]
        short_t = gate[:, 1, :]
        short_y = square[:, 0, :]
        mean = conv_sum
        sum_gained = conv_sum
        ffn_y = [gate[:, 0, :], gate[:, 1, :], conv_acc, conv_sum]
        strip = part[0:HEADS_B, 0, 0:3 * P]
        neg_sb = part[0:HEADS_B, 1, 0:3 * P]
        onehot_sb = convs[0:32, 0, 0:3 * P]
        table_sb = convs[0:32, 0, 3 * P:3 * P + HEADS_B]
        x_sum = part[:, 0, :]
        rstd_mem = gate[:, 0, 0:MEM]
        rstd2 = square[:, 0, :]
        probs_low = sb("probs_low", [P, 2, SEQ], F32R, square_at + 2)
        ones, ident = ones_sb[:, :], ident_sb[:, :]

        def col(name, j):
            return par[:, bass.ds(j + PARAMS[name], 1)]

        acc = ctx.enter_context(nc.psum_tensor("acc", [P, SLOTS, SEQ], F32))
        side = ctx.enter_context(nc.psum_tensor("side", [P, 4, SEQ], F32))
        strip_dram = nc.dram_tensor("strip_dram", [HEADS_B, 3 * P], F32, kind="Internal")

        rows_dram = nc.dram_tensor("rows_dram", [P, HEADS_B * 3 * P], F32, kind="Internal")

        landed = [sem(f"weights_landed{s}") for s in range(SLOTS)]
        weight_high = sem("weight_high")
        weight_low = sem("weight_low")
        unit_done = sem("unit_done")
        taken = [sem(f"result_taken{s}") for s in range(SLOTS)]
        x_landed = [sem(f"x_landed{i}") for i in range(2)]
        x_again = sem("x_again")
        mem_landed = [sem(f"mem_landed{i}") for i in range(2)]
        par_landed = sem("par_landed")
        consts_landed = sem("consts_landed")
        pads_set = sem("pads_set")
        squared = sem("squared")
        square_added = sem("square_added")
        sum_cleared = sem("sum_cleared")
        stat_done = sem("stat_done")
        stat_read = sem("stat_read")
        recip_done = sem("recip_done")
        root_done = sem("root_done")
        rstd_ready = sem("rstd_ready")
        scaled = sem("scaled")
        act_high = sem("act_high")
        act_low = sem("act_low")
        conv_step = sem("conv_step")
        short_step = sem("short_step")
        short_high = sem("short_high")
        short_low = sem("short_low")
        merge_part = sem("merge_part")
        merge_done = sem("merge_done")
        merged_high = sem("merged_high")
        merged_low = sem("merged_low")
        mean_done = sem("mean_done")
        mean_read = sem("mean_read")
        centred = sem("centred")
        ln_scaled = sem("ln_scaled")
        ln_silu = sem("ln_silu")
        ln_high = sem("ln_high")
        ln_low = sem("ln_low")
        key_high = sem("key_high")
        key_low = sem("key_low")
        query_high = sem("query_high")
        value_high = sem("value_high")
        value_low = sem("value_low")
        scores_done = sem("scores_done")
        row_max = sem("row_max")
        exp_done = sem("exp_done")
        recip_rows = sem("recip_rows")
        probs_ready = sem("probs_ready")
        probs_turned = sem("probs_turned")
        turned_high = sem("turned_high")
        turned_low = sem("turned_low")
        pv_done = sem("pv_done")
        o_high_done = sem("o_high_done")
        o_low_done = sem("o_low_done")
        ffn_first = sem("ffn_first")
        ffn_step = sem("ffn_step")
        ffn_silu = sem("ffn_silu")
        ffn_mul = sem("ffn_mul")
        ffn_high = sem("ffn_high")
        ffn_low = sem("ffn_low")
        tables_landed = sem("tables_landed")
        strip_done = sem("strip_done")
        strip_ready = sem("strip_ready")
        strip_stored = sem("strip_stored")
        bias_landed = sem("bias_landed")
        gain2_done = sem("gain2_done")
        gained_cleared = sem("gained_cleared")
        gained_squared = sem("gained_squared")
        gained_added = sem("gained_added")
        gained_stat = sem("gained_stat")
        second_step = sem("second_step")
        root2_done = sem("root2_done")
        rstd2_ready = sem("rstd2_ready")
        rstd2_kept = sem("rstd2_kept")
        rstd_mem_kept = sem("rstd_mem_kept")
        rstd_ffn_kept = sem("rstd_ffn_kept")
        gained_high = sem("gained_high")
        gained_low = sem("gained_low")
        first_scaled = sem("first_scaled")
        first_conv = sem("first_conv")
        y_ready = sem("y_ready")
        sw_scores = sem("sw_scores")
        sw_step = sem("sw_step")
        sw_minus = sem("sw_minus")
        sw_sum = sem("sw_sum")
        sw_recip = sem("sw_recip")
        sw_exp = sem("sw_exp")
        sw_ready = sem("sw_ready")
        sw_turned = sem("sw_turned")
        sw_own_turned = sem("sw_own_turned")
        sw_older_turned = sem("sw_older_turned")
        sw_pv = sem("sw_pv")
        sw_out = sem("sw_out")
        z_silu = sem("z_silu")
        gated = sem("gated")
        gated_high = sem("gated_high")
        gated_low = sem("gated_low")
        result_ready = sem("result_ready")
        stored = sem("stored")

        def uses(m, s):
            if not isinstance(m, int) or m < R_QKV:
                return m
            if m < R_LAST:
                return m - DOWN_SKIPS
            return R_Z - DOWN_SKIPS + m - R_LAST + (KT if s == Z_BANK else 0)

        def stats(norm, n):
            return (slice(4, 4 + n), 2) if norm == N_MEM else (slice(0, n), 3)

        def at_least(eng, s, n):
            if not isinstance(n, int) or n > 0:
                eng.wait_ge(s, n)

        def older(step):
            return sum(1 for t in range(step) if t % 8 >= 2)

        SILU_TILES = {2 * KT - 4: (0, 1, 2, 3, 4, 5), 2 * KT - 1: (6,)}
        GATE_TILES = {2 * KT - 2: (0, 1), 2 * KT - 1: (2, 3)}

        def take_window(act, it):
            p, n = it // 4, it % 4
            act.wait_ge(sw_pv, it + 1)
            act.activation(o2[:, 4 * p:4 * p + 4, n * P:(n + 1) * P],
                           acc[:, 2, :].rearrange("p (r c) -> p r c", r=4), ACT.Copy).then_inc(sw_out, 1)

        block = ctx.enter_context(nc.Block())

        @block.sync
        def _(sp):
            for s in range(2):
                sp.dma_start(raw[s][:, :], weights[s]).then_inc(landed[s], 16)
            for i in range(2):
                sp.dma_start(mem_in[:, 4 * i:4 * i + 4, :], mem[:, 4 * i:4 * i + 4, :]).then_inc(mem_landed[i], 16)
            for s in range(2, SLOTS):
                sp.dma_start(raw[s][:, :], weights[s]).then_inc(landed[s], 16)
            for i in range(2):
                sp.dma_start(x_in[:, 4 * i:4 * i + 4, :], x[:, 4 * i:4 * i + 4, :]).then_inc(x_landed[i], 16)
            with sp.Fori(1, ROUNDS) as m:
                for s in range(SLOTS):
                    sp.wait_ge(weight_low, 4 * m + (s - 3))
                    sp.dma_start(raw[s][:, :], weights[4 * m + s]).then_inc(landed[s], 16)
            for j in range(KT):
                sp.wait_ge(result_ready, j + 1)
                sp.dma_start(out[:, j, :], result[:, j, :]).then_inc(stored, 16)
            sp.wait_ge(stored, 16 * KT)

        @block.gpsimd
        def _(pool):
            pool.memset(long_u[:, :, 0:1], 0.0).then_inc(pads_set, 1)
            pool.memset(conv_sum, 0.0).then_inc(pads_set, 1)
            pool.memset(x_sum, 0.0).then_inc(pads_set, 1)
            pool.wait_ge(pads_set, 3)
            for k in range(KT):
                pool.wait_ge(squared, KT * N_X + k + 1)
                pool.wait_ge(square_added, KT * N_X + k)
                pool.tensor_tensor(x_sum, x_sum, square[:, k % 2, :], ALU.add)\
                    .then_inc(square_added, 1)
            pool.wait_ge(ln_low, KT)
            pool.dma_start(x1[:, :, :], x).then_inc(x_again, 16)
            pool.wait_ge(ffn_low, F_TILES)
            pool.dma_start(table_sb, table).then_inc(tables_landed, 16)
            pool.dma_start(onehot_sb, onehot[0:32, :]).then_inc(tables_landed, 16)
            pool.dma_start(neg_sb, onehot[32:48, :]).then_inc(tables_landed, 16)
            pool.wait_ge(strip_ready, 1)
            pool.dma_start(strip_dram[:, :], strip).then_inc(strip_stored, 16)
            pool.wait_ge(strip_stored, 16)
            row = HEADS_B * 3 * P
            pool.dma_start(rows_dram[:, :], bass.AP(strip_dram, 0, [[0, P], [1, row]])).then_inc(strip_stored, 16)
            pool.wait_ge(strip_stored, 32)
            toeplitz = bass.AP(rows_dram, P - 1, [[row - 1, P], [3 * P, HEADS_B], [1, 2 * P]])
            pool.wait_ge(unit_done, 4 * R_QKV)
            pool.dma_start(bias[:, :, :], toeplitz).then_inc(bias_landed, 16)
            pool.wait_ge(bias_landed, 16)

        @block.scalar
        def _(act):
            def round_high(m, s):
                if isinstance(m, int) and m >= ROUNDS:
                    return
                act.wait_ge(landed[s], 16 * m + 16)
                at_least(act, unit_done, 4 * m + (s - 3))
                act.activation(w_high[:, s, :], raw[s][:, :], ACT.Copy).then_inc(weight_high, 1)

            def ahead(m, s):
                round_high(m + (s + 2) // 4, (s + 2) % 4)

            def squares(norm, k, src, width, *waits):
                n = KT * norm + k
                for w in waits:
                    act.wait_ge(*w)
                at_least(act, square_added, n - 1)
                act.activation(square[:, k % 2, 0:width], src, ACT.Square).then_inc(squared, 1)

            def root(norm, n=SEQ // P):
                cols, _ = stats(norm, n)
                act.wait_ge(recip_done, norm + 1)
                act.activation(root_col[:, cols], stat_col[:, cols], ACT.Sqrt).then_inc(root_done, 1)

            def high_tiles(first, high, width):
                for k in range(KT):
                    act.wait_ge(scaled, first - KT + k + 1)
                    act.activation(high[:, k, :], part[:, k % 2, 0:width], ACT.Copy).then_inc(act_high, 1)

            def gate_of(m, half, bias_col=None):
                act.wait_ge(unit_done, 4 * m + (2 * half + 1))
                at_least(act, taken[2 * half + 1], m)
                act.activation(gate[:, half, :], acc[:, 2 * half, :], ACT.Sigmoid,
                               bias=0.0 if bias_col is None else bias_col).then_inc(taken[2 * half], 1)

            def x_high(k):
                act.wait_ge(scaled, k + 1)
                act.activation(h_high[:, k, :], part[:, k % 2, :], ACT.Copy).then_inc(act_high, 1)

            act.dma_start(par[:, :], params).then_inc(par_landed, 16)
            act.dma_start(ones, consts[:, 0:P]).then_inc(consts_landed, 16)
            act.dma_start(ident, consts[:, P:2 * P]).then_inc(consts_landed, 16)
            round_high(0, 0)
            round_high(0, 1)
            act.wait_ge(par_landed, 16)
            for k in range(KT):
                act.wait_ge(mem_landed[k // 4], 16)
                act.activation(mem_high[:, k, :], mem_in[:, k, :], ACT.Copy, scale=col("g_mem", k))\
                   .then_inc(act_high, 1)

            for m in range(R_KV, R_LONG):
                for s in range(SLOTS):
                    ahead(m, s)
                    if m == 0 and s == 0:
                        for k in range(KT):
                            squares(N_MEM, k, mem_in[:, k, :], MEM, (mem_landed[k // 4], 16))
                    if m == 0 and s == 2:
                        root(N_MEM, MEM // P)
                    for k in X_SQUARES.get(4 * m + s, ()):
                        squares(N_X, k, x_in[:, k, :], SEQ, (x_landed[k // 4], 16))
                    if m >= 2 and s % 2 == 1:
                        act.wait_ge(unit_done, 4 * m + s + 1)
                        at = 4 * P * (m - 2) + 2 * P * (s // 2)
                        for t in range(2):
                            act.activation(v_mem[:, t, at:at + 2 * P], acc[:, s - 1 + t, 0:2 * P], ACT.Copy,
                                           scale=root_col[:, 4 + t:5 + t]).then_inc(taken[s - 1 + t], 1)
                    if 4 * m + s == X_ROOT:
                        root(N_X)
                    if 4 * m + s - 1 in X_TILES:
                        x_high(X_TILES.index(4 * m + s - 1))

            for s in range(SLOTS):
                act.wait_ge(taken[s], 2)
            with act.Fori(R_LONG, R_Q) as m:
                for s in range(SLOTS):
                    ahead(m, s)
                    if s % 2 == 1:
                        gate_of(m, s // 2)
                        j = 2 * m + (s // 2 - 2 * R_LONG)
                        act.activation(k_high[:, j, :], k_mem[:, j, :], ACT.Copy).then_inc(key_high, 1)
            act.wait_ge(key_low, KT)
            for b in range(2):
                act.activation(v_high[:, b, :], v_mem[:, b, :], ACT.Copy).then_inc(value_high, 1)
            with act.Fori(R_Q, R_SHORT) as m:
                for s in range(SLOTS):
                    ahead(m, s)
                    act.wait_ge(unit_done, 4 * m + (s + 1))
                    act.activation(q_high[:, 4 * m + (s - 4 * R_Q), :], acc[:, s, :], ACT.Copy,
                                   scale=1.0 / 16).then_inc(query_high, 1)

            def attend(head, stage):
                if stage == 1:
                    act.wait_ge(scores_done, head + 1)
                    act.wait_ge(row_max, head + 1)
                    for t in range(4):
                        act.activation(probs[:, t, :], side[:, t // 2, MEM * (t % 2):MEM * (t % 2) + MEM], ACT.Exp,
                                       bias=small[:, 0, t:t + 1], accum_out=small[:, 1, t:t + 1])\
                           .then_inc(exp_done, 1)
                if stage == 4:
                    act.wait_ge(probs_turned, head + 1)
                    at_least(act, pv_done, head)
                    for b in range(2):
                        act.activation(probs_high[:, b, :], side[:, 2 + b, :], ACT.Copy).then_inc(turned_high, 1)
                if stage == 0 and head:
                    head -= 1
                    act.wait_ge(pv_done, head + 1)
                    for d in range(2):
                        act.activation(o_high[:, 2 * head + d, :], side[:, d, :], ACT.Copy)\
                           .then_inc(o_high_done, 1)

            def short_body(i):
                for e in range(12):
                    m, s, tile, what = 3 * i + (R_SHORT + e // 4), e % 4, 4 * i + e // 3, e % 3
                    ahead(m, s)
                    attend(2 * i + e // 6, e % 6)
                    if what == 0:
                        act.wait_ge(unit_done, 4 * m + (s + 1))
                        at_least(act, short_step, 4 * tile - 3)
                        if tile == 0:
                            act.wait_ge(taken[1], R_SHORT)
                        act.activation(short_c, acc[:, s, :], ACT.Copy).then_inc(taken[s], 1)
                    if what == 2:
                        act.wait_ge(short_step, 4 * tile + 4)
                        act.activation(ya_high[:, tile, :], part[:, e // 3 % 2, :], ACT.Copy)\
                           .then_inc(short_high, 1)

            for i in range(2):
                short_body(i)
            attend(HEADS_A, 0)

            def mix_round(m, first, branch, extra=None):
                for s in range(SLOTS):
                    ahead(m, s)
                    if s % 2 == 1:
                        gate_of(m, s // 2, col("gate_b", 2 * m + (s // 2 - 2 * first + KT * branch)))
                    if extra:
                        extra(m, s)

            def merge_high(m, s):
                if s % 2 == 1:
                    j = 2 * m + (s // 2 - 2 * R_MIX_B)
                    act.wait_ge(merge_done, j + (KT + 1))
                    act.activation(m_high[:, j, :], merged[:, j, :], ACT.Copy).then_inc(merged_high, 1)

            with act.Fori(R_MIX_A, R_MIX_C) as m:
                mix_round(m, R_MIX_A, 0)

            def ln_work(m, s):
                i = 4 * (m - R_MIX_C) + s
                if i in LN_CENTRE:
                    for k in LN_CENTRE[i]:
                        squares(N_LN, k, long_u[:, k, 1:SEQ + 1], SEQ, (centred, k + 1))
                if i == LN_ROOT:
                    root(N_LN)
                for k in LN_TILES.get(i, ()):
                    act.wait_ge(ln_scaled, k + 1)
                    act.activation(part[:, k % 2, :], part[:, k % 2, :], ACT.Silu, bias=col("ln_b", k),
                                   scale=col("ln_g", k)).then_inc(ln_silu, 1)
                    act.wait_ge(ln_silu, k + 1)
                    act.activation(yb_high[:, k, :], part[:, k % 2, :], ACT.Copy).then_inc(ln_high, 1)

            for m in range(R_MIX_C, R_MIX_B):
                mix_round(m, R_MIX_C, 2, ln_work)
            with act.Fori(R_MIX_B, R_OUT) as m:
                mix_round(m, R_MIX_B, 1, merge_high)

            def residual_round(m, first, norm, src, gained=False):
                for s in range(SLOTS):
                    ahead(m, s)
                    n = 4 * m + (s - 4 * first)
                    act.wait_ge(taken[s], uses(first, s) + 1 + (m - first))
                    at_least(act, square_added, n + (KT * norm - 1))
                    act.activation(square[:, s % 2, :], src[:, n, :], ACT.Square).then_inc(squared, 1)
                    if gained:
                        act.activation(xg_high[:, n, :], src[:, n, :], ACT.Copy, scale=col("g_ffn", n))\
                           .then_inc(gained_high, 1)

            with act.Fori(R_OUT, R_UP) as m:
                residual_round(m, R_OUT, N_FFN, x1, True)
            for s in range(2):
                ahead(R_UP, s)
            root(N_FFN)
            high_tiles(2 * KT, h_high, SEQ)

            def up_round(m, opening=False, second=False):
                for s in range(SLOTS):
                    first_pair = opening and s < 2
                    if first_pair:
                        ahead(m, s + 2)
                    elif not opening and not (second and s == 0):
                        ahead(m, s)
                    half = s // 2
                    j = 2 * m + (half - 2 * R_UP)
                    w = 3 * j + (3 * F_TILES * (s % 2) + 2)
                    if first_pair:
                        act.wait_ge(first_scaled, s + 1)
                    else:
                        act.wait_ge(unit_done, 4 * m + (s + 1))
                    at_least(act, ffn_mul, 2 * m + (half - 2 * R_UP - 1))
                    act.activation(ffn_y[s], square[:, s, :] if first_pair else acc[:, s, :], ACT.Copy,
                                   scale=col("ffn_w", w)).then_inc(ffn_first, 1)
                    if s % 2 == 1:
                        if first_pair:
                            act.wait_ge(first_conv, 1)
                        else:
                            act.wait_ge(taken[s - 1], m + 1)
                        act.activation(ffn_y[s - 1], ffn_y[s - 1], ACT.Silu).then_inc(ffn_silu, 1)
                        act.wait_ge(ffn_mul, j + 1)
                        act.activation(f_high[:, j, :], part[:, half, :], ACT.Copy).then_inc(ffn_high, 1)
                        if first_pair:
                            ahead(m + 1, 0)

            up_round(R_UP, True)
            up_round(R_UP + 1, second=True)
            with act.Fori(R_UP + 2, R_DOWN) as m:
                up_round(m)

            def down_body(i):
                for e in range(12):
                    m, s, n = 3 * i + (R_DOWN + e // 4), e % 4, 4 * i + e // 3
                    ahead(m, s)
                    if e % 3 == 2:
                        act.wait_ge(taken[e // 3], i + (R_DOWN + 1))
                        at_least(act, square_added, n + (KT * N_FINAL - 1))
                        act.activation(square[:, e // 3 % 2, :], x2[:, n, :], ACT.Square).then_inc(squared, 1)
                        at_least(act, gained_added, n - 1)
                        act.activation(gate[:, e // 3 % 2, :], x2[:, n, :], ACT.Square, scale=col("g_final", n))\
                           .then_inc(gained_squared, 1)
                        act.activation(xn_high[:, n, :], x2[:, n, :], ACT.Copy, scale=gain2[:, n:n + 1])\
                           .then_inc(act_high, 1)

            act.wait_ge(gain2_done, 1)
            for i in range(2):
                down_body(i)
            for m in range(R_QKV, R_Z):
                for s in range(SLOTS):
                    ahead(m, s)
                    if m == R_QKV and s == 1:
                        act.wait_ge(second_step, 2)
                        act.activation(root_col[:, 4:8], stat_col[:, 4:8], ACT.Sqrt, scale=float(D))\
                           .then_inc(root2_done, 1)
                        root(N_FINAL)
            def exps(step):
                lo = 0 if step % 8 >= 2 else P
                pr, sm = sw_probs[step % 3], sw_small[step % 3]
                act.wait_ge(sw_minus, step + 1)
                act.wait_ge(sw_step, 6 * step + 6)
                for r in range(4):
                    act.activation(pr[:, r, lo:], pr[:, r, lo:], ACT.Exp, bias=sm[:, 0, r:r + 1],
                                   accum_out=sm[:, 1, r:r + 1]).then_inc(sw_exp, 1)
                act.activation(sm[:, 2, :], sm[:, 2, :], ACT.Exp).then_inc(sw_exp, 1)

            def gate_high(k):
                act.wait_ge(gated, k + 1)
                act.activation(o2_high[:, k, :], part[:, k % 2, :], ACT.Copy).then_inc(gated_high, 1)

            def silus(tiles):
                for k in tiles:
                    act.wait_ge(taken[Z_BANK], uses(R_Z, 0) + k + 1)
                    act.activation(z[:, k, :], z[:, k, :], ACT.Silu).then_inc(z_silu, 1)

            exps(0)
            exps(1)
            act.wait_ge(root2_done, 1)
            act.wait_ge(unit_done, 4 * R_Z)
            for t in range(4):
                v = act.activation(v2[:, t, :], acc[:, 2 + t // 2, 2 * P * (t % 2):2 * P * (t % 2 + 1)], ACT.Copy,
                                   scale=root_col[:, 4 + t:5 + t])
                if t % 2 == 1:
                    v.then_inc(taken[2 + t // 2], 1)
            ahead(R_Z, 0)
            for step in range(2 * KT):
                if step % 2 == 0 and 0 < step < 2 * KT - 2:
                    ahead(R_Z + step // 8, step // 2 % 4)
                if step < 2 * KT - 3:
                    act.wait_ge(sw_turned, step + 1)
                    at_least(act, sw_pv, (step - 3) // 2 + 1)
                    act.activation(sw_probs_t[step % 3][:, 1, :], acc[:, 1, :], ACT.Copy)\
                       .then_inc(sw_own_turned, 1)
                if step % 2 == 0 and step:
                    take_window(act, step // 2 - 1)
                if step == 0:
                    exps(2)
                if step + 3 < 2 * KT:
                    exps(step + 3)
                if step == 2 * KT - 4:
                    ahead(R_Z + 1, KT - 5)
                silus(SILU_TILES.get(step, ()))
                for k in GATE_TILES.get(step, ()):
                    gate_high(k)
            silus((KT - 1,))
            take_window(act, KT - 1)
            for k in range(4, KT):
                gate_high(k)
            for m in range(R_LAST, ROUNDS):
                residual_round(m, R_LAST, N_LAST, x3)
            root(N_LAST)

        @block.tensor
        def _(pe):
            def product(m, s, moving, width=SEQ, blocks=range(KT), bank=None, first=True, last=True,
                        used=None, ready=None, skip=0, ends=True):
                bank = s if bank is None else bank
                pe.wait_ge(weight_low, 4 * m + (s + 1))
                if first:
                    at_least(pe, taken[bank], uses(m, bank) if used is None else used)
                for b, k in enumerate(blocks):
                    if ready:
                        pe.wait_ge(ready[0], ready[1] + k + 1)
                    for w, v in ((w_high, 0), (w_high, 1), (w_low, 0)):
                        mm = pe.matmul(acc[:, bank, 0:width], w[:, s, (skip + b) * P:(skip + b + 1) * P],
                                       moving[v][:, k, :], start=first and b == 0 and w is w_high and v == 0,
                                       stop=last and b == len(blocks) - 1 and w is w_low)
                if ends:
                    mm.then_inc(unit_done, 1)

            def two(m, s, moving, ready, width=SEQ, between={}):
                for i in range(2):
                    pe.wait_ge(weight_low, 4 * m + (s + i + 1))
                    at_least(pe, taken[s + i], uses(m, s + i))
                for k in range(KT):
                    if k in between:
                        between[k]()
                    pe.wait_ge(ready[0], ready[1] + k + 1)
                    for i in range(2):
                        for w, v in ((w_high, 0), (w_high, 1), (w_low, 0)):
                            mm = pe.matmul(acc[:, s + i, 0:width], w[:, s + i, k * P:(k + 1) * P],
                                           moving[v][:, k, :], start=k == 0 and w is w_high and v == 0,
                                           stop=k == KT - 1 and w is w_low)
                        if k == KT - 1:
                            mm.then_inc(unit_done, 1)

            def rows(m, s, still, tiles, of=None):
                pe.wait_ge(weight_low, 4 * m + (s + 2))
                for i in range(2):
                    at_least(pe, taken[s + i], uses(m, s + i))
                half = tiles // 2
                for t in range(tiles) if of is None else of:
                    at = 2 * P * (t % half)
                    for k in range(KT):
                        for v, w in ((0, w_high), (0, w_low), (1, w_high)):
                            mm = pe.matmul(acc[:, s + t // half, at:at + 2 * P], still[v][:, k, t * P:(t + 1) * P],
                                           w[:, s:s + 2, k * P:(k + 1) * P], start=k == 0 and v == 0 and w is w_high,
                                           stop=k == KT - 1 and v == 1)
                if t == tiles - 1:
                    mm.then_inc(unit_done, 2)

            def total(norm, width):
                pe.wait_ge(square_added, KT * (norm + 1))
                bank = stats(norm, 1)[1]
                sums = x_sum if norm == N_X else sum_sq
                for t in range(width // P):
                    mm = pe.matmul(side[:, bank, t:t + 1], sums[:, t * P:(t + 1) * P], ones[:, 0:1],
                                   start=True, stop=True)
                mm.then_inc(stat_done, 1)

            def spread(norm, width):
                pe.wait_ge(root_done, norm + 1)
                cols, bank = stats(norm, width // P)
                for t in range(width // P):
                    mm = pe.matmul(side[:, bank, t * P:(t + 1) * P], root_col[:, cols][:, t:t + 1].broadcast_to((P, P)), ident,
                                   start=True, stop=True)
                mm.then_inc(rstd_ready, 1)

            h = (h_high, h_low)
            memory = (mem_high, mem_low)
            two(0, 0, memory, (act_low, 0), MEM)
            pe.wait_ge(consts_landed, 32)
            for i in range(2, 2 * SLOTS):
                product(i // 4, i % 4, memory, MEM)
                if i == 2:
                    total(N_MEM, MEM)
                if i == 3:
                    spread(N_MEM, MEM)
                if i == X_ROOT - 1:
                    total(N_X, SEQ)
                if i == X_ROOT:
                    spread(N_X, SEQ)
            for m in range(R_KV + 2, R_LONG):
                for s in (0, 2):
                    rows(m, s, memory, 2)
            two(R_LONG, 0, h, (act_low, KT))
            for s in range(2, SLOTS):
                product(R_LONG, s, h)
            with pe.Fori(R_LONG + 1, R_SHORT) as m:
                for s in range(SLOTS):
                    product(m, s, h)

            def attend(head, stage):
                if stage == 0:
                    for s in range(SLOTS):
                        pe.wait_ge(taken[s], R_SHORT)
                    at_least(pe, o_low_done, 2 * head)
                    pe.wait_ge(key_low, KT)
                    for t in range(4):
                        for d in range(2):
                            for query, key in ((q_high, k_high), (q_high, k_low), (q_low, k_high)):
                                mm = pe.matmul(side[:, t // 2, MEM * (t % 2):MEM * (t % 2) + MEM],
                                               query[:, 2 * head + d, t * P:(t + 1) * P], key[:, 2 * head + d, :],
                                               start=d == 0 and query is q_high and key is k_high,
                                               stop=d == 1 and query is q_low)
                    mm.then_inc(scores_done, 1)
                if stage == 3:
                    pe.wait_ge(probs_ready, 4 * head + 4)
                    at_least(pe, turned_low, 2 * head)
                    for t in range(4):
                        for b in range(2):
                            mm = pe.transpose(side[:, 2 + b, t * P:(t + 1) * P], probs[:, t, b * P:(b + 1) * P],
                                              ident)
                    mm.then_inc(probs_turned, 1)
                if stage == 5:
                    pe.wait_ge(value_low, 2)
                    pe.wait_ge(turned_low, 2 * head + 2)
                    for d in range(2):
                        for b in range(2):
                            for i, (v, p) in enumerate(((v_high, probs_high[:, b, :]), (v_high, probs_low[:, b, :]),
                                                        (v_low, probs_high[:, b, :]))):
                                mm = pe.matmul(side[:, d, :], v[:, b, (2 * head + d) * P:(2 * head + d + 1) * P],
                                               p, start=b == 0 and i == 0, stop=b == 1 and i == 2)
                    mm.then_inc(pv_done, 1)

            for i in range(2):
                for e in range(12):
                    m, s = 3 * i + R_SHORT + e // 4, e % 4
                    product(m, s, h)
                    attend(2 * i + e // 6, e % 6)

            product(R_MIX_A, 0, h)
            pe.wait_ge(short_low, KT)
            product(R_MIX_A, 1, (ya_high, ya_low))
            product(R_MIX_A, 2, h)
            product(R_MIX_A, 3, (ya_high, ya_low))

            def mix_round(m, moving):
                for s in range(SLOTS):
                    product(m, s, h if s % 2 == 0 else moving)

            with pe.Fori(R_MIX_A + 1, R_MIX_C) as m:
                mix_round(m, (ya_high, ya_low))
            pe.wait_ge(o_low_done, KT)
            for m in range(R_MIX_C, R_MIX_B):
                for s in range(SLOTS):
                    product(m, s, h if s % 2 == 0 else (o_high, o_low))
                    i = 4 * (m - R_MIX_C) + s
                    if i == LN_MEAN:
                        pe.wait_ge(conv_step, 32 * KT)
                        pe.matmul(side[:, 2, :], ones, conv_sum, start=True, stop=True).then_inc(mean_done, 1)
                    if i == LN_TOTAL:
                        total(N_LN, SEQ)
                    if i == LN_ROOT:
                        spread(N_LN, SEQ)
            product(R_MIX_B, 0, h)
            product(R_MIX_B, 1, (yb_high, yb_low), ready=(ln_low, 0))
            product(R_MIX_B, 2, h)
            product(R_MIX_B, 3, (yb_high, yb_low))
            with pe.Fori(R_MIX_B + 1, R_OUT) as m:
                mix_round(m, (yb_high, yb_low))
            two(R_OUT, 0, (m_high, m_low), (merged_low, 0))
            for s in range(2, SLOTS):
                product(R_OUT, s, (m_high, m_low))
            for s in range(SLOTS):
                product(R_OUT + 1, s, (m_high, m_low))
            two(R_UP, 0, (xg_high, xg_low), (gained_low, 0),
                between={2: lambda: total(N_FFN, SEQ), 4: lambda: spread(N_FFN, SEQ)})
            two(R_UP, 2, h, (act_low, 2 * KT))
            with pe.Fori(R_UP + 1, R_DOWN) as m:
                for s in range(SLOTS):
                    product(m, s, h)

            def down_body(i):
                for e in range(12):
                    m, s = 3 * i + (R_DOWN + e // 4), e % 4
                    blocks = (range(0, 8), range(8, 15), range(15, 22))[e % 3]
                    if e < 3:
                        pe.wait_ge(ffn_low, blocks[-1] + 1)
                    product(m, s, (f_high, f_low), blocks=blocks, bank=e // 3, first=e % 3 == 0,
                            last=e % 3 == 2, used=i + R_DOWN)

            down_body(0)
            pe.wait_ge(tables_landed, 48)
            pe.matmul(side[0:HEADS_B, 2, 0:3 * P], table_sb, onehot_sb, start=True, stop=True)\
              .then_inc(strip_done, 1)
            down_body(1)
            xn = (xn_high, xn_low)
            two(R_QKV, 0, xn, (act_low, 3 * KT))
            total(N_FINAL, SEQ)
            pe.wait_ge(gained_added, KT)
            for t in range(SEQ // P):
                mm = pe.matmul(side[:, 2, t:t + 1], sum_gained[:, t * P:(t + 1) * P], ones[:, 0:1],
                               start=True, stop=True)
            mm.then_inc(gained_stat, 1)
            product(R_QKV, 2, xn)
            pe.wait_ge(root2_done, 1)
            for t in range(SEQ // P):
                mm = pe.matmul(side[:, 2, t * P:(t + 1) * P], root_col[:, 4 + t:5 + t].broadcast_to((P, P)), ident,
                               start=True, stop=True)
            mm.then_inc(rstd2_ready, 1)
            spread(N_FINAL, SEQ)
            product(R_QKV, 3, xn)
            for s in range(SLOTS):
                product(R_QKV + 1, s, xn)
            for s in range(2):
                product(R_QKV + 2, s, xn)
            rows(R_QKV + 2, 2, xn, 4, range(2))

            def window_of(step):
                g, n = 2 * (step // 8) + step % 2, step % 8 // 2
                return g, g // 2, 64 * (g % 2), n, (0, 1) if n else (1,)

            def scores(step):
                g, p, at, n, blocks = window_of(step)
                at_least(pe, sw_step, 6 * (step - 2) + 4)
                for r in range(4):
                    mm = pe.matmul(side[:, 2 * (step % 2) + r // 2, MEM * (r % 2) + P * blocks[0]:MEM * (r % 2) + MEM],
                                   q2[at:at + 64, 4 * p + r, n * P:(n + 1) * P],
                                   k2[at:at + 64, p, (n - 1 + blocks[0]) * P:(n + 1) * P], start=True, stop=True)
                mm.then_inc(sw_scores, 1)

            def turn(step):
                blocks = window_of(step)[4]
                pe.wait_ge(sw_ready, step + 1)
                at_least(pe, sw_own_turned, step)
                at_least(pe, sw_older_turned, older(step))
                for b in blocks:
                    for r in range(4):
                        mm = pe.transpose(acc[:, b, r * P:(r + 1) * P], sw_probs[step % 3][:, r, b * P:(b + 1) * P],
                                          ident)
                mm.then_inc(sw_turned, 1)

            def outputs(it):
                step = 2 * it
                n, blocks = window_of(step)[3:]
                pe.wait_ge(sw_own_turned, step + 2)
                at_least(pe, sw_older_turned, older(step + 2))
                at_least(pe, sw_out, it)
                for b in blocks:
                    for e in range(2):
                        g, _, at = window_of(step + e)[:3]
                        mm = pe.matmul(acc[at:at + 64, 2, :], v2[:, n - 1 + b, g * 64:(g + 1) * 64],
                                       sw_probs_t[(step + e) % 3][:, b, :], start=b == blocks[0], stop=b == 1)
                mm.then_inc(sw_pv, 1)

            for s in range(2):
                pe.wait_ge(taken[s], uses(R_Z, s))
            pe.wait_ge(y_ready, KT)
            scores(0)
            scores(1)
            rows(R_QKV + 2, 2, xn, 4, range(2, 4))
            scores(2)
            for s in range(2, SLOTS):
                pe.wait_ge(taken[s], uses(R_Z, s))
            for step in range(2 * KT):
                turn(step)
                if step + 3 < 2 * KT:
                    scores(step + 3)
                j, half = step // 2, step % 2
                product(R_Z + j // 4, j % 4, xn, blocks=range(4 * half, 4 * half + 4), bank=Z_BANK,
                        skip=4 * half, first=half == 0, last=half == 1, ends=half == 1,
                        used=uses(R_Z, 0) + j)
                if step % 2 == 1:
                    outputs(step // 2)
            two(R_LAST, 0, (o2_high, o2_low), (gated_low, 0))
            pe.wait_ge(sw_out, KT)
            for s in range(2, SLOTS):
                product(R_LAST, s, (o2_high, o2_low))
            for s in range(SLOTS):
                product(R_LAST + 1, s, (o2_high, o2_low))
            total(N_LAST, SEQ)
            spread(N_LAST, SEQ)

        @block.vector
        def _(dve):
            def take_low(m, s):
                if isinstance(m, int) and m >= ROUNDS:
                    return
                dve.wait_ge(weight_high, 4 * m + (s + 1))
                dve.tensor_tensor(w_low[:, s, :], raw[s][:, :], w_high[:, s, :].bitcast(F32), ALU.subtract)\
                   .then_inc(weight_low, 1)

            def ahead(m, s):
                take_low(m + (s + 2) // 4, (s + 2) % 4)

            def clear_sum(n):
                dve.memset(sum_sq[:, :], 0.0).then_inc(sum_cleared, 1)

            def add_square(norm, k, slot, width=SEQ):
                n = k + KT * norm
                dve.wait_ge(squared, n + 1)
                at_least(dve, square_added, n)
                dve.wait_ge(sum_cleared, norm + 1)
                dve.tensor_tensor(sum_sq[:, 0:width], sum_sq[:, 0:width], square[:, slot, 0:width], ALU.add)\
                   .then_inc(square_added, 1)

            def mean_square(norm, width):
                n = width // P
                cols, bank = stats(norm, n)
                dve.wait_ge(stat_done, norm + 1)
                dve.tensor_scalar(stat_col[:, cols], side[:, bank, 0:n], 1.0 / D, EPS, ALU.mult, ALU.add)\
                   .then_inc(stat_read, 1)
                dve.wait_ge(stat_read, norm + 1)
                dve.reciprocal(stat_col[:, cols], stat_col[:, cols]).then_inc(recip_done, 1)
                if norm != N_X:
                    clear_sum(norm + 1)

            def scale_tile(first, k, src, gain, width):
                dve.scalar_tensor_tensor(part[:, k % 2, 0:width], src, col(gain, k), side[:, 3, 0:width],
                                         ALU.mult, ALU.mult).then_inc(scaled, 1)

            def low_tile(first, k, high, low, width):
                dve.wait_ge(act_high, first + k + 1)
                dve.tensor_tensor(low[:, k, :], part[:, k % 2, 0:width], high[:, k, :].bitcast(F32), ALU.subtract)\
                   .then_inc(act_low, 1)

            def scale_all(norm, first, src, gain, high, low, width):
                dve.wait_ge(rstd_ready, norm + 1)
                for k in range(KT):
                    at_least(dve, act_low, first + k - 1)
                    scale_tile(first, k, src[:, k, :], gain, width)
                    if k:
                        low_tile(first, k - 1, high, low, width)
                low_tile(first, KT - 1, high, low, width)

            taps = list(range(1, TAPS)) + [0]

            def conv(tile, ops):
                for n in ops:
                    if n == TAPS:
                        dve.wait_ge(conv_step, 32 * tile + n)
                        dve.tensor_tensor(conv_sum, conv_sum, long_u[:, tile, 1:SEQ + 1], ALU.add)\
                           .then_inc(conv_step, 1)
                        continue
                    shift = taps[n]
                    w = col("long_w", TAPS * tile + (TAPS - 1 - shift))
                    if n == 0:
                        dve.wait_ge(taken[1 + 2 * (tile % 2)], R_LONG + tile // 2 + 1)
                        at_least(dve, conv_step, 32 * tile)
                        dve.tensor_scalar(conv_acc, long_u[:, tile, 0:SEQ], w, col("long_b", tile),
                                          ALU.mult, ALU.add).then_inc(conv_step, 1)
                    elif shift:
                        dve.wait_ge(conv_step, 32 * tile + n)
                        dve.scalar_tensor_tensor(conv_acc[:, shift:SEQ], long_u[:, tile, 1:SEQ + 1 - shift], w,
                                                 conv_acc[:, shift:SEQ], ALU.mult, ALU.add).then_inc(conv_step, 1)
                    else:
                        dve.wait_ge(conv_step, 32 * tile + n)
                        dve.scalar_tensor_tensor(long_u[:, tile, 1:SEQ + 1], long_u[:, tile, 1:SEQ + 1], w,
                                                 conv_acc, ALU.mult, ALU.add).then_inc(conv_step, 1)

            dve.memset(sum_sq[:, :], 0.0).then_inc(sum_cleared, 1)
            take_low(0, 0)
            take_low(0, 1)
            dve.wait_ge(par_landed, 16)
            for k in range(KT):
                dve.wait_ge(act_high, k + 1)
                dve.scalar_tensor_tensor(mem_low[:, k, :], mem_in[:, k, :], col("g_mem", k),
                                         mem_high[:, k, :].bitcast(F32), ALU.mult, ALU.subtract).then_inc(act_low, 1)
            for m in range(R_KV, R_LONG):
                for s in range(SLOTS):
                    ahead(m, s)
                    i = 4 * m + s
                    if i == 0:
                        for k in range(KT):
                            add_square(N_MEM, k, k % 2, MEM)
                    if i == 1:
                        mean_square(N_MEM, MEM)
                    for k in ((0, 1, 2) if i == 2 else (i,) if 2 < i < 2 * SLOTS else ()):
                        if k == 0:
                            dve.wait_ge(rstd_ready, N_MEM + 1)
                            dve.tensor_copy(rstd_mem, side[:, 2, 0:MEM]).then_inc(rstd_mem_kept, 1)
                            dve.wait_ge(rstd_mem_kept, 1)
                        dve.wait_ge(unit_done, k + 1)
                        dve.tensor_tensor(k_mem[:, k, :], acc[:, k % 4, 0:MEM], rstd_mem, ALU.mult)\
                           .then_inc(taken[k % 4], 1)
                    if i == X_ROOT:
                        mean_square(N_X, SEQ)
                    if i in X_TILES:
                        k = X_TILES.index(i)
                        if k == 0:
                            dve.wait_ge(rstd_ready, N_X + 1)
                        if k > 1:
                            dve.wait_ge(act_low, KT + k - 1)
                        scale_tile(KT, k, x_in[:, k, :], "g_mix", SEQ)
                        if k:
                            low_tile(KT, k - 1, h_high, h_low, SEQ)
            low_tile(KT, KT - 1, h_high, h_low, SEQ)

            dve.wait_ge(pads_set, 3)
            steps = TAPS + 1

            def conv_by(n, at=[0]):
                for _ in range(n):
                    conv(at[0] // steps, [at[0] % steps])
                    at[0] += 1

            for m in range(R_LONG, R_Q):
                for s in range(SLOTS):
                    ahead(m, s)
                    if m > R_LONG:
                        conv_by(CONV_LONG[s % 2])
                    if s % 2 == 1:
                        half = s // 2
                        dve.wait_ge(taken[s - 1], m + 1)
                        dve.wait_ge(unit_done, 4 * m + (s + 1))
                        dve.tensor_tensor(long_u[:, 2 * (m - R_LONG) + half, 1:SEQ + 1], acc[:, s, :],
                                          gate[:, half, :], ALU.mult).then_inc(taken[s], 1)
                        j = 2 * (m - R_LONG) + half
                        dve.wait_ge(key_high, j + 1)
                        dve.tensor_tensor(k_low[:, j, :], k_mem[:, j, :], k_high[:, j, :].bitcast(F32),
                                          ALU.subtract).then_inc(key_low, 1)
            for m in range(R_Q, R_SHORT):
                for s in range(SLOTS):
                    ahead(m, s)
                    conv_by(CONV_Q)
                    j = 4 * (m - R_Q) + s
                    dve.wait_ge(query_high, j + 1)
                    dve.scalar_tensor_tensor(q_low[:, j, :], acc[:, s, :], 1.0 / 16, q_high[:, j, :].bitcast(F32),
                                             ALU.mult, ALU.subtract).then_inc(taken[s], 1)
                    if j in (1, 2):
                        dve.wait_ge(value_high, 2)
                        dve.tensor_tensor(v_low[:, j - 1, :], v_mem[:, j - 1, :], v_high[:, j - 1, :].bitcast(F32),
                                          ALU.subtract).then_inc(value_low, 1)

            def attend(head, stage):
                if stage == 1:
                    dve.wait_ge(scores_done, head + 1)
                    dve.tensor_reduce(small[:, 0, :], side[:, 0:2, :].rearrange("p a (b c) -> p (a b) c", b=2),
                                      AX_X, ALU.max, negate=True).then_inc(row_max, 1)
                if stage == 2:
                    dve.wait_ge(exp_done, 4 * head + 4)
                    dve.reciprocal(small[:, 2, :], small[:, 1, :]).then_inc(recip_rows, 1)
                    dve.wait_ge(recip_rows, head + 1)
                    for t in range(4):
                        dve.tensor_scalar(probs[:, t, :], probs[:, t, :], small[:, 2, t:t + 1], None, ALU.mult)\
                           .then_inc(probs_ready, 1)
                if stage == 4:
                    dve.wait_ge(probs_turned, head + 1)
                    at_least(dve, pv_done, head)
                    for b in range(2):
                        dve.wait_ge(turned_high, 2 * head + b + 1)
                        dve.tensor_tensor(probs_low[:, b, :], side[:, 2 + b, :], probs_high[:, b, :].bitcast(F32),
                                          ALU.subtract).then_inc(turned_low, 1)
                if stage == 0 and head:
                    head -= 1
                    dve.wait_ge(pv_done, head + 1)
                    for d in range(2):
                        dve.wait_ge(o_high_done, 2 * head + (d + 1))
                        dve.tensor_tensor(o_low[:, 2 * head + d, :], side[:, d, :],
                                          o_high[:, 2 * head + d, :].bitcast(F32), ALU.subtract)\
                           .then_inc(o_low_done, 1)

            def short_body(i):
                for e in range(12):
                    m, s, t, what = 3 * i + (R_SHORT + e // 4), e % 4, e // 3, e % 3
                    tile = 4 * i + t
                    ahead(m, s)
                    attend(2 * i + e // 6, e % 6)
                    conv_by(CONV_SHORT[e % 6])
                    n = 4 * tile
                    if what == 1:
                        dve.wait_ge(taken[(s - 1) % 4], m + (1 if s else 0))
                        dve.wait_ge(unit_done, 4 * m + (s + 1))
                        at_least(dve, short_step, n)
                        dve.tensor_tensor(short_t, acc[:, s, :], short_c, ALU.mult).then_inc(short_step, 1)
                        dve.wait_ge(short_step, n + 1)
                        dve.tensor_scalar(short_y, short_t, col("short_w", 3 * tile + 2), None, ALU.mult)\
                           .then_inc(short_step, 1)
                        for shift in (1, 2):
                            dve.wait_ge(short_step, n + 1 + shift)
                            ins = dve.scalar_tensor_tensor(
                                square[:, 0, shift:SEQ], gate[:, 1, 0:SEQ - shift],
                                col("short_w", 3 * tile + (2 - shift)), square[:, 0, shift:SEQ], ALU.mult, ALU.add)
                            ins.then_inc(short_step if shift == 1 else taken[s], 1)
                    if what == 2:
                        dve.wait_ge(unit_done, 4 * m + (s + 1))
                        dve.wait_ge(taken[(s - 1) % 4], m + (1 if s else 0))
                        at_least(dve, short_low, tile - 1)
                        dve.tensor_tensor(part[:, t % 2, :], acc[:, s, :], short_y, ALU.mult).then_inc(short_step, 1)
                        dve.wait_ge(short_step, n + 4)
                        dve.memset(small[:, 5, 0:1], 0.0).then_inc(taken[s], 1)
                        dve.wait_ge(short_high, tile + 1)
                        dve.tensor_tensor(ya_low[:, tile, :], part[:, t % 2, :], ya_high[:, tile, :].bitcast(F32),
                                          ALU.subtract).then_inc(short_low, 1)

            for i in range(2):
                short_body(i)
            attend(HEADS_A, 0)
            clear_sum(N_LN)

            def mix_round(m, first, kind, extra=None):
                for s in range(SLOTS):
                    ahead(m, s)
                    if s % 2 == 1:
                        half = s // 2
                        j = 2 * m + (half - 2 * first)
                        dve.wait_ge(taken[s - 1], m + 1)
                        dve.wait_ge(unit_done, 4 * m + (s + 1))
                        if kind == 0:
                            dve.tensor_tensor(merged[:, j, :], acc[:, s, :], gate[:, half, :], ALU.mult)\
                               .then_inc(taken[s], 1)
                        else:
                            dve.tensor_tensor(gate[:, half, :], acc[:, s, :], gate[:, half, :], ALU.mult)\
                               .then_inc(merge_part, 1)
                            dve.wait_ge(merge_part, j + (KT * (kind - 1) + 1))
                            dve.tensor_tensor(merged[:, j, :], merged[:, j, :], gate[:, half, :], ALU.add)\
                               .then_inc(merge_done, 1)
                            dve.wait_ge(merge_done, j + (KT * (kind - 1) + 1))
                            dve.memset(small[:, 5, 0:1], 0.0).then_inc(taken[s], 1)
                    if extra:
                        extra(m, s)

            def conv_part(m, s):
                conv_by(CONV_A[s % 2])

            for m in range(R_MIX_A, R_MIX_C):
                mix_round(m, R_MIX_A, 0, conv_part)

            def ln_work(m, s):
                i = 4 * (m - R_MIX_C) + s
                if i <= CONV_ENDS:
                    rest = steps * KT - 6 * sum(CONV_LONG) - 8 * CONV_Q - 4 * sum(CONV_SHORT) - 8 * sum(CONV_A)
                    conv_by(rest * (i + 1) // (CONV_ENDS + 1) - rest * i // (CONV_ENDS + 1))
                if i == LN_MEAN:
                    dve.wait_ge(mean_done, 1)
                    dve.tensor_scalar(mean, side[:, 2, :], 1.0 / D, None, ALU.mult).then_inc(mean_read, 1)
                    dve.wait_ge(mean_read, 1)
                if i in LN_CENTRE:
                    for k in LN_CENTRE[i]:
                        dve.tensor_tensor(long_u[:, k, 1:SEQ + 1], long_u[:, k, 1:SEQ + 1], mean,
                                          ALU.subtract).then_inc(centred, 1)
                    for k in LN_CENTRE[i]:
                        add_square(N_LN, k, k % 2)
                if i == LN_ROOT:
                    mean_square(N_LN, SEQ)
                if i == LN_ROOT + 1:
                    dve.wait_ge(rstd_ready, N_LN + 1)
                for k in LN_TILES.get(i, ()):
                    at_least(dve, ln_low, k - 1)
                    dve.tensor_tensor(part[:, k % 2, :], long_u[:, k, 1:SEQ + 1], side[:, 3, :], ALU.mult)\
                       .then_inc(ln_scaled, 1)
                for k in LN_TILES.get(i, ()):
                    dve.wait_ge(ln_high, k + 1)
                    dve.tensor_tensor(yb_low[:, k, :], part[:, k % 2, :], yb_high[:, k, :].bitcast(F32),
                                      ALU.subtract).then_inc(ln_low, 1)

            for m in range(R_MIX_C, R_MIX_B):
                mix_round(m, R_MIX_C, 1, ln_work)

            def merge_low(m, s):
                if s % 2 == 1:
                    j = 2 * m + (s // 2 - 2 * R_MIX_B)
                    dve.wait_ge(merged_high, j + 1)
                    dve.tensor_tensor(m_low[:, j, :], merged[:, j, :], m_high[:, j, :].bitcast(F32), ALU.subtract)\
                       .then_inc(merged_low, 1)

            with dve.Fori(R_MIX_B, R_OUT) as m:
                mix_round(m, R_MIX_B, 2, merge_low)
            dve.wait_ge(x_again, 16)

            def residual_round(m, first, norm, dst, src, gained=False):
                for s in range(SLOTS):
                    ahead(m, s)
                    n = 4 * m + (s - 4 * first)
                    dve.wait_ge(unit_done, 4 * m + (s + 1))
                    dve.tensor_tensor(dst[:, n, :], acc[:, s, :], src[:, n, :], ALU.add).then_inc(taken[s], 1)
                    add_square(norm, n, s % 2)
                    if gained:
                        dve.wait_ge(gained_high, n + 1)
                        dve.scalar_tensor_tensor(xg_low[:, n, :], dst[:, n, :], col("g_ffn", n),
                                                 xg_high[:, n, :].bitcast(F32), ALU.mult, ALU.subtract)\
                           .then_inc(gained_low, 1)

            with dve.Fori(R_OUT, R_UP) as m:
                residual_round(m, R_OUT, N_FFN, x1, x1, True)
            for s in range(2):
                ahead(R_UP, s)
            mean_square(N_FFN, SEQ)
            dve.wait_ge(rstd_ready, N_FFN + 1)
            dve.tensor_copy(rstd_ffn[:, :], side[:, 3, :]).then_inc(rstd_ffn_kept, 1)
            scale_all(N_FFN, 2 * KT, x1, "g_ffn", h_high, h_low, SEQ)

            def up_round(m, opening=False, second=False):
                if opening:
                    dve.wait_ge(rstd_ffn_kept, 1)
                    for s in range(2):
                        ahead(m, s + 2)
                        dve.wait_ge(unit_done, 4 * m + s + 1)
                        dve.tensor_tensor(square[:, s, :], acc[:, s, :], rstd_ffn[:, :], ALU.mult)\
                           .then_inc(first_scaled, 1)
                        dve.wait_ge(first_scaled, s + 1)
                        dve.memset(small[:, 5, 0:1], 0.0).then_inc(taken[s], 1)
                for s in range(SLOTS):
                    if not opening and not (second and s == 0):
                        ahead(m, s)
                    first_pair = opening and s < 2
                    u = square[:, s, :] if first_pair else acc[:, s, :]
                    half = s // 2
                    j = 2 * m + (half - 2 * R_UP)
                    w = 3 * j + 3 * F_TILES * (s % 2)
                    dve.wait_ge(ffn_first, 4 * m + (s + 1 - 4 * R_UP))
                    y = ffn_y[s]
                    dve.scalar_tensor_tensor(y[:, 1:SEQ], u[:, 0:SEQ - 1], col("ffn_w", w + 1), y[:, 1:SEQ],
                                             ALU.mult, ALU.add).then_inc(ffn_step, 1)
                    dve.wait_ge(ffn_step, 4 * m + (s + 1 - 4 * R_UP))
                    dve.scalar_tensor_tensor(y[:, 2:SEQ], u[:, 0:SEQ - 2], col("ffn_w", w), y[:, 2:SEQ],
                                             ALU.mult, ALU.add).then_inc(first_conv if first_pair else taken[s], 1)
                    if s % 2 == 1:
                        if first_pair:
                            dve.wait_ge(first_conv, 2)
                        else:
                            dve.wait_ge(taken[s], m + 1)
                        dve.wait_ge(ffn_silu, j + 1)
                        at_least(dve, ffn_low, j - 1)
                        dve.tensor_tensor(part[:, half, :], ffn_y[s - 1], y, ALU.mult).then_inc(ffn_mul, 1)
                        dve.wait_ge(ffn_high, j + 1)
                        dve.tensor_tensor(f_low[:, j, :], part[:, half, :], f_high[:, j, :].bitcast(F32),
                                          ALU.subtract).then_inc(ffn_low, 1)
                        if first_pair:
                            ahead(m + 1, 0)

            up_round(R_UP, True)
            up_round(R_UP + 1, second=True)
            with dve.Fori(R_UP + 2, R_DOWN) as m:
                up_round(m)

            def down_body(i):
                for e in range(12):
                    m, s, n = 3 * i + (R_DOWN + e // 4), e % 4, 4 * i + e // 3
                    ahead(m, s)
                    if e % 3 == 2:
                        dve.wait_ge(unit_done, 4 * m + (s + 1))
                        dve.tensor_tensor(x2[:, n, :], acc[:, e // 3, :], x1[:, n, :], ALU.add)\
                           .then_inc(taken[e // 3], 1)
                        add_square(N_FINAL, n, e // 3 % 2)
                        dve.wait_ge(gained_squared, n + 1)
                        at_least(dve, gained_added, n)
                        dve.tensor_tensor(sum_gained, sum_gained, gate[:, e // 3 % 2, :], ALU.add)\
                           .then_inc(gained_added, 1)
                        dve.wait_ge(act_high, 3 * KT + n + 1)
                        dve.scalar_tensor_tensor(xn_low[:, n, :], x2[:, n, :], gain2[:, n:n + 1],
                                                 xn_high[:, n, :].bitcast(F32), ALU.mult, ALU.subtract)\
                           .then_inc(act_low, 1)

            dve.wait_ge(ffn_mul, F_TILES)
            dve.memset(sum_gained, 0.0).then_inc(gained_cleared, 1)
            dve.wait_ge(gained_cleared, 1)
            g_final = par[:, PARAMS["g_final"]:PARAMS["g_final"] + KT]
            g_second = par[:, PARAMS["g_second"]:PARAMS["g_second"] + KT]
            dve.tensor_tensor(gain2[:, :], g_final, g_second, ALU.mult).then_inc(gain2_done, 1)
            down_body(0)
            dve.wait_ge(strip_done, 1)
            dve.tensor_tensor(strip, side[0:HEADS_B, 2, 0:3 * P], neg_sb, ALU.add).then_inc(strip_ready, 1)
            down_body(1)
            def root_times(k):
                dve.wait_ge(unit_done, 4 * R_QKV + k + 1)
                dst, scale = (q2[:, k, :], 1.0 / 8) if k < KT else (k2[:, k - KT, :], 1.0)
                dve.scalar_tensor_tensor(dst, acc[:, k % 4, :], scale, rstd2, ALU.mult, ALU.mult)\
                   .then_inc(taken[k % 4], 1)

            for s in range(2):
                ahead(R_QKV, s)
            dve.wait_ge(stat_done, N_FINAL + 1)
            dve.tensor_scalar(stat_col[:, 0:4], side[:, 3, 0:4], 1.0 / D, EPS, ALU.mult, ALU.add)\
               .then_inc(stat_read, 1)
            dve.wait_ge(stat_read, N_FINAL + 1)
            dve.wait_ge(gained_stat, 1)
            dve.scalar_tensor_tensor(stat_col[:, 4:8], stat_col[:, 0:4], EPS * D, side[:, 2, 0:4],
                                     ALU.mult, ALU.add).then_inc(second_step, 1)
            dve.wait_ge(second_step, 1)
            dve.reciprocal(stat_col[:, 4:8], stat_col[:, 4:8]).then_inc(second_step, 1)
            dve.reciprocal(stat_col[:, 0:4], stat_col[:, 0:4]).then_inc(recip_done, 1)
            clear_sum(N_FINAL + 1)
            for m in range(R_QKV, R_Z):
                for s in range(SLOTS):
                    k = 4 * (m - R_QKV) + s
                    if k > 1:
                        ahead(m, s)
                    if k == 2:
                        dve.wait_ge(rstd2_ready, 1)
                        dve.tensor_copy(rstd2, side[:, 2, :]).then_inc(rstd2_kept, 1)
                        dve.wait_ge(rstd2_kept, 1)
                        for j in range(2):
                            root_times(j)
                        dve.wait_ge(rstd_ready, N_FINAL + 1)
                    if 2 <= k < KT + 2:
                        root_times(k)
                        dve.scalar_tensor_tensor(y_res[:, k - 2, :], x2[:, k - 2, :], col("g_final", k - 2),
                                                 side[:, 3, :], ALU.mult, ALU.mult).then_inc(y_ready, 1)
            dve.wait_ge(bias_landed, 16)

            def biased(step):
                g, n = 2 * (step // 8) + step % 2, step % 8 // 2
                lo = 0 if n else P
                pr, sm = sw_probs[step % 3], sw_small[step % 3]
                dve.wait_ge(sw_scores, step + 1)
                at_least(dve, sw_turned, step - 2)
                for r in range(4):
                    at = MEM * (r % 2)
                    dve.tensor_tensor_reduce(pr[:, r, lo:], side[:, 2 * (step % 2) + r // 2, at + lo:at + MEM],
                                             bias[:, 4 * g + r, lo:], 1.0, NEG, ALU.add, ALU.max,
                                             sm[:, 3, r:r + 1]).then_inc(sw_step, 1)
                dve.wait_ge(sw_step, 6 * step + 4)
                sink = par[:, PARAMS["sinks"] + 4 * g:PARAMS["sinks"] + 4 * g + 4]
                dve.tensor_tensor(sm[:, 5, :], sm[:, 3, :], sink, ALU.max).then_inc(sw_step, 1)
                dve.wait_ge(sw_step, 6 * step + 5)
                dve.tensor_scalar(sm[:, 0, :], sm[:, 5, :], -1.0, None, ALU.mult).then_inc(sw_minus, 1)
                dve.tensor_tensor(sm[:, 2, :], sink, sm[:, 5, :], ALU.subtract).then_inc(sw_step, 1)

            def normalised(step):
                lo = 0 if step % 8 >= 2 else P
                pr, sm = sw_probs[step % 3], sw_small[step % 3]
                dve.wait_ge(sw_exp, 5 * step + 5)
                dve.tensor_tensor(sm[:, 4, :], sm[:, 1, :], sm[:, 2, :], ALU.add).then_inc(sw_sum, 1)
                dve.wait_ge(sw_sum, step + 1)
                dve.reciprocal(sm[:, 4, :], sm[:, 4, :]).then_inc(sw_recip, 1)
                dve.wait_ge(sw_recip, step + 1)
                dve.tensor_tensor(pr[:, :, lo:], pr[:, :, lo:],
                                  sm[:, 4, :].unsqueeze(2).broadcast_to((P, 4, 2 * P - lo)), ALU.mult)\
                   .then_inc(sw_ready, 1)

            def gate_tile(k):
                dve.wait_ge(z_silu, k + 1)
                dve.wait_ge(sw_out, 4 * (k // 4) + 4)
                at_least(dve, gated_low, k - 1)
                dve.tensor_tensor(part[:, k % 2, :], o2[:, k, :], z[:, k, :], ALU.mult).then_inc(gated, 1)

            def gated_low_of(k):
                dve.wait_ge(gated_high, k + 1)
                dve.tensor_tensor(o2_low[:, k, :], part[:, k % 2, :], o2_high[:, k, :].bitcast(F32), ALU.subtract)\
                   .then_inc(gated_low, 1)

            def gate_result(j):
                dve.wait_ge(unit_done, 4 * R_Z + j + 1)
                dve.tensor_tensor(z[:, j, :], acc[:, Z_BANK, :], rstd2, ALU.mult).then_inc(taken[Z_BANK], 1)

            biased(0)
            biased(1)
            normalised(0)
            ahead(R_Z, 0)
            normalised(1)
            biased(2)
            for step in range(2 * KT):
                if step % 2 == 0 and step:
                    gate_result(step // 2 - 1)
                if step % 8 >= 2:
                    dve.wait_ge(sw_turned, step + 1)
                    at_least(dve, sw_pv, (step - 3) // 2 + 1)
                    dve.tensor_copy(sw_probs_t[step % 3][:, 0, :], acc[:, 0, :]).then_inc(sw_older_turned, 1)
                    if step >= 2 * KT - 3:
                        dve.tensor_copy(sw_probs_t[step % 3][:, 1, :], acc[:, 1, :]).then_inc(sw_own_turned, 1)
                if 0 < step < 2 * KT - 1:
                    normalised(step + 1)
                if step % 2 == 0 and step:
                    ahead(R_Z + step // 8, step // 2 % 4)
                for k in GATE_TILES.get(step, ()):
                    gate_tile(k)
                for k in GATE_TILES.get(step, ()):
                    gated_low_of(k)
                if step + 3 < 2 * KT:
                    biased(step + 3)
            gate_result(KT - 1)
            for k in range(4, KT):
                gate_tile(k)
                if k > 4:
                    gated_low_of(k - 1)
            gated_low_of(KT - 1)
            for m in range(R_LAST, ROUNDS):
                residual_round(m, R_LAST, N_LAST, x3, y_res)
            mean_square(N_LAST, SEQ)
            dve.wait_ge(rstd_ready, N_LAST + 1)
            for k in range(KT):
                dve.scalar_tensor_tensor(result[:, k, :], x3[:, k, :], col("g_last", k), side[:, 3, :],
                                         ALU.mult, ALU.mult).then_inc(result_ready, 1)


def distance_columns():
    import numpy as np
    exact, buckets, far = 16, 32, 128
    picks = np.zeros((48, 3 * P), np.float32)
    for i in range(3 * P):
        dist = 2 * P - 1 - i
        if 0 <= dist < WINDOW:
            large = exact + int(np.float32(np.log(max(dist, 1) / exact)) / np.log(far / exact) * (buckets - exact)) \
                if dist >= exact else 0
            picks[dist if dist < exact else min(large, buckets - 1), i] = 1.0
        else:
            picks[32:, i] = NEG
    return picks


def kernel(**inputs):
    import numpy as np
    import concourse.bacc as bacc
    from concourse.bass_utils import run_bass_kernel_spmd as run

    a = {k: np.asarray(v) for k, v in inputs.items()}

    def units(w):
        n = w.shape[1] // P
        return w.reshape(KT, P, n, P).transpose(2, 1, 0, 3).reshape(n, P, UNIT)

    def pairs(u, v):
        return np.stack([u, v], 1).reshape(-1, P, UNIT)

    w_in = units(a["w_in"][0])
    gb, gc, v, u, ug, wq = (w_in[8 * i:8 * i + 8] for i in range(6))
    g0, g1, g2 = (w_in[48 + 8 * i:56 + 8 * i] for i in range(3))
    w_up = units(a["w_up"][0])
    down = a["w_down"][0].reshape(F_TILES, P, KT, P).transpose(2, 1, 0, 3)
    down_units = np.zeros((KT, 3, P, KT, P), np.float32)
    for i, (lo, hi) in enumerate(((0, 8), (8, 15), (15, 22))):
        down_units[:, i, :, :hi - lo, :] = down[:, :, lo:hi, :]

    order = np.array([(4 * (2 * p + e) + r) * 64 + c for p in range(2) for r in range(4) for e in range(2)
                      for c in range(64)])
    w2 = a["a_w_in_2"][0]
    qkv = np.concatenate([w2[:, 0:D][:, order], w2[:, D:D + 512]], 1)
    w_z = w2[:, D + 512:][:, order]
    w_last = a["a_w_out_2"][0][order, :]
    weights = np.concatenate([
        units(a["w_kv"][0]), pairs(ug, u), wq,
        np.stack([gc, v, gb], 1).reshape(-1, P, UNIT),
        pairs(g0, units(a["w_a_out"][0])), pairs(g2, units(a["w_att_out"][0])), pairs(g1, units(a["w_b_out"][0])),
        units(a["w_o"][0]), pairs(w_up[:F_TILES], w_up[F_TILES:]), down_units.reshape(-1, P, UNIT),
        units(qkv), units(w_z), units(w_last),
    ])

    def channels(t):
        return np.ascontiguousarray(t.reshape(-1, KT, P).transpose(2, 1, 0))

    def cols(t):
        t = np.atleast_2d(t)
        return t.reshape(t.shape[0], -1, P).transpose(2, 1, 0).reshape(P, -1)

    params = np.concatenate([
        cols(a["norm_mix_g"][0]), cols(a["norm_mem_g"][0]), cols(a["conv_b_w"][0]), cols(a["conv_b_bias"][0]),
        cols(a["ln_b_g"][0]), cols(a["ln_b_b"][0]), cols(a["b_gate"][0]), cols(a["conv_a_w"][0]),
        cols(a["norm_ffn_g"][0]), cols(a["conv_ffn_w"][0]), cols(a["norm_final_g"]), cols(a["norm_g_2"][0]),
        cols(a["final_g_2"]), np.broadcast_to(a["a_sinks_2"][0], (P, HEADS_B)),
    ], 1)
    arrays = {
        "weights": np.ascontiguousarray(weights),
        "x": channels(a["x"][0]),
        "mem": channels(a["mem"][0]),
        "params": np.ascontiguousarray(params),
        "consts": np.concatenate([np.ones((P, P), np.float32), np.eye(P, dtype=np.float32)], 1),
        "table": np.ascontiguousarray(a["t5_table_2"]),
        "onehot": distance_columns(),
    }
    nc = bacc.Bacc("TRN2", target_bir_lowering=False, num_devices=1)
    args = [nc.dram_tensor(n, v.shape, mybir.dt.from_np(v.dtype), kind="ExternalInput").ap()
            for n, v in arrays.items()]
    out = nc.dram_tensor("out", (P, KT, SEQ), F32, kind="ExternalOutput").ap()
    build(nc, *args, out)
    r = run(nc, [arrays], core_ids=[0])
    got = r.results[0]["out"]
    return np.ascontiguousarray(got.transpose(2, 1, 0)).reshape(1, SEQ, D)
```
